# Optimizing a Trainium2 kernel written in Bass

```python
import math
import jax, jax.numpy as jnp
from jax import lax
import numpy as np

D_MODEL = 1024
BATCH = 1
SEQ = 1024
DEPTH = 1
DEC_BATCH = 8
DEC_SEQ = 1
PAST_LEN = 2048
PAGE_SIZE = 128

HEAD_DIM = 64
DIL_GROUPS = ((128, 1), (512, 4), (2048, 16))
N_GROUPS = 3
HEADS_PER_GROUP = 4
N_DIL_HEADS = N_GROUPS * HEADS_PER_GROUP
DIL_WIDTH = N_DIL_HEADS * HEAD_DIM
DIL_OUT = HEADS_PER_GROUP * HEAD_DIM
BLOCK = 128
POOL_WINDOWS = (2, 4, 8, 16)
POOL_GROUP = 128
POOL_WIDTH = POOL_GROUP * len(POOL_WINDOWS)
POOL_STATE = max(POOL_WINDOWS) - 1
MEM_LEN = 256
MEM_HEADS = 4
MEM_HEAD_DIM = 128
MEM_WIDTH = MEM_HEADS * MEM_HEAD_DIM
N_BUCKETS = 32
MAX_DISTANCE = 2048
D_FF = 2816
N_BRANCH = 3
IN_COLS = 3 * DIL_WIDTH + POOL_WIDTH + MEM_WIDTH + N_BRANCH * D_MODEL
EPS = 1e-6
NEG_INF = -1e30

kernel_name = "hybrid_dilated_pool_memory_decoder_step"

def rms_norm(x, g):
    xf = x.astype(jnp.float32)
    xf = xf * lax.rsqrt(jnp.mean(xf * xf, axis=-1, keepdims=True) + EPS)
    return xf.astype(x.dtype) * g

def swiglu(h, wg, wu, wd):
    return (jax.nn.silu(h @ wg) * (h @ wu)) @ wd

def ffn_half(x, g, wg, wu, wd):
    return x + 0.5 * swiglu(rms_norm(x, g), wg, wu, wd)

def rel_bucket(n):
    max_exact = N_BUCKETS // 2
    nf = jnp.maximum(n, 1).astype(jnp.float32)
    large = max_exact + (jnp.log(nf / max_exact) / math.log(MAX_DISTANCE / max_exact)
                         * (N_BUCKETS - max_exact)).astype(jnp.int32)
    large = jnp.minimum(large, N_BUCKETS - 1)
    return jnp.where(n < max_exact, n, large)

def dilation_bias(rel_bias, g, window, dil):
    j = jnp.arange(window // dil + 1, dtype=jnp.int32)
    b = rel_bias[rel_bucket(j * dil)]
    return b[:, g * HEADS_PER_GROUP:(g + 1) * HEADS_PER_GROUP].astype(jnp.float32)

def split_proj(u, w_in_l):
    n, t, _ = u.shape
    p = u @ w_in_l
    o = 3 * DIL_WIDTH
    qkv = p[..., :o].reshape(n, t, 3, N_GROUPS, HEADS_PER_GROUP, HEAD_DIM)
    z = p[..., o:o + POOL_WIDTH]
    o += POOL_WIDTH
    qm = p[..., o:o + MEM_WIDTH].reshape(n, t, MEM_HEADS, MEM_HEAD_DIM)
    o += MEM_WIDTH
    gates = jax.nn.sigmoid(p[..., o:].astype(jnp.float32)).astype(u.dtype)
    return qkv, z, qm, gates.reshape(n, t, N_BRANCH, D_MODEL)

def dilated_prompt(q, k, v, bias_j, dil, window):
    n, s, h, dh = q.shape
    nk = window // dil
    L = s // dil
    nb = -(-L // BLOCK)
    Lp = nb * BLOCK

    def to_blocks(a):
        a = a.reshape(n, L, dil, h, dh).transpose(0, 2, 1, 3, 4)
        a = jnp.pad(a, ((0, 0), (0, 0), (0, Lp - L), (0, 0), (0, 0)))
        return a.reshape(n, dil, nb, BLOCK, h, dh)

    def with_prev(a):
        prev = jnp.concatenate([jnp.zeros_like(a[:, :, :1]), a[:, :, :-1]], axis=2)
        return jnp.concatenate([prev, a], axis=3)

    qb = to_blocks(q)
    kk = with_prev(to_blocks(k))
    vv = with_prev(to_blocks(v))
    scores = jnp.einsum('brnqhd,brnkhd->brnhqk', qb, kk,
                        preferred_element_type=jnp.float32) * (1.0 / math.sqrt(dh))
    qi = jnp.arange(BLOCK)[:, None]
    ki = jnp.arange(2 * BLOCK)[None, :]
    rel = qi + BLOCK - ki
    valid = (rel >= 0) & (rel <= nk)
    key_exists = (jnp.arange(nb)[:, None] > 0) | (ki >= BLOCK)
    bias = bias_j[jnp.clip(rel, 0, nk)].transpose(2, 0, 1)
    mask = valid[None, :, :] & key_exists[:, None, :]
    logits = jnp.where(mask[None, None, :, None], scores + bias, NEG_INF)
    lse = jax.nn.logsumexp(logits, axis=-1)
    pr = jnp.exp(logits - lse[..., None])
    o = jnp.einsum('brnhqk,brnkhd->brnqhd', pr, vv.astype(jnp.float32))
    o = o.reshape(n, dil, Lp, h, dh)[:, :, :L].transpose(0, 2, 1, 3, 4).reshape(n, s, h, dh)
    lse = lse.transpose(0, 1, 2, 4, 3).reshape(n, dil, Lp, h)[:, :, :L]
    lse = lse.transpose(0, 2, 1, 3).reshape(n, s, h)
    return o, lse

def dilated_sample(q, kv_buf, k_new, v_new, bias_j, dil, window):
    wb = kv_buf.shape[1]
    t = q.shape[1]
    kc = jnp.concatenate([kv_buf[:, :, 0], k_new], axis=1)
    vc = jnp.concatenate([kv_buf[:, :, 1], v_new], axis=1)
    nk = window // dil
    idx = wb + jnp.arange(t)[:, None] - dil * jnp.arange(nk + 1)[None, :]
    valid = idx >= 0
    idxc = jnp.maximum(idx, 0)
    kg = kc[:, idxc]
    vg = vc[:, idxc]
    scores = jnp.einsum('nthd,ntjhd->nhtj', q, kg,
                        preferred_element_type=jnp.float32) * (1.0 / math.sqrt(q.shape[-1]))
    logits = jnp.where(valid[None, None], scores + bias_j.T[None, :, None, :], NEG_INF)
    lse = jax.nn.logsumexp(logits, axis=-1)
    pr = jnp.exp(logits - lse[..., None])
    o = jnp.einsum('nhtj,ntjhd->nthd', pr, vg.astype(jnp.float32))
    return o, lse.transpose(0, 2, 1)

def combine_groups(outs, lses):
    o = jnp.stack(outs, axis=2)
    w = jax.nn.softmax(jnp.stack(lses, axis=2), axis=2)
    o = jnp.sum(w[..., None] * o, axis=2)
    return o.reshape(o.shape[0], o.shape[1], DIL_OUT)

def pool_mixer(z_hist, z_new, pos0, w_pool_l, pool_scale_l):
    n, lh, c = z_hist.shape
    t = z_new.shape[1]
    zf = jnp.concatenate([z_hist, z_new], axis=1).astype(jnp.float32)
    c0 = jnp.concatenate([jnp.zeros((n, 1, c), jnp.float32), jnp.cumsum(zf, axis=1)], axis=1)
    r = lh + jnp.arange(t)
    pos = pos0 + jnp.arange(t)
    hi = c0[:, r + 1]
    outs = []
    for gi, kw in enumerate(POOL_WINDOWS):
        sl = slice(gi * POOL_GROUP, (gi + 1) * POOL_GROUP)
        lo = c0[:, jnp.maximum(r + 1 - kw, 0), sl]
        cnt = jnp.minimum(kw, pos + 1).astype(jnp.float32)
        outs.append((hi[..., sl] - lo) / cnt[None, :, None] - zf[:, lh:, sl])
    pooled = jnp.stack(outs, axis=2)
    mixed = jnp.einsum('ntgc,gcd->ntgd', pooled, w_pool_l.astype(jnp.float32)).reshape(n, t, POOL_WIDTH)
    return mixed * pool_scale_l.astype(jnp.float32)

def memory_kv(mem, g_mem_l, w_mem_kv_l):
    n = mem.shape[0]
    return (rms_norm(mem, g_mem_l) @ w_mem_kv_l).reshape(n, MEM_LEN, 2, MEM_HEADS, MEM_HEAD_DIM)

def mem_attend(qm, kv):
    scores = jnp.einsum('nthd,nmhd->nhtm', qm, kv[:, :, 0],
                        preferred_element_type=jnp.float32) * (1.0 / math.sqrt(MEM_HEAD_DIM))
    pr = jax.nn.softmax(scores, axis=-1)
    o = jnp.einsum('nhtm,nmhd->nthd', pr, kv[:, :, 1].astype(jnp.float32))
    return o.reshape(o.shape[0], o.shape[1], MEM_WIDTH)

def merge(a_out, b_out, c_out, gates, w_oa_l, w_ob_l, w_oc_l, w_out_l):
    m = (gates[:, :, 0] * (a_out @ w_oa_l) + gates[:, :, 1] * (b_out @ w_ob_l)
         + gates[:, :, 2] * (c_out @ w_oc_l))
    return m @ w_out_l

def setup_inputs(seed: int = 0) -> dict:
    key = jax.random.key(seed)
    ks = iter(jax.random.split(key, 40))
    f32 = jnp.float32

    def nrm(shape, scale):
        return jax.random.normal(next(ks), shape, f32) * scale

    def gain(shape):
        return 1.0 + nrm(shape, 0.1)

    D = D_MODEL
    inp = {}
    inp["x_prompt"] = nrm((BATCH, SEQ, D), 1.0)
    inp["x_sample"] = nrm((DEC_BATCH, DEC_SEQ, D), 1.0)
    for g, (win, dil) in enumerate(DIL_GROUPS):
        inp["cache_win%d_kv" % g] = nrm((DEPTH, DEC_BATCH, min(win, PAST_LEN), 2, HEADS_PER_GROUP, HEAD_DIM), 1.0)
    inp["state_pool"] = nrm((DEPTH, DEC_BATCH, POOL_STATE, POOL_WIDTH), 1.0)
    inp["cache_mem_kv"] = nrm((DEPTH, DEC_BATCH, MEM_LEN, 2, MEM_HEADS, MEM_HEAD_DIM), 1.0)
    inp["mem_prompt"] = nrm((BATCH, MEM_LEN, D), 1.0)
    inp["rel_bias"] = nrm((N_BUCKETS, N_DIL_HEADS), 0.5)
    inp["g_ffn1"] = gain((DEPTH, D))
    inp["w1_gate"] = nrm((DEPTH, D, D_FF), D ** -0.5)
    inp["w1_up"] = nrm((DEPTH, D, D_FF), D ** -0.5)
    inp["w1_down"] = nrm((DEPTH, D_FF, D), D_FF ** -0.5)
    inp["g_mix"] = gain((DEPTH, D))
    inp["w_in"] = nrm((DEPTH, D, IN_COLS), D ** -0.5)
    inp["w_pool"] = nrm((DEPTH, len(POOL_WINDOWS), POOL_GROUP, POOL_GROUP), POOL_GROUP ** -0.5)
    inp["pool_scale"] = gain((DEPTH, POOL_WIDTH))
    inp["g_mem"] = gain((DEPTH, D))
    inp["w_mem_kv"] = nrm((DEPTH, D, 2 * MEM_WIDTH), D ** -0.5)
    inp["w_oa"] = nrm((DEPTH, DIL_OUT, D), DIL_OUT ** -0.5)
    inp["w_ob"] = nrm((DEPTH, POOL_WIDTH, D), POOL_WIDTH ** -0.5)
    inp["w_oc"] = nrm((DEPTH, MEM_WIDTH, D), MEM_WIDTH ** -0.5)
    inp["w_out"] = nrm((DEPTH, D, D), D ** -0.5)
    inp["g_ffn2"] = gain((DEPTH, D))
    inp["w2_gate"] = nrm((DEPTH, D, D_FF), D ** -0.5)
    inp["w2_up"] = nrm((DEPTH, D, D_FF), D ** -0.5)
    inp["w2_down"] = nrm((DEPTH, D_FF, D), D_FF ** -0.5)
    inp["g_final"] = gain((D,))
    return inp

def reference(x_prompt, x_sample, cache_win0_kv, cache_win1_kv, cache_win2_kv, state_pool, cache_mem_kv,
              mem_prompt, rel_bias, g_ffn1, w1_gate, w1_up, w1_down, g_mix, w_in, w_pool, pool_scale,
              g_mem, w_mem_kv, w_oa, w_ob, w_oc, w_out, g_ffn2, w2_gate, w2_up, w2_down, g_final):
    win_caches = (cache_win0_kv, cache_win1_kv, cache_win2_kv)
    biases = [dilation_bias(rel_bias, g, win, dil) for g, (win, dil) in enumerate(DIL_GROUPS)]

    def block(x, l, mix_fn):
        x = ffn_half(x, g_ffn1[l], w1_gate[l], w1_up[l], w1_down[l])
        u = rms_norm(x, g_mix[l])
        qkv, z, qm, gates = split_proj(u, w_in[l])
        a_out, b_out, c_out, states = mix_fn(qkv, z, qm)
        dt = x.dtype
        x = x + merge(a_out.astype(dt), b_out.astype(dt), c_out.astype(dt), gates,
                      w_oa[l], w_ob[l], w_oc[l], w_out[l])
        x = ffn_half(x, g_ffn2[l], w2_gate[l], w2_up[l], w2_down[l])
        return x, states

    st_p = [[] for _ in range(5)]
    st_s = [[] for _ in range(4)]
    xp = x_prompt
    xs = x_sample
    for l in range(DEPTH):
        def prompt_mix(qkv, z, qm):
            s = qkv.shape[1]
            outs, lses, wins = [], [], []
            for g, (win, dil) in enumerate(DIL_GROUPS):
                q_g, k_g, v_g = qkv[:, :, 0, g], qkv[:, :, 1, g], qkv[:, :, 2, g]
                o, lse = dilated_prompt(q_g, k_g, v_g, biases[g], dil, win)
                outs.append(o)
                lses.append(lse)
                wins.append(jnp.stack([k_g, v_g], axis=2)[:, s - min(win, s):])
            a_out = combine_groups(outs, lses)
            b_out = pool_mixer(z[:, :0], z, 0, w_pool[l], pool_scale[l])
            mkv = memory_kv(mem_prompt, g_mem[l], w_mem_kv[l])
            c_out = mem_attend(qm, mkv)
            return a_out, b_out, c_out, (wins[0], wins[1], wins[2], z[:, s - POOL_STATE:], mkv)

        def sample_mix(qkv, z, qm):
            outs, lses, rows = [], [], []
            for g, (win, dil) in enumerate(DIL_GROUPS):
                q_g, k_g, v_g = qkv[:, :, 0, g], qkv[:, :, 1, g], qkv[:, :, 2, g]
                o, lse = dilated_sample(q_g, win_caches[g][l], k_g, v_g, biases[g], dil, win)
                outs.append(o)
                lses.append(lse)
                rows.append(jnp.stack([k_g, v_g], axis=2))
            a_out = combine_groups(outs, lses)
            b_out = pool_mixer(state_pool[l], z, PAST_LEN, w_pool[l], pool_scale[l])
            c_out = mem_attend(qm, cache_mem_kv[l])
            return a_out, b_out, c_out, (rows[0], rows[1], rows[2], z)

        xp, sp = block(xp, l, prompt_mix)
        xs, ss = block(xs, l, sample_mix)
        for i in range(5):
            st_p[i].append(sp[i])
        for i in range(4):
            st_s[i].append(ss[i])

    y_prompt = rms_norm(xp, g_final)
    y_sample = rms_norm(xs, g_final)
    new_win0_kv_prompt = jnp.stack(st_p[0], axis=0)
    new_win1_kv_prompt = jnp.stack(st_p[1], axis=0)
    new_win2_kv_prompt = jnp.stack(st_p[2], axis=0)
    new_pool_prompt = jnp.stack(st_p[3], axis=0)
    new_mem_kv_prompt = jnp.stack(st_p[4], axis=0)
    new_win0_kv_sample = jnp.stack(st_s[0], axis=0)
    new_win1_kv_sample = jnp.stack(st_s[1], axis=0)
    new_win2_kv_sample = jnp.stack(st_s[2], axis=0)
    new_pool_sample = jnp.stack(st_s[3], axis=0)
    return (y_prompt, y_sample, new_win0_kv_prompt, new_win1_kv_prompt, new_win2_kv_prompt, new_pool_prompt,
            new_mem_kv_prompt, new_win0_kv_sample, new_win1_kv_sample, new_win2_kv_sample, new_pool_sample)


_drawn_inputs = setup_inputs


def setup_inputs(seed=0):
    import zlib

    import numpy as np

    out = dict(_drawn_inputs(seed))
    spreads = {}
    factors = {}
    for name, (base, spread) in spreads.items():
        noise = np.random.default_rng([zlib.crc32(name.encode()), seed]).standard_normal(out[name].shape)
        drawn = base * np.exp(spread * noise) if base else spread * noise
        out[name] = __import__('jax').numpy.asarray(drawn.astype(out[name].dtype))
    for name, factor in factors.items():
        out[name] = (out[name] * factor).astype(out[name].dtype)
    return out
```

```python
from contextlib import ExitStack

import numpy as np

import concourse.bass as bass
from concourse import mybir

F32 = mybir.dt.float32
F32R = mybir.dt.float32r
ALU = mybir.AluOpType
ACT = mybir.ActivationFunctionType
AX_X = mybir.AxisListType.X

P = 128
D = 1024
SEQ = 1024
NS = 8
T = SEQ + NS
KD = D // P
CHUNKS = ((0, 352), (352, 352), (704, 328))
NCH = len(CHUNKS)
CH = CHUNKS[0][1]
TB = SEQ // P
F = 2816
EPS = 1e-6
G_FFN1, G_MIX, G_MEM, G_FFN2, G_FINAL = range(5)
GAIN_ROWS = 5 * KD
NPOOL = 4


class Count:

    def __init__(self, eng, sem, base=0):
        self.eng, self.sem, self.base, self.n = eng, sem, base, 0

    def then_wait(self, ins):
        self.n += 1
        ins.then_inc(self.sem, 1)
        self.eng.wait_ge(self.sem, self.base + self.n)


SEMS = []


def clear_semaphores(nc):
    nc.clear_and_free_semaphores(SEMS)
    SEMS.clear()
    nc.all_engine_barrier()


class Stage:

    def __init__(self, nc, name):
        self.nc, self.name, self.ctx = nc, name, ExitStack()

    def __enter__(self):
        return self

    def __exit__(self, *e):
        return self.ctx.__exit__(*e)

    def sbuf(self, name, shape, dt=F32):
        return self.ctx.enter_context(self.nc.sbuf_tensor(f"{self.name}_{name}", shape, dt))

    def sem(self, name):
        sem = self.nc.alloc_semaphore(f"{self.name}_{name}")
        SEMS.append(sem)
        return sem

    def block(self):
        return self.ctx.enter_context(self.nc.Block())


def chunk(c):
    return slice(CHUNKS[c][0], CHUNKS[c][0] + CHUNKS[c][1])


def width(c):
    return slice(0, CHUNKS[c][1])


def load_tokens(nc, m, x_prompt, x_sample, gains, pool_scale, ident_in):
    with Stage(nc, "load") as st:
        tok = st.sbuf("tok", [P, TB, D])
        stok = st.sbuf("stok", [NS, D])
        grow = st.sbuf("grow", [GAIN_ROWS + NPOOL, P])
        tok_in = [st.sem(f"tok_in{b}") for b in range(TB)]
        small_in = st.sem("small_in")
        turned = st.sem("turned")
        taken_dve = st.sem("taken_dve")
        taken_act = st.sem("taken_act")
        ones_set = st.sem("ones_set")
        block = st.block()
        xp = x_prompt.rearrange("a (b p) d -> p (a b) d", p=P)

        @block.sync
        def _(sp):
            sp.dma_start(m.ident[:, :], ident_in).then_inc(small_in, 16)
            for n, g in enumerate(gains):
                src = g.rearrange("a (k p) -> (a k) p", p=P) if len(g.shape) == 2 else g.rearrange("(k p) -> k p", p=P)
                sp.dma_start(grow[n * KD:(n + 1) * KD, :], src).then_inc(small_in, 16)
            sp.dma_start(grow[GAIN_ROWS:, :], pool_scale.rearrange("a (k p) -> (a k) p", p=P)).then_inc(small_in, 16)
            sp.dma_start(stok[:, :], x_sample.rearrange("n a d -> (n a) d")).then_inc(small_in, 16)
            for b in range(TB):
                sp.dma_start(tok[:, b, :], xp[:, b, :]).then_inc(tok_in[b], 16)

        @block.tensor
        def _(pe):
            pe.wait_ge(small_in, 16 * (len(gains) + 3))
            pe.transpose(m.ps[:, 0, 0:GAIN_ROWS + NPOOL], grow[:, :], m.ident[0:GAIN_ROWS + NPOOL, 0:GAIN_ROWS + NPOOL])
            for k in range(KD):
                last = pe.transpose(m.ps[:, 0, 64 + NS * k:64 + NS * (k + 1)], stok[:, k * P:(k + 1) * P],
                                    m.ident[0:NS, 0:NS])
            last.then_inc(turned, 1)
            for n in range(2 * TB):
                b, half = divmod(n, 2)
                if half == 0:
                    pe.wait_ge(tok_in[b], 16)
                if n >= 6:
                    pe.wait_ge(taken_dve if n % 2 == 0 else taken_act, (n - 6) // 2 + 1)
                for k in range(4):
                    kk = 4 * half + k
                    last = pe.transpose(m.ps[:, 1 + n % 6, k * P:(k + 1) * P], tok[:, b, kk * P:(kk + 1) * P],
                                        m.ident[:, :])
                last.then_inc(turned, 1)

        def target(n):
            b, half = divmod(n, 2)
            return m.x[:, 4 * half:4 * half + 4, b * P:(b + 1) * P]

        def source(n):
            return m.ps[:, 1 + n % 6, :].rearrange("p (k t) -> p k t", k=4)

        @block.vector
        def _(dve):
            dve.memset(m.mean[:, :], 1.0 / D).then_inc(ones_set, 1)
            for n in range(0, 2 * TB, 2):
                dve.wait_ge(turned, n + 2)
                dve.tensor_copy(target(n), source(n)).then_inc(taken_dve, 1)

        @block.scalar
        def _(act):
            act.wait_ge(turned, 1)
            act.activation(m.gain[:, :], m.ps[:, 0, 0:GAIN_ROWS + NPOOL], ACT.Copy)
            act.activation(m.x[:, :, SEQ:T], m.ps[:, 0, 64:128].rearrange("p (k n) -> p k n", k=KD), ACT.Copy)
            for n in range(1, 2 * TB, 2):
                act.wait_ge(turned, n + 2)
                act.activation(target(n), source(n), ACT.Copy).then_inc(taken_act, 1)


class Norm:

    def __init__(self, st, m, which, banks, high, low):
        self.m, self.which, self.banks, self.high, self.low = m, which, banks, high, low
        self.sq = st.sbuf("sq", [P, KD, CH])
        self.xn = self.sq
        self.ssum = st.sbuf("ssum", [P, NCH, CH])
        self.rstd = self.ssum
        self.squared = st.sem("squared")
        self.summed = st.sem("summed")
        self.meaned = st.sem("meaned")
        self.shifted = st.sem("shifted")
        self.rooted = st.sem("rooted")
        self.inverted = st.sem("inverted")
        self.scaled = st.sem("scaled")
        self.high_done = st.sem("high_done")
        self.ready = st.sem("normed")

    def scalar(self, act):
        m = self.m
        for c in range(NCH):
            if c:
                act.wait_ge(self.summed, c)
            act.activation(self.sq[:, :, width(c)], m.x[:, :, chunk(c)], ACT.Square).then_inc(self.squared, 1)
        for c in range(NCH):
            act.wait_ge(self.shifted, c + 1)
            act.activation(self.rstd[:, c, width(c)], self.ssum[:, c, width(c)], ACT.Sqrt).then_inc(self.rooted, 1)
        for c in range(NCH):
            act.wait_ge(self.scaled, c + 1)
            for k in range(KD):
                act.activation(self.high[:, k, chunk(c)], self.xn[:, k, width(c)], ACT.Copy,
                               scale=m.gain[:, self.which * KD + k:self.which * KD + k + 1]).then_inc(self.high_done, 1)

    def tensor(self, pe):
        for c in range(NCH):
            pe.wait_ge(self.summed, c + 1)
            pe.matmul(self.m.ps[:, self.banks[c], width(c)], self.m.mean[:, :], self.ssum[:, c, width(c)],
                      start=True, stop=True).then_inc(self.meaned, 1)

    def vector(self, dve):
        m = self.m
        for c in range(NCH):
            dve.wait_ge(self.squared, c + 1)
            dve.tensor_reduce(self.ssum[:, c, width(c)], self.sq[:, :, width(c)].rearrange("p k t -> p t k"), AX_X,
                              ALU.add).then_inc(self.summed, 1)
        for c in range(NCH):
            dve.wait_ge(self.meaned, c + 1)
            dve.tensor_scalar(self.ssum[:, c, width(c)], m.ps[:, self.banks[c], width(c)], EPS, None,
                              ALU.add).then_inc(self.shifted, 1)
        for c in range(NCH):
            dve.wait_ge(self.rooted, c + 1)
            dve.reciprocal(self.rstd[:, c, width(c)], self.rstd[:, c, width(c)]).then_inc(self.inverted, 1)
            dve.wait_ge(self.inverted, c + 1)
            if c:
                dve.wait_ge(self.high_done, KD * c)
            dve.tensor_tensor(self.xn[:, :, width(c)], m.x[:, :, chunk(c)],
                              self.rstd[:, c, width(c)].unsqueeze(1).to_broadcast([P, KD, CHUNKS[c][1]]),
                              ALU.mult).then_inc(self.scaled, 1)
            if self.low is None:
                continue
            dve.wait_ge(self.scaled, c + 1)
            for k in range(KD):
                dve.wait_ge(self.high_done, KD * c + k + 1)
                ins = dve.scalar_tensor_tensor(self.low[:, k, chunk(c)], self.xn[:, k, width(c)],
                                               m.gain[:, self.which * KD + k:self.which * KD + k + 1],
                                               self.high[:, k, chunk(c)].bitcast(F32), ALU.mult, ALU.subtract)
            ins.then_inc(self.ready, 1)


FT = F // P
PAIRS = FT // 2
GU_UNITS = 2 * NCH
DOWN_UNITS = NCH * KD


def product(pe, out, w_high, w_low, a_high, a_low, first, last):
    pe.matmul(out, w_high, a_high, start=first, stop=False)
    pe.matmul(out, w_low, a_high, start=False, stop=False)
    return pe.matmul(out, w_high, a_low, start=False, stop=last)


def ffn(nc, m, name, which, w_gate, w_up, w_down):
    with Stage(nc, name) as st:
        norm = Norm(st, m, which, (5, 6, 7), m.uh, m.ul)
        raw_gu = st.sbuf("raw_gu", [P, 2 * KD, 2 * P])
        gu_h = [st.sbuf(f"gu_h{t}", [P, 2 * KD, P], F32R) for t in range(2)]
        gu_l = [st.sbuf(f"gu_l{t}", [P, 2 * KD, P], F32R) for t in range(2)]
        raw_d = st.sbuf("raw_d", [P, 2, D])
        d_h = st.sbuf("d_h", [P, 2, D], F32R)
        d_l = st.sbuf("d_l", [P, 2, D], F32R)
        hid_h = st.sbuf("hid_h", [P, 2, T], F32R)
        hid_l = st.sbuf("hid_l", [P, 2, T], F32R)
        silu = st.sbuf("silu", [P, 2, CH])
        gu_in = st.sem("gu_in")
        d_in = st.sem("d_in")
        gu_high = st.sem("gu_high")
        gu_split = st.sem("gu_split")
        d_high = st.sem("d_high")
        d_split = st.sem("d_split")
        gu_done = st.sem("gu_done")
        silu_done = st.sem("silu_done")
        hid_done = st.sem("hid_done")
        down_done = st.sem("down_done")
        down_added = st.sem("down_added")
        own = st.sem("own")
        block = st.block()
        wg = w_gate.rearrange("a (k p) f -> p (a k) f", p=P)
        wu = w_up.rearrange("a (k p) f -> p (a k) f", p=P)
        wd = w_down.rearrange("a (t p) d -> p (a t) d", p=P)

        @block.sync
        def _(sp):
            def load_gu(i):
                sp.dma_start(raw_gu[:, 0:KD, :], wg[:, :, bass.ts(i, 2 * P)]).then_inc(gu_in, 16)
                sp.dma_start(raw_gu[:, KD:2 * KD, :], wu[:, :, bass.ts(i, 2 * P)]).then_inc(gu_in, 16)

            def load_d(i):
                sp.dma_start(raw_d[:, :, :], wd[:, bass.ts(i, 2), :]).then_inc(d_in, 16)

            load_gu(0)
            load_d(0)
            with sp.Fori(1, PAIRS) as i:
                sp.wait_ge(gu_split, i * 2)
                load_gu(i)
                sp.wait_ge(d_split, i)
                load_d(i)

        @block.tensor
        def _(pe):
            norm.tensor(pe)
            with pe.Fori(0, PAIRS) as i:
                for n in range(GU_UNITS):
                    t, c = divmod(n, NCH)
                    if c == 0:
                        pe.wait_ge(gu_split, i * 2 + (t + 1))
                    pe.wait_ge(norm.ready, c + 1)
                    pe.wait_ge(hid_done, i * GU_UNITS + (n + 1))
                    for side in range(2):
                        for k in range(KD):
                            kk = side * KD + k
                            last = product(pe, m.ps[:, 2 * (n % 2) + side, width(c)], gu_h[t][:, kk, :], gu_l[t][:, kk, :],
                                           m.uh[:, k, chunk(c)], m.ul[:, k, chunk(c)], k == 0, k == KD - 1)
                    last.then_inc(gu_done, 1)
                pe.wait_ge(d_split, i + 1)
                for n in range(DOWN_UNITS):
                    c, o = divmod(n, KD)
                    if o == 0:
                        pe.wait_ge(hid_done, i * GU_UNITS + (NCH + c + 3))
                    pe.wait_ge(down_added, i * DOWN_UNITS + (n + 1))
                    for t in range(2):
                        last = product(pe, m.ps[:, 4 + n % 4, width(c)], d_h[:, t, o * P:(o + 1) * P],
                                       d_l[:, t, o * P:(o + 1) * P], hid_h[:, t, chunk(c)], hid_l[:, t, chunk(c)],
                                       t == 0, t == 1)
                    last.then_inc(down_done, 1)

        @block.scalar
        def _(act):
            def high_gu(i, t):
                act.activation(gu_h[t][:, :, :], raw_gu[:, :, t * P:(t + 1) * P], ACT.Copy).then_inc(gu_high, 1)

            act.wait_ge(gu_in, 32)
            for t in range(2):
                high_gu(0, t)
            norm.scalar(act)

            def pair(i, more):
                act.wait_ge(d_in, (i + 1) * 16)
                act.wait_ge(down_added, i * DOWN_UNITS + 4)
                act.activation(d_h[:, :, :], raw_d[:, :, :], ACT.Copy).then_inc(d_high, 1)
                for n in range(GU_UNITS):
                    t, c = divmod(n, NCH)
                    act.wait_ge(gu_done, i * GU_UNITS + (n + 1))
                    act.wait_ge(hid_done, i * GU_UNITS + (n + 1))
                    act.activation(silu[:, n % 2, width(c)], m.ps[:, 2 * (n % 2), width(c)], ACT.Silu).then_inc(silu_done, 1)
                    if more and c == NCH - 1:
                        if t == 0:
                            act.wait_ge(gu_in, (i + 2) * 32)
                        high_gu(i + 1, t)

            with act.Fori(0, PAIRS - 1) as i:
                pair(i, True)
            pair(PAIRS - 1, False)

        @block.vector
        def _(dve):
            def low_gu(i, t):
                dve.wait_ge(gu_high, i * 2 + (t + 1))
                dve.tensor_tensor(gu_l[t][:, :, :], raw_gu[:, :, t * P:(t + 1) * P], gu_h[t][:, :, :].bitcast(F32),
                                  ALU.subtract).then_inc(gu_split, 1)

            dve.sem_inc(hid_done, 2)
            dve.sem_inc(down_added, 4)
            for t in range(2):
                low_gu(0, t)
            norm.vector(dve)

            def pair(i, more):
                dve.wait_ge(d_high, i + 1)
                dve.tensor_tensor(d_l[:, :, :], raw_d[:, :, :], d_h[:, :, :].bitcast(F32),
                                  ALU.subtract).then_inc(d_split, 1)
                order = Count(dve, own, i * (2 * GU_UNITS))
                for n in range(GU_UNITS):
                    t, c = divmod(n, NCH)
                    dve.wait_ge(silu_done, i * GU_UNITS + (n + 1))
                    hid = silu[:, n % 2, width(c)]
                    order.then_wait(dve.tensor_tensor(hid, hid, m.ps[:, 2 * (n % 2) + 1, width(c)], ALU.mult))
                    order.then_wait(dve.tensor_copy(hid_h[:, t, chunk(c)], hid))
                    dve.tensor_tensor(hid_l[:, t, chunk(c)], hid, hid_h[:, t, chunk(c)].bitcast(F32),
                                      ALU.subtract).then_inc(hid_done, 1)
                    if more and c == NCH - 1:
                        low_gu(i + 1, t)
                for n in range(DOWN_UNITS):
                    c, o = divmod(n, KD)
                    dve.wait_ge(down_done, i * DOWN_UNITS + (n + 1))
                    dve.scalar_tensor_tensor(m.x[:, o, chunk(c)], m.ps[:, 4 + n % 4, width(c)], 0.5, m.x[:, o, chunk(c)],
                                             ALU.mult, ALU.add).then_inc(down_added, 1)

            with dve.Fori(0, PAIRS - 1) as i:
                pair(i, True)
            pair(PAIRS - 1, False)


def final(nc, m, y_prompt, y_sample):
    with Stage(nc, "final") as st:
        yt = st.sbuf("yt", [P, KD, T])
        norm = Norm(st, m, G_FINAL, (5, 6, 7), yt, None)
        tok = st.sbuf("tok", [P, TB, D])
        stok = st.sbuf("stok", [NS, D])
        turned = st.sem("turned")
        taken = st.sem("taken")
        taken_sample = st.sem("taken_sample")
        out_done = st.sem("out_done")
        block = st.block()
        yp = y_prompt.rearrange("a (b p) d -> p (a b) d", p=P)

        @block.tensor
        def _(pe):
            norm.tensor(pe)
            for n in range(2 * TB):
                b, half = divmod(n, 2)
                last_chunk = ((b + 1) * P - 1) // CH
                pe.wait_ge(norm.high_done, KD * (last_chunk + 1))
                if n < 4:
                    pe.wait_ge(norm.shifted, NCH)
                else:
                    pe.wait_ge(taken, n - 3)
                for k in range(4):
                    last = pe.transpose(m.ps[:, n % 4, k * P:(k + 1) * P], yt[:, 4 * half + k, b * P:(b + 1) * P],
                                        m.ident[:, :])
                last.then_inc(turned, 1)
            for k in range(KD):
                last = pe.transpose(m.ps[0:NS, 4 + k // 4, (k % 4) * P:(k % 4 + 1) * P], yt[:, k, SEQ:T], m.ident[:, :])
            last.then_inc(turned, 1)

        @block.scalar
        def _(act):
            norm.scalar(act)

        @block.vector
        def _(dve):
            norm.vector(dve)
            for n in range(2 * TB):
                b, half = divmod(n, 2)
                dve.wait_ge(turned, n + 1)
                dve.tensor_copy(tok[:, b, half * 512:(half + 1) * 512], m.ps[:, n % 4, :]).then_inc(taken, 1)
            dve.wait_ge(turned, 2 * TB + 1)
            dve.tensor_copy(stok[:, :].rearrange("n (a f) -> n a f", a=2), m.ps[0:NS, 4:6, :]).then_inc(taken_sample, 1)

        @block.sync
        def _(sp):
            for b in range(TB):
                sp.wait_ge(taken, 2 * (b + 1))
                sp.dma_start(yp[:, b, :], tok[:, b, :]).then_inc(out_done, 16)
            sp.wait_ge(taken_sample, 1)
            sp.dma_start(y_sample.rearrange("n a d -> (n a) d"), stok[:, :]).then_inc(out_done, 16)
            sp.wait_ge(out_done, 16 * (TB + 1))


GROUPS = ((128, 1), (512, 4), (2048, 16))
NG = len(GROUPS)
HG = 4
DH = 64
GW = HG * DH
QKV = NG * GW
NPOOL = 4
POOL_W = NPOOL * P
MH = 4
MEM = 256
MEM_W = MH * P
Z_COL = 3 * QKV
QM_COL = Z_COL + POOL_W
GATE_COL = QM_COL + MEM_W
NEG = -1e30
REACH = 128
RES = GW + 2 * HG


class Product:

    def __init__(self, st, m, w, cols, pairs, name, dve_alone=False):
        self.m, self.w, self.cols, self.pairs, self.dve_alone = m, w, cols, pairs, dve_alone
        self.raw = st.sbuf(f"{name}_raw", [P, KD, 2 * P])
        self.high = [st.sbuf(f"{name}_h{t}", [P, KD, P], F32R) for t in range(2)]
        self.low = [st.sbuf(f"{name}_l{t}", [P, KD, P], F32R) for t in range(2)]
        self.w_in = st.sem(f"{name}_w_in")
        self.w_high = st.sem(f"{name}_w_high")
        self.w_split = st.sem(f"{name}_w_split")
        self.done = st.sem(f"{name}_done")
        self.taken_act = st.sem(f"{name}_taken_act")
        self.taken_dve = st.sem(f"{name}_taken_dve")

    def load(self, sp):
        def one(i):
            sp.dma_start(self.raw[:, :, :], self.w[:, :, bass.ds(self.cols(i), 2 * P)]).then_inc(self.w_in, 16)

        one(0)
        if self.pairs > 1:
            with sp.Fori(1, self.pairs) as i:
                sp.wait_ge(self.w_split, i * 2)
                one(i)

    def tensor(self, pe, ready=None):
        with pe.Fori(0, self.pairs) as i:
            for n in range(2 * NCH):
                t, c = divmod(n, NCH)
                if c == 0:
                    pe.wait_ge(self.w_split, i * 2 + (t + 1))
                if ready is not None:
                    pe.wait_ge(ready, c + 1)
                if self.dve_alone:
                    pe.wait_ge(self.taken_dve, i * (2 * NCH) + (n + 1))
                else:
                    pe.wait_ge(self.taken_act if n % 2 == 0 else self.taken_dve, i * NCH + (n // 2 + 1))
                for k in range(KD):
                    last = product(pe, self.m.ps[:, n, width(c)], self.high[t][:, k, :], self.low[t][:, k, :],
                                   self.m.uh[:, k, chunk(c)], self.m.ul[:, k, chunk(c)], k == 0, k == KD - 1)
                last.then_inc(self.done, 1)

    def scalar_first(self, act):
        act.sem_inc(self.taken_act, NCH)
        act.wait_ge(self.w_in, 16)
        for t in range(2):
            self.split_high(act, 0, t)

    def split_high(self, act, i, t):
        act.activation(self.high[t][:, :, :], self.raw[:, :, t * P:(t + 1) * P], ACT.Copy).then_inc(self.w_high, 1)

    def vector_first(self, dve):
        dve.sem_inc(self.taken_dve, 2 * NCH if self.dve_alone else NCH)
        for t in range(2):
            self.split_low(dve, 0, t)

    def split_low(self, dve, i, t):
        dve.wait_ge(self.w_high, i * 2 + (t + 1))
        dve.tensor_tensor(self.low[t][:, :, :], self.raw[:, :, t * P:(t + 1) * P], self.high[t][:, :, :].bitcast(F32),
                          ALU.subtract).then_inc(self.w_split, 1)

    def scalar(self, act, take):
        def pair(i, more):
            for n in range(2 * NCH):
                t, c = divmod(n, NCH)
                if n % 2 == 0 and not self.dve_alone:
                    act.wait_ge(self.done, i * (2 * NCH) + (n + 1))
                    take(act, i, t, c, self.m.ps[:, n, width(c)]).then_inc(self.taken_act, 1)
                if more and c == NCH - 1:
                    act.wait_ge(self.done, i * (2 * NCH) + (n + 1))
                    act.wait_ge(self.w_in, (i + 2) * 16)
                    self.split_high(act, i + 1, t)
        self.each(act, pair)

    def vector(self, dve, take):
        def pair(i, more):
            for n in range(2 * NCH):
                t, c = divmod(n, NCH)
                if n % 2 == 1 or self.dve_alone:
                    dve.wait_ge(self.done, i * (2 * NCH) + (n + 1))
                    take(dve, i, t, c, self.m.ps[:, n, width(c)]).then_inc(self.taken_dve, 1)
                if more and c == NCH - 1:
                    self.split_low(dve, i + 1, t)
        self.each(dve, pair)

    def each(self, eng, pair):
        if self.pairs > 1:
            with eng.Fori(0, self.pairs - 1) as i:
                pair(i, True)
        pair(self.pairs - 1, False)


def copy(eng, act, out, src):
    return eng.activation(out, src, ACT.Copy) if act else eng.tensor_copy(out, src)


def bias_tables(nc, m, rel_bias, onehot_in):
    with Stage(nc, "bias") as st:
        rel = st.sbuf("rel", [32, NG * HG])
        hot = st.sbuf("hot", [32, 2, NG, REACH + 1])
        rows = st.sbuf("table", [NG * HG, NG, 384])
        loaded = st.sem("loaded")
        cleared = st.sem("cleared")
        made = st.sem("made")
        taken = st.sem("taken")
        stored = st.sem("stored")
        block = st.block()

        @block.sync
        def _(sp):
            sp.dma_start(rel[:, :], rel_bias).then_inc(loaded, 16)
            sp.dma_start(hot[:, :, :, :], onehot_in).then_inc(loaded, 16)
            sp.wait_ge(taken, 3)
            sp.dma_start(m.bias_rows.rearrange("g h y -> h g y"), rows[:, :, :]).then_inc(stored, 16)
            sp.wait_ge(stored, 16)

        @block.tensor
        def _(pe):
            pe.wait_ge(loaded, 32)
            for g in range(NG):
                pe.matmul(m.ps[0:NG * HG, g, 0:REACH + 1], rel[:, :], hot[:, 1, g, :], start=True, stop=True)
                pe.matmul(m.ps[:, 3, 16 * g:16 * g + NG * HG], hot[:, 0, g, 0:REACH], rel[:, :], start=True, stop=True)
            pe.matmul(m.ps[0:NS, 4, 0:NG * HG], hot[:, 0, 0, REACH:REACH + 1].to_broadcast([32, NS]), rel[:, :],
                      start=True, stop=True).then_inc(made, 1)

        @block.vector
        def _(dve):
            dve.memset(rows[:, :, :], NEG).then_inc(cleared, 1)
            dve.wait_ge(cleared, 1)
            dve.wait_ge(made, 1)
            dve.tensor_copy(rows[:, :, 127:127 + REACH + 1], m.ps[0:NG * HG, 0:NG, 0:REACH + 1]).then_inc(taken, 1)
            for g in range(NG):
                ins = dve.tensor_copy(m.cache_bias[:, g, :], m.ps[:, 3, 16 * g + HG * g:16 * g + HG * g + HG])
            ins.then_inc(taken, 1)
            dve.tensor_copy(m.new_bias[:, :], m.ps[0:NS, 4, 0:NG * HG]).then_inc(taken, 1)


def blocks_of(g):
    in_residue = SEQ // GROUPS[g][1] // P
    return [(b, in_residue > 1 and b % in_residue != 0) for b in range(TB)]


def attention(nc, m, g, w_in, new_kv, norm_first):
    window, dil = GROUPS[g]
    length = SEQ // dil
    blocks = blocks_of(g)
    with Stage(nc, f"att{g}") as st:
        qkv = st.sbuf("qkv", [P, 6, T])
        with Stage(nc, f"qkv{g}") as pt:
            proj = Product(pt, m, w_in, lambda i: i * QKV + g * GW, 3, "w")
            norm = Norm(pt, m, G_MIX, (6, 7, 5), m.uh, m.ul) if norm_first else None
            block = pt.block()

            def take(act):
                def one(eng, i, t, c, src):
                    n_l = (min(CHUNKS[c][0] + CHUNKS[c][1], SEQ) - CHUNKS[c][0]) // dil
                    l0 = CHUNKS[c][0] // dil
                    out = qkv[:, bass.ds(i * 2 + t, 1), 0:SEQ].rearrange("p a (r l) -> p (a r) l", r=dil)[:, :, l0:l0 + n_l]
                    return copy(eng, act, out, src[:, 0:n_l * dil].rearrange("p (l r) -> p r l", r=dil))
                return one

            samples_taken = pt.sem("samples_taken")

            @block.sync
            def _(sp):
                proj.load(sp)

            @block.tensor
            def _(pe):
                if norm:
                    norm.tensor(pe)
                    pe.wait_ge(norm.shifted, NCH)
                proj.tensor(pe, norm.ready if norm else None)

            @block.scalar
            def _(act):
                proj.scalar_first(act)
                if norm:
                    norm.scalar(act)
                one = take(True)

                def with_samples(eng, i, t, c, src):
                    if c == NCH - 1:
                        eng.activation(m.s_qkv[:, bass.ds(i * (2 * NG) + (2 * g + t), 1), :],
                                       src[:, SEQ - CHUNKS[c][0]:].unsqueeze(1), ACT.Copy)
                    return one(eng, i, t, c, src)
                proj.scalar(act, with_samples)

            @block.vector
            def _(dve):
                proj.vector_first(dve)
                if norm:
                    norm.vector(dve)
                one = take(False)

                def with_samples(eng, i, t, c, src):
                    if c == NCH - 1:
                        eng.tensor_copy(m.s_qkv[:, bass.ds(i * (2 * NG) + (2 * g + t), 1), :],
                                        src[:, SEQ - CHUNKS[c][0]:].unsqueeze(1)).then_inc(samples_taken, 1)
                    return one(eng, i, t, c, src)
                proj.vector(dve, with_samples)

        kv = st.sbuf("kv", [P, TB, 2 * GW])
        bias = st.sbuf("bias", [P, HG, 2 * P])
        falling = st.sbuf("falling", [P, HG, 2 * P])
        logit = st.sbuf("logit", [P, 2, HG, 2 * P])
        prob = st.sbuf("prob", [P, 2, HG, 2 * P])
        turned = st.sbuf("turned", [P, 2, 2, HG, P])
        res = st.sbuf("res", [P, TB, RES])
        neg = st.sbuf("neg", [P, 2, HG])
        bias_in = st.sem("bias_in")
        bias_ready = st.sem("bias_ready")
        kv_turned = st.sem("kv_turned")
        kv_taken = st.sem("kv_taken")
        scored = st.sem("scored")
        logits = st.sem("logits")
        maxed = st.sem("maxed")
        negated = st.sem("negated")
        exped = st.sem("exped")
        p_turned = st.sem("p_turned")
        p_taken_act = st.sem("p_taken_act")
        p_taken_dve = st.sem("p_taken_dve")
        weighed = st.sem("weighed")
        res_taken = st.sem("res_taken")
        stored = st.sem("stored")
        block = st.block()
        head_at = [2 * (i % 2) + i // 2 for i in range(HG)]

        def seen(b):
            return slice(0 if blocks[b][1] else P, 2 * P)

        kv_out = new_kv.rearrange("a n t c h d -> (a n t) (c h d)")
        kept = kv_out.shape[0]

        @block.sync
        def _(sp):
            for i, h in enumerate(head_at):
                row = m.bias_rows[g, g * HG + h, :]
                tile = bass.AP(row.tensor, row.offset, [[1, P], [1, 2 * P]])
                sp.dma_start(falling[:, i, :], tile).then_inc(bias_in, 16)
            n_out = 0
            for b in range(TB):
                for part in range(max(1, P // length)):
                    rows = min(P, length)
                    r, l0 = divmod(b * P + part * rows, length)
                    t_first = l0 * dil + r
                    if t_first >= SEQ - kept or g == 2:
                        n_out += 1
                        if part == 0:
                            sp.wait_ge(kv_taken, b + 1)
                        dst = kv_out.rearrange("(l r) c -> r l c", r=dil)[r, l0 - (SEQ - kept) // dil:l0 - (SEQ - kept) // dil + rows, :]
                        sp.dma_start(dst, kv[part * rows:(part + 1) * rows, b, :]).then_inc(stored, 16)
            for b in range(TB):
                sp.wait_ge(res_taken, b + 1)
                for part in range(max(1, P // length)):
                    rows = min(P, length)
                    r, l0 = divmod(b * P + part * rows, length)
                    dst = m.group_out.rearrange("(l r) g c -> r l g c", r=dil)[r, l0:l0 + rows, g, :]
                    n_out += 1
                    sp.dma_start(dst, res[part * rows:(part + 1) * rows, b, :]).then_inc(stored, 16)
            sp.wait_ge(stored, 16 * n_out)

        @block.tensor
        def _(pe):
            for b in range(TB):
                if b >= 2:
                    pe.wait_ge(kv_taken, b - 1)
                for i in range(4):
                    last = pe.transpose(m.ps[:, 4 + b % 2, i * P:(i + 1) * P], qkv[:, 2 + i, b * P:(b + 1) * P],
                                        m.ident[:, :])
                last.then_inc(kv_turned, 1)

            def scores(b):
                if b >= 2:
                    pe.wait_ge(logits, b - 1)
                for i, h in enumerate(head_at):
                    rows = slice(DH * (h % 2), DH * (h % 2) + DH)
                    bank = 2 * (b % 2) + i // 2
                    w = seen(b)
                    last = pe.matmul(m.ps[:, bank, (i % 2) * 2 * P + w.start:(i % 2 + 1) * 2 * P],
                                     qkv[rows, h // 2, b * P:(b + 1) * P],
                                     qkv[rows, 2 + h // 2, (b - 1) * P + w.start:(b + 1) * P], start=True, stop=True)
                last.then_inc(scored, 1)

            def turn(b):
                pe.wait_ge(exped, HG * (b + 1))
                if b == 0:
                    pe.wait_ge(kv_taken, TB)
                else:
                    pe.wait_ge(p_taken_act, b)
                    pe.wait_ge(p_taken_dve, b)
                for kb in range(0 if blocks[b][1] else 1, 2):
                    for i in range(HG):
                        last = pe.transpose(m.ps[:, 4 + kb, i * P:(i + 1) * P], prob[:, b % 2, i, kb * P:(kb + 1) * P],
                                            m.ident[:, :])
                last.then_inc(p_turned, 1)

            def weigh(b):
                pe.wait_ge(p_taken_act, b + 1)
                pe.wait_ge(p_taken_dve, b + 1)
                if b >= 2:
                    pe.wait_ge(res_taken, b - 1)
                for i, h in enumerate(head_at):
                    first = 0 if blocks[b][1] else 1
                    for kb in range(first, 2):
                        last = pe.matmul(m.ps[:, 6 + b % 2, h * DH:(h + 1) * DH], turned[:, b % 2, kb, i, :],
                                         kv[:, b - 1 + kb, GW + h * DH:GW + (h + 1) * DH],
                                         start=kb == first, stop=kb == 1)
                last.then_inc(weighed, 1)

            scores(0)
            scores(1)
            for b in range(TB):
                turn(b)
                if b + 2 < TB:
                    scores(b + 2)
                weigh(b)

        @block.scalar
        def _(act):
            def exps(b):
                act.wait_ge(negated, b + 1)
                if b >= 2:
                    act.wait_ge(p_turned, b - 1)
                w = seen(b)
                for i in range(HG):
                    act.activation(prob[:, b % 2, i, w], logit[:, b % 2, i, w], ACT.Exp, bias=neg[:, b % 2, i:i + 1],
                                   accum_out=res[:, b, GW + i:GW + i + 1]).then_inc(exped, 1)

            exps(0)
            for b in range(TB):
                if b + 1 < TB:
                    exps(b + 1)
                act.wait_ge(p_turned, b + 1)
                if b >= 2:
                    act.wait_ge(weighed, b - 1)
                act.activation(turned[:, b % 2, 1, :, :], m.ps[:, 5, :].rearrange("p (i q) -> p i q", i=HG),
                               ACT.Copy).then_inc(p_taken_act, 1)

        @block.vector
        def _(dve):
            for b in range(TB):
                dve.wait_ge(kv_turned, b + 1)
                dve.tensor_copy(kv[:, b, :], m.ps[:, 4 + b % 2, :]).then_inc(kv_taken, 1)
            dve.wait_ge(bias_in, 16 * HG)
            dve.tensor_copy(bias[:, :, :], falling[:, :, ::-1]).then_inc(bias_ready, 1)
            dve.wait_ge(bias_ready, 1)
            if length < P:
                dve.memset(bias[length:P, :, P:P + length], NEG).then_inc(bias_ready, 1)
                dve.wait_ge(bias_ready, 2)

            def soft(b):
                w = seen(b)
                dve.wait_ge(scored, b + 1)
                if b >= 2:
                    dve.wait_ge(exped, HG * (b - 1))
                src = m.ps[:, 2 * (b % 2):2 * (b % 2) + 2, :].rearrange("p a (i k) -> p (a i) k", k=2 * P)
                dve.scalar_tensor_tensor(logit[:, b % 2, :, w], src[:, :, w], DH ** -0.5, bias[:, :, w], ALU.mult,
                                         ALU.add).then_inc(logits, 1)
                dve.wait_ge(logits, b + 1)
                dve.tensor_reduce(res[:, b, GW + HG:GW + 2 * HG], logit[:, b % 2, :, w], AX_X,
                                  ALU.max).then_inc(maxed, 1)
                dve.wait_ge(maxed, b + 1)
                dve.tensor_scalar(neg[:, b % 2, :], res[:, b, GW + HG:GW + 2 * HG], -1.0, None,
                                  ALU.mult).then_inc(negated, 1)

            soft(0)
            for b in range(TB):
                if b + 1 < TB:
                    soft(b + 1)
                dve.wait_ge(p_turned, b + 1)
                if b >= 2:
                    dve.wait_ge(weighed, b - 1)
                if blocks[b][1]:
                    dve.tensor_copy(turned[:, b % 2, 0, :, :], m.ps[:, 4, :].rearrange("p (i q) -> p i q", i=HG)
                                    ).then_inc(p_taken_dve, 1)
                else:
                    dve.sem_inc(p_taken_dve, 1)
                if b >= 1:
                    dve.wait_ge(weighed, b)
                    dve.tensor_copy(res[:, b - 1, 0:GW], m.ps[:, 6 + (b - 1) % 2, 0:GW]).then_inc(res_taken, 1)
            dve.wait_ge(weighed, TB)
            dve.tensor_copy(res[:, TB - 1, 0:GW], m.ps[:, 6 + (TB - 1) % 2, 0:GW]).then_inc(res_taken, 1)


def combine(nc, m, ah, al):
    with Stage(nc, "combine") as st:
        part = st.sbuf("part", [P, TB, NG, RES])
        top = st.sbuf("top", [P, TB, HG])
        fall = st.sbuf("fall", [P, NG, TB, HG])
        den = st.sbuf("den", [P, TB, HG])
        whole = st.sbuf("whole", [P, TB, GW])
        loaded = st.sem("loaded")
        shifted = st.sem("shifted")
        exped = st.sem("exped")
        summed = st.sem("summed")
        turned = st.sem("turned")
        high = st.sem("high")
        own = st.sem("own")
        block = st.block()

        @block.sync
        def _(sp):
            sp.dma_start(part[:, :, :, :], m.group_out.rearrange("(b p) g c -> p b g c", p=P)).then_inc(loaded, 16)

        @block.vector
        def _(dve):
            order = Count(dve, own)
            dve.wait_ge(loaded, 16)
            maxima = [part[:, :, g, GW + HG:RES] for g in range(NG)]
            order.then_wait(dve.tensor_tensor(top[:, :, :], maxima[0], maxima[1], ALU.max))
            order.then_wait(dve.tensor_tensor(top[:, :, :], top[:, :, :], maxima[2], ALU.max))
            for g in range(NG):
                ins = dve.tensor_tensor(fall[:, g, :, :], maxima[g], top[:, :, :], ALU.subtract)
                ins.then_inc(shifted, 1)
            dve.wait_ge(exped, 1)
            for g in range(NG):
                sums = part[:, :, g, GW:GW + HG]
                order.then_wait(dve.tensor_tensor(sums, sums, fall[:, g, :, :], ALU.mult))
            order.then_wait(dve.tensor_tensor(den[:, :, :], part[:, :, 0, GW:GW + HG], part[:, :, 1, GW:GW + HG], ALU.add))
            order.then_wait(dve.tensor_tensor(den[:, :, :], den[:, :, :], part[:, :, 2, GW:GW + HG], ALU.add))
            order.then_wait(dve.reciprocal(den[:, :, :], den[:, :, :]))
            for g in range(NG):
                order.then_wait(dve.tensor_tensor(fall[:, g, :, :], fall[:, g, :, :], den[:, :, :], ALU.mult))
            for g in range(NG):
                for par in range(2):
                    vals = part[:, :, g, 0:GW].rearrange("p b (hh par d) -> p par b hh d", hh=2, par=2)[:, par]
                    w = fall[:, g, :, 2 * par:2 * par + 2].unsqueeze(3).to_broadcast([P, TB, 2, DH])
                    order.then_wait(dve.tensor_tensor(vals, vals, w, ALU.mult))
            sl = [part[:, :, g, 0:GW] for g in range(NG)]
            order.then_wait(dve.tensor_tensor(whole[:, :, :], sl[0], sl[1], ALU.add))
            dve.tensor_tensor(whole[:, :, :], whole[:, :, :], sl[2], ALU.add).then_inc(summed, 1)
            for n in range(4):
                dve.wait_ge(high, n + 1)
                k, half = divmod(n, 2)
                dve.tensor_tensor(al[:, k, half * 512:(half + 1) * 512], m.ps[:, n, :],
                                  ah[:, k, half * 512:(half + 1) * 512].bitcast(F32), ALU.subtract)
            dve.wait_ge(high, 5)
            dve.tensor_tensor(al[:, :, SEQ:T], m.s_att[:, :, :], ah[:, :, SEQ:T].bitcast(F32), ALU.subtract)

        @block.scalar
        def _(act):
            act.wait_ge(shifted, NG)
            act.activation(fall[:, :, :, :], fall[:, :, :, :], ACT.Exp).then_inc(exped, 1)
            for n in range(4):
                k, half = divmod(n, 2)
                act.wait_ge(turned, n + 1)
                act.activation(ah[:, k, half * 512:(half + 1) * 512], m.ps[:, n, :], ACT.Copy).then_inc(high, 1)
            act.activation(ah[:, :, SEQ:T], m.s_att[:, :, :], ACT.Copy).then_inc(high, 1)

        @block.tensor
        def _(pe):
            pe.wait_ge(summed, 1)
            for n in range(4):
                k, half = divmod(n, 2)
                for b in range(4):
                    last = pe.transpose(m.ps[:, n, b * P:(b + 1) * P], whole[:, 4 * half + b, k * P:(k + 1) * P],
                                        m.ident[:, :])
                last.then_inc(turned, 1)


def merge(nc, m, name, branch, first, w_in, w_o, bh, bl, kt):
    with Stage(nc, name) as st:
        raw_g = st.sbuf("raw_g", [P, KD, 2 * P])
        raw_o = st.sbuf("raw_o", [P, kt, 2 * P])
        w_h = [st.sbuf(f"w_h{t}", [P, KD + kt, P], F32R) for t in range(2)]
        w_l = [st.sbuf(f"w_l{t}", [P, KD + kt, P], F32R) for t in range(2)]
        gate = st.sbuf("gate", [P, 2, CH])
        w_arrived = st.sem("w_arrived")
        w_high = st.sem("w_high")
        w_split = st.sem("w_split")
        done = st.sem("done")
        gated = st.sem("gated")
        own = st.sem("own")
        mixed = st.sem("mixed")
        block = st.block()
        units = 2 * NCH
        pairs = KD // 2

        @block.sync
        def _(sp):
            def load(i):
                sp.dma_start(raw_g[:, :, :], w_in[:, :, bass.ds(i * (2 * P) + (GATE_COL + branch * D), 2 * P)]).then_inc(w_arrived, 16)
                sp.dma_start(raw_o[:, :, :], w_o[:, :, bass.ds(i * (2 * P), 2 * P)]).then_inc(w_arrived, 16)

            load(0)
            with sp.Fori(1, pairs) as i:
                sp.wait_ge(w_split, i * 2)
                load(i)

        @block.tensor
        def _(pe):
            with pe.Fori(0, pairs) as i:
                for n in range(units):
                    t, c = divmod(n, NCH)
                    if c == 0:
                        pe.wait_ge(w_split, i * 2 + (t + 1))
                    pe.wait_ge(mixed, i * units + (n + 1))
                    for k in range(KD):
                        product(pe, m.ps[:, 2 * (n % 3), width(c)], w_h[t][:, k, :], w_l[t][:, k, :],
                                m.uh[:, k, chunk(c)], m.ul[:, k, chunk(c)], k == 0, k == KD - 1)
                    for k in range(kt):
                        last = product(pe, m.ps[:, 2 * (n % 3) + 1, width(c)], w_h[t][:, KD + k, :], w_l[t][:, KD + k, :],
                                       bh[:, k, chunk(c)], bl[:, k, chunk(c)], k == 0, k == kt - 1)
                    last.then_inc(done, 1)

        @block.scalar
        def _(act):
            def high(i, t):
                act.activation(w_h[t][:, 0:KD, :], raw_g[:, :, t * P:(t + 1) * P], ACT.Copy)
                act.activation(w_h[t][:, KD:, :], raw_o[:, :, t * P:(t + 1) * P], ACT.Copy).then_inc(w_high, 1)

            act.wait_ge(w_arrived, 32)
            for t in range(2):
                high(0, t)

            def pair(i, more):
                for n in range(units):
                    t, c = divmod(n, NCH)
                    act.wait_ge(done, i * units + (n + 1))
                    act.wait_ge(mixed, i * units + (n + 2))
                    act.activation(gate[:, n % 2, width(c)], m.ps[:, 2 * (n % 3), width(c)], ACT.Sigmoid).then_inc(gated, 1)
                    if more and c == NCH - 1:
                        if t == 0:
                            act.wait_ge(w_arrived, (i + 2) * 32)
                        high(i + 1, t)

            with act.Fori(0, pairs - 1) as i:
                pair(i, True)
            pair(pairs - 1, False)

        @block.vector
        def _(dve):
            def low(i, t):
                dve.wait_ge(w_high, i * 2 + (t + 1))
                dve.tensor_tensor(w_l[t][:, 0:KD, :], raw_g[:, :, t * P:(t + 1) * P], w_h[t][:, 0:KD, :].bitcast(F32),
                                  ALU.subtract)
                dve.tensor_tensor(w_l[t][:, KD:, :], raw_o[:, :, t * P:(t + 1) * P], w_h[t][:, KD:, :].bitcast(F32),
                                  ALU.subtract).then_inc(w_split, 1)

            dve.sem_inc(mixed, 3)
            for t in range(2):
                low(0, t)

            def pair(i, more):
                order = Count(dve, own, i * units)
                for n in range(units):
                    t, c = divmod(n, NCH)
                    dve.wait_ge(gated, i * units + (n + 1))
                    g = gate[:, n % 2, width(c)]
                    proj = m.ps[:, 2 * (n % 3) + 1, width(c)]
                    mix = m.mix[:, bass.ds(i * 2 + t, 1), chunk(c)].rearrange("p a t -> p (a t)")
                    if first:
                        dve.tensor_tensor(mix, g, proj, ALU.mult).then_inc(mixed, 1)
                    else:
                        order.then_wait(dve.tensor_tensor(g, g, proj, ALU.mult))
                        dve.tensor_tensor(mix, mix, g, ALU.add).then_inc(mixed, 1)
                    if more and c == NCH - 1:
                        low(i + 1, t)

            with dve.Fori(0, pairs - 1) as i:
                pair(i, True)
            pair(pairs - 1, False)


def mix_out(nc, m, w_out):
    with Stage(nc, "mix_out") as st:
        proj = Product(st, m, w_out, lambda i: i * (2 * P), KD // 2, "w", dve_alone=True)
        high = st.sem("high")
        low = st.sem("low")
        block = st.block()

        @block.sync
        def _(sp):
            proj.load(sp)

        @block.tensor
        def _(pe):
            proj.tensor(pe, low)

        @block.scalar
        def _(act):
            proj.scalar_first(act)
            for c in range(NCH):
                act.activation(m.uh[:, :, chunk(c)], m.mix[:, :, chunk(c)], ACT.Copy).then_inc(high, 1)
            proj.scalar(act, None)

        @block.vector
        def _(dve):
            proj.vector_first(dve)
            for c in range(NCH):
                dve.wait_ge(high, c + 1)
                dve.tensor_tensor(m.ul[:, :, chunk(c)], m.mix[:, :, chunk(c)], m.uh[:, :, chunk(c)].bitcast(F32),
                                  ALU.subtract).then_inc(low, 1)

            def add(eng, i, t, c, src):
                x = m.x[:, bass.ds(i * 2 + t, 1), chunk(c)].rearrange("p a t -> p (a t)")
                return eng.tensor_tensor(x, x, src, ALU.add)
            proj.vector(dve, add)


def sample_attention(nc, m, caches, new_kv):
    rows = NS * HG
    with Stage(nc, "samp") as st:
        cache = [st.sbuf(f"cache{g}", [REACH, NS, 2 * GW]) for g in range(NG)]
        tok = st.sbuf("tok", [NS, 3 * QKV])
        sel = st.sbuf("sel", [NS, NS, P])
        own_of = st.sbuf("own_of", [rows, NS])
        prod = st.sbuf("prod", [P, QKV])
        score = st.sbuf("score", [P, NG, NS, HG])
        new_prod = st.sbuf("new_prod", [NS, QKV])
        new_score = st.sbuf("new_score", [NS, NG, HG])
        prob = st.sbuf("prob", [rows, NG, REACH + 1])
        small = st.sbuf("small", [rows, 4])
        diag = st.sbuf("diag", [rows, NG, rows])
        p_cols = st.sbuf("p_cols", [P, NG, rows])
        new_p = st.sbuf("new_p", [NS, NG, rows])
        cache_in = [st.sem(f"cache_in{g}") for g in range(NG)]
        const_in = st.sem("const_in")
        stored = st.sem("stored")
        new_out = st.sem("new_out")
        new_back = st.sem("new_back")
        pe_done = st.sem("pe_done")
        spread = st.sem("spread")
        tok_taken = st.sem("tok_taken")
        new_scored = st.sem("new_scored")
        scored = st.sem("scored")
        own = st.sem("own")
        logits = st.sem("logits")
        maxed = st.sem("maxed")
        exped = st.sem("exped")
        normal = st.sem("normal")
        cols_taken = st.sem("cols_taken")
        block = st.block()
        STEP_TOK, STEP_ROWS, STEP_COLS, STEP_OUT = 1, 2, 3, 4

        @block.sync
        def _(sp):
            sp.dma_start(sel[:, :, :], m.sel_in).then_inc(const_in, 16)
            sp.dma_start(own_of[:, :], m.own_in).then_inc(const_in, 16)
            for g in range(NG):
                src = caches[g].rearrange("a n (r d) c h e -> r d (a n) (c h e)", d=GROUPS[g][1])[:, 0]
                sp.dma_start(cache[g][:, :, :], src).then_inc(cache_in[g], 16)
            sp.wait_ge(tok_taken, 5)
            for g in range(NG):
                dst = new_kv[g].rearrange("a n t c h e -> (a n t) c (h e)")
                for side in range(2):
                    sp.dma_start(dst[:, side, :], tok[:, (1 + side) * QKV + g * GW:(1 + side) * QKV + (g + 1) * GW]
                                 ).then_inc(stored, 16)
            sp.wait_ge(new_scored, 1)
            with nc.allow_non_contiguous_dma(reason="96 scores"):
                for g in range(NG):
                    sp.dma_start(m.new_scores[:, :, g], new_score[:, g, :]).then_inc(new_out, 16)
                sp.wait_ge(new_out, 16 * NG)
                sp.dma_start(prob[:, :, REACH], m.new_scores.rearrange("n h g -> (n h) g")).then_inc(new_back, 16)
            sp.wait_ge(stored, 16 * 2 * NG)

        @block.tensor
        def _(pe):
            for i in range(18):
                last = pe.transpose(m.ps[0:NS, i // 4, (i % 4) * P:(i % 4 + 1) * P], m.s_qkv[:, i, :], m.ident[:, :])
            last.then_inc(pe_done, 1)
            pe.wait_ge(tok_taken, 5)
            pe.wait_ge(const_in, 32)
            for n in range(NS):
                if n >= 2:
                    pe.wait_ge(own, n - 1)
                for g in range(NG):
                    at = g * GW
                    last = pe.matmul(m.ps[:, 2 * (n % 2) + at // 512, at % 512:at % 512 + GW], sel[:, n, :],
                                     tok[:, at:at + GW], start=True, stop=True)
                last.then_inc(spread, 1)
            pe.wait_ge(logits, 1)
            for g in range(NG):
                last = pe.transpose(m.ps[0:rows, 4, g * P:(g + 1) * P], score[:, g, :, :].rearrange("p n h -> p (n h)"),
                                    m.ident[:, :])
            last.then_inc(pe_done, 1)
            pe.wait_ge(normal, 2)
            for g in range(NG):
                pe.transpose(m.ps[:, 5, g * rows:(g + 1) * rows], prob[:, g, 0:REACH], m.ident[0:rows, 0:rows])
            pe.matmul(m.ps[0:NS, 6, 0:NG * rows], own_of[:, :], diag[:, :, :].rearrange("p g r -> p (g r)"),
                      start=True, stop=True).then_inc(pe_done, 1)
            pe.wait_ge(cols_taken, 2)
            for c in range(2):
                for g in range(NG):
                    v = 2 * QKV + g * GW + c * P
                    pe.matmul(m.ps[:, c, 0:rows], tok[:, v:v + P], new_p[:, g, :], start=g == 0, stop=False,
                              skip_group_check=True)
                for n in range(NS):
                    for g in range(NG):
                        last = pe.matmul(m.ps[:, c, n * HG:(n + 1) * HG], cache[g][:, n, GW + c * P:GW + (c + 1) * P],
                                         p_cols[:, g, n * HG:(n + 1) * HG], start=False,
                                         stop=n == NS - 1 and g == NG - 1, skip_group_check=True)
            last.then_inc(pe_done, 1)

        @block.vector
        def _(dve):
            order = Count(dve, own)
            dve.wait_ge(pe_done, STEP_TOK)
            for b in range(5):
                w = min(512, 3 * QKV - b * 512)
                dve.tensor_copy(tok[:, b * 512:b * 512 + w], m.ps[0:NS, b, 0:w]).then_inc(tok_taken, 1)
            for g in range(NG):
                dve.wait_ge(cache_in[g], 16)
            for n in range(NS):
                dve.wait_ge(spread, n + 1)
                if n >= 1:
                    dve.wait_ge(scored, n)
                for g in range(NG):
                    at = g * GW
                    ins = dve.tensor_tensor(prod[:, at:at + GW], cache[g][:, n, 0:GW],
                                            m.ps[:, 2 * (n % 2) + at // 512, at % 512:at % 512 + GW], ALU.mult)
                order.then_wait(ins)
                dve.tensor_reduce(score[:, :, n, :], prod[:, :].rearrange("p (g h d) -> p g h d", g=NG, h=HG), AX_X,
                                  ALU.add).then_inc(scored, 1)
            dve.wait_ge(scored, NS)
            for g in range(NG):
                ins = dve.scalar_tensor_tensor(score[:, g, :, :], score[:, g, :, :], DH ** -0.5,
                                               m.cache_bias[:, g, :].unsqueeze(1).to_broadcast([P, NS, HG]),
                                               ALU.mult, ALU.add)
            ins.then_inc(logits, 1)
            dve.wait_ge(tok_taken, 5)
            order.then_wait(dve.tensor_tensor(new_prod[:, :], tok[:, 0:QKV], tok[:, QKV:2 * QKV], ALU.mult))
            order.then_wait(dve.tensor_reduce(new_score[:, :, :].rearrange("n g h -> n (g h)"),
                                              new_prod[:, :].rearrange("n (s d) -> n s d", d=DH), AX_X, ALU.add))
            dve.scalar_tensor_tensor(new_score[:, :, :].rearrange("n g h -> n (g h)"),
                                     new_score[:, :, :].rearrange("n g h -> n (g h)"), DH ** -0.5, m.new_bias[:, :],
                                     ALU.mult, ALU.add).then_inc(new_scored, 1)
            dve.wait_ge(pe_done, STEP_ROWS)
            order.then_wait(dve.tensor_copy(prob[:, :, 0:REACH], m.ps[0:rows, 4, 0:NG * P].rearrange("p (g r) -> p g r", g=NG)))
            dve.wait_ge(new_back, 16)
            flat = prob[:, :, :].rearrange("p g r -> p (g r)")
            order.then_wait(dve.tensor_reduce(small[:, 0:1], flat, AX_X, ALU.max))
            dve.tensor_scalar(small[:, 1:2], small[:, 0:1], -1.0, None, ALU.mult).then_inc(maxed, 1)
            dve.wait_ge(exped, 1)
            order.then_wait(dve.reciprocal(small[:, 3:4], small[:, 2:3]))
            dve.tensor_scalar(flat, flat, small[:, 3:4], None, ALU.mult).then_inc(normal, 1)
            dve.wait_ge(normal, 1)
            for g in range(NG):
                ins = dve.tensor_scalar(diag[:, g, :], m.ident[0:rows, 0:rows], prob[:, g, REACH:REACH + 1], None, ALU.mult)
            ins.then_inc(normal, 1)
            dve.wait_ge(pe_done, STEP_COLS)
            dve.tensor_copy(p_cols[:, :, :], m.ps[:, 5, 0:NG * rows].rearrange("p (g r) -> p g r", g=NG)
                            ).then_inc(cols_taken, 1)
            dve.tensor_copy(new_p[:, :, :], m.ps[0:NS, 6, 0:NG * rows].rearrange("p (g r) -> p g r", g=NG)
                            ).then_inc(cols_taken, 1)
            dve.wait_ge(pe_done, STEP_OUT)
            for c in range(2):
                for half in range(2):
                    part = slice(half * DH, (half + 1) * DH)
                    src = m.ps[part, c, 0:rows].rearrange("p (n h) -> p h n", h=HG)[:, 2 * c + half, :]
                    dve.tensor_copy(m.s_att[part, c, :], src)

        @block.scalar
        def _(act):
            act.wait_ge(maxed, 1)
            flat = prob[:, :, :].rearrange("p g r -> p (g r)")
            act.activation(flat, flat, ACT.Exp, bias=small[:, 1:2], accum_out=small[:, 2:3]).then_inc(exped, 1)


POOL_WINDOWS = (2, 4, 8, 16)
HIST = 15
PAD = 16


def pooling(nc, m, w_in, state_pool, w_pool, new_pool_prompt, new_pool_sample, bh, bl):
    with Stage(nc, "pool") as st:
        z = st.sbuf("z", [P, NPOOL, PAD + T])
        with Stage(nc, "z") as pt:
            proj = Product(pt, m, w_in, lambda i: i * (2 * P) + Z_COL, NPOOL // 2, "w")
            cleared = pt.sem("cleared")
            block = pt.block()

            def take(act):
                def one(eng, i, t, c, src):
                    out = z[:, bass.ds(i * 2 + t, 1), PAD + CHUNKS[c][0]:PAD + CHUNKS[c][0] + CHUNKS[c][1]]
                    return copy(eng, act, out.rearrange("p a t -> p (a t)"), src)
                return one

            @block.sync
            def _(sp):
                proj.load(sp)

            @block.tensor
            def _(pe):
                proj.tensor(pe)

            @block.scalar
            def _(act):
                proj.scalar_first(act)
                proj.scalar(act, take(True))

            @block.vector
            def _(dve):
                dve.memset(z[:, :, 0:PAD], 0.0).then_inc(cleared, 1)
                proj.vector_first(dve)
                proj.vector(dve, take(False))

        sums = st.sbuf("sums", [P, 2, PAD + SEQ])
        hist = st.sbuf("hist", [NS * HIST, POOL_W])
        w = st.sbuf("w", [P, NPOOL, P])
        inv = st.sbuf("inv", [P, NPOOL, PAD])
        first = st.sbuf("first", [P, PAD])
        past = st.sbuf("past", [P, NPOOL, NS])
        ztok = st.sbuf("ztok", [HIST, POOL_W])
        zstok = st.sbuf("zstok", [NS, POOL_W])
        loaded = st.sem("loaded")
        turned = st.sem("turned")
        taken = st.sem("taken")
        stored = st.sem("stored")
        own = st.sem("own")
        ready = st.sem("ready")
        mapped = st.sem("mapped")
        high = st.sem("high")
        split = st.sem("split")
        block = st.block()

        @block.sync
        def _(sp):
            sp.dma_start(hist[:, :], state_pool.rearrange("a n r c -> (a n r) c")).then_inc(loaded, 16)
            sp.dma_start(w[:, :, :], w_pool.rearrange("a g c d -> c (a g) d")).then_inc(loaded, 16)
            sp.dma_start(inv[:, :, :], m.inv_in).then_inc(loaded, 16)
            sp.wait_ge(taken, 2)
            sp.dma_start(new_pool_prompt.rearrange("a n r c -> (a n r) c"), ztok[:, :]).then_inc(stored, 16)
            sp.dma_start(new_pool_sample.rearrange("a n r c -> (a n r) c"), zstok[:, :]).then_inc(stored, 16)
            sp.wait_ge(stored, 32)

        @block.tensor
        def _(pe):
            for k in range(NPOOL):
                pe.transpose(m.ps[0:HIST, 0, k * P:(k + 1) * P], z[:, k, PAD + SEQ - HIST:PAD + SEQ], m.ident[:, :])
                pe.transpose(m.ps[0:NS, 1, k * P:(k + 1) * P], z[:, k, PAD + SEQ:PAD + T], m.ident[:, :])
            pe.wait_ge(loaded, 48)
            for k in range(NPOOL):
                last = pe.transpose(m.ps[:, 2, k * NS * HIST:(k + 1) * NS * HIST], hist[:, k * P:(k + 1) * P],
                                    m.ident[0:NS * HIST, 0:NS * HIST])
            last.then_inc(turned, 1)
            for k in range(NPOOL):
                pe.wait_ge(ready, k + 1)
                for c in range(NCH):
                    n = k * NCH + c
                    if n >= 5:
                        pe.wait_ge(split, n - 4)
                    pe.matmul(m.ps[:, 3 + n % 5, width(c)], w[:, k, :], z[:, k, PAD + CHUNKS[c][0]:PAD + CHUNKS[c][0] + CHUNKS[c][1]], start=True,
                              stop=True).then_inc(mapped, 1)

        @block.scalar
        def _(act):
            for n in range(NPOOL * NCH):
                k, c = divmod(n, NCH)
                act.wait_ge(mapped, n + 1)
                act.activation(bh[:, k, chunk(c)], m.ps[:, 3 + n % 5, width(c)], ACT.Copy,
                               scale=m.gain[:, GAIN_ROWS + k:GAIN_ROWS + k + 1]).then_inc(high, 1)

        @block.vector
        def _(dve):
            order = Count(dve, own)
            order.then_wait(dve.memset(sums[:, :, 0:PAD], 0.0))
            dve.wait_ge(turned, 1)
            dve.tensor_copy(ztok[:, :], m.ps[0:HIST, 0, :]).then_inc(taken, 1)
            dve.tensor_copy(zstok[:, :], m.ps[0:NS, 1, :]).then_inc(taken, 1)
            dve.wait_ge(loaded, 48)
            for k, window in enumerate(POOL_WINDOWS):
                past_rows = m.ps[:, 2, k * NS * HIST:(k + 1) * NS * HIST].rearrange("p (n r) -> p n r", n=NS)
                dve.tensor_reduce(past[:, k, :], past_rows[:, :, HIST + 1 - window:HIST], AX_X, ALU.add).then_inc(own, 1)
                order.n += 1
                src = z[:, k, :]
                for j in range(k + 1):
                    dst = sums[:, j % 2, :]
                    order.then_wait(dve.tensor_tensor(dst[:, PAD:PAD + SEQ], src[:, PAD:PAD + SEQ],
                                                      src[:, PAD - 2 ** j:PAD + SEQ - 2 ** j], ALU.add))
                    src = dst
                zk = z[:, k, PAD:PAD + SEQ]
                dve.scalar_tensor_tensor(zk[:, PAD:SEQ], src[:, 2 * PAD:PAD + SEQ], 1.0 / window,
                                         zk[:, PAD:SEQ], ALU.mult, ALU.subtract)
                order.then_wait(dve.tensor_tensor(first[:, :], src[:, PAD:2 * PAD], inv[:, k, :], ALU.mult))
                order.then_wait(dve.tensor_tensor(zk[:, 0:PAD], first[:, :], zk[:, 0:PAD], ALU.subtract))
                zs = z[:, k, PAD + SEQ:PAD + T]
                order.then_wait(dve.tensor_tensor(past[:, k, :], past[:, k, :], zs, ALU.add))
                dve.scalar_tensor_tensor(zs, past[:, k, :], 1.0 / window, zs, ALU.mult,
                                         ALU.subtract).then_inc(ready, 1)
                dve.wait_ge(ready, k + 1)
            for n in range(NPOOL * NCH):
                k, c = divmod(n, NCH)
                dve.wait_ge(high, n + 1)
                dve.scalar_tensor_tensor(bl[:, k, chunk(c)], m.ps[:, 3 + n % 5, width(c)],
                                         m.gain[:, GAIN_ROWS + k:GAIN_ROWS + k + 1], bh[:, k, chunk(c)].bitcast(F32),
                                         ALU.mult, ALU.subtract).then_inc(split, 1)


def memory_attention(nc, m, w_in, mem_prompt, w_mem_kv, new_mem_kv, ch, cl):
    MT = MEM // P
    scale = P ** -0.5
    with Stage(nc, "mem") as st:
        kv = st.sbuf("kv", [P, MT, 2 * MEM_W])
        kt = st.sbuf("kt", [P, MH, MEM])
        with Stage(nc, "memkv") as kt_st:
            tok = kt_st.sbuf("tok", [P, MT, D])
            w = kt_st.sbuf("w", [P, KD, D // 2])
            turned_m = kt_st.sbuf("turned", [P, KD, MEM])
            stat = kt_st.sbuf("stat", [P, MT])
            tok_in = kt_st.sem("tok_in")
            w_arrived = kt_st.sem("w_arrived")
            squared = kt_st.sem("squared")
            own = kt_st.sem("own")
            rooted = kt_st.sem("rooted")
            normed = kt_st.sem("normed")
            turned = kt_st.sem("turned_sem")
            gained = kt_st.sem("gained")
            done = kt_st.sem("done")
            taken = kt_st.sem("taken")
            kt_done = kt_st.sem("kt_done")
            stored = kt_st.sem("stored")
            block = kt_st.block()
            out = new_mem_kv.rearrange("a n (t p) c h e -> p (a n t) (c h e)", p=P)
            w_v = w_mem_kv.rearrange("a (k p) f -> p (a k) f", p=P)

            @block.sync
            def _(sp):
                sp.dma_start(tok[:, :, :], mem_prompt.rearrange("a (t p) d -> p (a t) d", p=P)).then_inc(tok_in, 16)
                sp.dma_start(w[:, :, :], w_v[:, :, 0:D // 2]).then_inc(w_arrived, 16)
                sp.wait_ge(done, MT)
                sp.dma_start(w[:, :, :], w_v[:, :, D // 2:D]).then_inc(w_arrived, 16)
                sp.wait_ge(taken, 2 * MT)
                sp.dma_start(out, kv[:, :, :]).then_inc(stored, 16)
                sp.wait_ge(stored, 16)

            @block.scalar
            def _(act):
                act.wait_ge(tok_in, 16)
                for t in range(MT):
                    if t:
                        act.wait_ge(squared, t)
                    act.activation(m.ps[:, 6:8, :].rearrange("p a f -> p (a f)"), tok[:, t, :], ACT.Square, accum_out=stat[:, t:t + 1]).then_inc(squared, 1)
                act.wait_ge(own, 1)
                act.activation(stat[:, :], stat[:, :], ACT.Sqrt).then_inc(rooted, 1)
                for k in range(KD):
                    act.wait_ge(turned, k // 2 + 1)
                    act.activation(turned_m[:, k, :], m.ps[:, k // 2, (k % 2) * MEM:(k % 2 + 1) * MEM], ACT.Copy,
                                   scale=m.gain[:, G_MEM * KD + k:G_MEM * KD + k + 1]).then_inc(gained, 1)
                for h in range(MH):
                    act.wait_ge(kt_done, 1)
                    act.activation(kt[:, h, :], m.ps[:, h // 2, (h % 2) * MEM:(h % 2 + 1) * MEM], ACT.Copy)

            @block.vector
            def _(dve):
                order = Count(dve, own)
                dve.wait_ge(squared, MT)
                order.then_wait(dve.tensor_scalar(stat[:, :], stat[:, :], 1.0 / D, EPS, ALU.mult, ALU.add))
                dve.wait_ge(rooted, 1)
                order.then_wait(dve.reciprocal(stat[:, :], stat[:, :]))
                for t in range(MT):
                    dve.tensor_scalar(tok[:, t, :], tok[:, t, :], stat[:, t:t + 1], None, ALU.mult).then_inc(normed, 1)
                for n in range(2 * MT):
                    half, t = divmod(n, MT)
                    dve.wait_ge(done, n + 1)
                    dve.tensor_copy(kv[:, t, half * 512:(half + 1) * 512], m.ps[:, 4 + n, :]).then_inc(taken, 1)

            @block.tensor
            def _(pe):
                pe.wait_ge(normed, MT)
                for k in range(KD):
                    for t in range(MT):
                        last = pe.transpose(m.ps[:, k // 2, (k % 2) * MEM + t * P:(k % 2) * MEM + (t + 1) * P],
                                            tok[:, t, k * P:(k + 1) * P], m.ident[:, :])
                    if k % 2:
                        last.then_inc(turned, 1)
                pe.wait_ge(gained, KD)
                for half in range(2):
                    pe.wait_ge(w_arrived, 16 * (half + 1))
                    for t in range(MT):
                        for k in range(KD):
                            last = pe.matmul(m.ps[:, 4 + half * MT + t, :], turned_m[:, k, t * P:(t + 1) * P], w[:, k, :],
                                             start=k == 0, stop=k == KD - 1)
                        last.then_inc(done, 1)
                pe.wait_ge(taken, MT)
                for h in range(MH):
                    for t in range(MT):
                        last = pe.transpose(m.ps[:, h // 2, (h % 2) * MEM + t * P:(h % 2) * MEM + (t + 1) * P],
                                            kv[:, t, h * P:(h + 1) * P], m.ident[:, :])
                last.then_inc(kt_done, 1)

        q = st.sbuf("q", [P, MH, T])
        with Stage(nc, "qm") as pt:
            proj = Product(pt, m, w_in, lambda i: i * (2 * P) + QM_COL, MH // 2, "w")
            block = pt.block()

            def take(act):
                def one(eng, i, t, c, src):
                    return copy(eng, act, q[:, bass.ds(i * 2 + t, 1), chunk(c)].rearrange("p a t -> p (a t)"), src)
                return one

            @block.sync
            def _(sp):
                proj.load(sp)

            @block.tensor
            def _(pe):
                proj.tensor(pe)

            @block.scalar
            def _(act):
                proj.scalar_first(act)
                proj.scalar(act, take(True))

            @block.vector
            def _(dve):
                proj.vector_first(dve)
                proj.vector(dve, take(False))

        prob = st.sbuf("prob", [P, 2, MH, MEM])
        turned_p = st.sbuf("turned_p", [P, 2, MT, MH, P])
        stat = st.sbuf("stat", [P, 2, 4, MH])
        scored = st.sem("scored")
        own = st.sem("own")
        negated = st.sem("negated")
        exped = st.sem("exped")
        normal = st.sem("normal")
        p_turned = st.sem("p_turned")
        p_taken_act = st.sem("p_taken_act")
        p_taken_dve = st.sem("p_taken_dve")
        weighed = st.sem("weighed")
        high = st.sem("high")
        split = st.sem("split")
        sampled = st.sem("sampled")
        block = st.block()

        @block.tensor
        def _(pe):
            def scores(b):
                if b >= 2:
                    pe.wait_ge(exped, MH * (b - 1))
                for h in range(MH):
                    last = pe.matmul(m.ps[:, 2 * (b % 2) + h // 2, (h % 2) * MEM:(h % 2 + 1) * MEM],
                                     q[:, h, b * P:(b + 1) * P], kt[:, h, :], start=True, stop=True)
                last.then_inc(scored, 1)

            def turn(b):
                pe.wait_ge(normal, b + 1)
                if b >= 1:
                    pe.wait_ge(p_taken_act, b)
                    pe.wait_ge(p_taken_dve, b)
                for t in range(MT):
                    for h in range(MH):
                        last = pe.transpose(m.ps[:, 4 + t, h * P:(h + 1) * P], prob[:, b % 2, h, t * P:(t + 1) * P],
                                            m.ident[:, :])
                last.then_inc(p_turned, 1)

            def weigh(b):
                pe.wait_ge(p_taken_act, b + 1)
                pe.wait_ge(p_taken_dve, b + 1)
                if b >= 2:
                    pe.wait_ge(split, b - 1)
                for h in range(MH):
                    for t in range(MT):
                        last = pe.matmul(m.ps[:, 6 + b % 2, h * P:(h + 1) * P], kv[:, t, MEM_W + h * P:MEM_W + (h + 1) * P],
                                         turned_p[:, b % 2, t, h, :], start=t == 0, stop=t == MT - 1)
                last.then_inc(weighed, 1)

            scores(0)
            scores(1)
            for b in range(TB):
                turn(b)
                if b + 2 < TB:
                    scores(b + 2)
                weigh(b)

        @block.scalar
        def _(act):
            act.activation(m.s_qm[:, :, :], q[:, :, SEQ:T], ACT.Copy).then_inc(sampled, 1)

            def exps(b):
                act.wait_ge(negated, b + 1)
                if b >= 2:
                    act.wait_ge(p_turned, b - 1)
                for h in range(MH):
                    act.activation(prob[:, b % 2, h, :], m.ps[:, 2 * (b % 2) + h // 2, (h % 2) * MEM:(h % 2 + 1) * MEM],
                                   ACT.Exp, bias=stat[:, b % 2, 1, h:h + 1], scale=scale,
                                   accum_out=stat[:, b % 2, 2, h:h + 1]).then_inc(exped, 1)

            def result(b):
                act.wait_ge(weighed, b + 1)
                act.activation(ch[:, :, b * P:(b + 1) * P], m.ps[:, 6 + b % 2, :].rearrange("p (h q) -> p h q", h=MH),
                               ACT.Copy).then_inc(high, 1)

            exps(0)
            for b in range(TB):
                if b + 1 < TB:
                    exps(b + 1)
                act.wait_ge(p_turned, b + 1)
                if b >= 2:
                    act.wait_ge(weighed, b - 1)
                act.activation(turned_p[:, b % 2, 1, :, :], m.ps[:, 5, :].rearrange("p (h q) -> p h q", h=MH),
                               ACT.Copy).then_inc(p_taken_act, 1)
                if b >= 1:
                    result(b - 1)
            result(TB - 1)

        @block.vector
        def _(dve):
            order = Count(dve, own)

            def top(b):
                dve.wait_ge(scored, b + 1)
                if b >= 2:
                    dve.wait_ge(normal, b - 1)
                src = m.ps[:, 2 * (b % 2):2 * (b % 2) + 2, :].rearrange("p a (i k) -> p (a i) k", k=MEM)
                order.then_wait(dve.tensor_reduce(stat[:, b % 2, 0, :], src, AX_X, ALU.max))
                dve.tensor_scalar(stat[:, b % 2, 1, :], stat[:, b % 2, 0, :], -scale, None, ALU.mult).then_inc(negated, 1)

            def normalise(b):
                dve.wait_ge(exped, MH * (b + 1))
                order.then_wait(dve.reciprocal(stat[:, b % 2, 3, :], stat[:, b % 2, 2, :]))
                dve.tensor_tensor(prob[:, b % 2, :, :], prob[:, b % 2, :, :],
                                  stat[:, b % 2, 3, :].unsqueeze(2).to_broadcast([P, MH, MEM]), ALU.mult).then_inc(normal, 1)

            def result(b):
                dve.wait_ge(high, b + 1)
                dve.tensor_tensor(cl[:, :, b * P:(b + 1) * P], m.ps[:, 6 + b % 2, :].rearrange("p (h q) -> p h q", h=MH),
                                  ch[:, :, b * P:(b + 1) * P].bitcast(F32), ALU.subtract).then_inc(split, 1)

            top(0)
            for b in range(TB):
                normalise(b)
                if b + 1 < TB:
                    top(b + 1)
                dve.wait_ge(p_turned, b + 1)
                if b >= 2:
                    dve.wait_ge(weighed, b - 1)
                dve.tensor_copy(turned_p[:, b % 2, 0, :, :], m.ps[:, 4, :].rearrange("p (h q) -> p h q", h=MH)
                                ).then_inc(p_taken_dve, 1)
                if b >= 1:
                    result(b - 1)
            result(TB - 1)


def sample_memory(nc, m, cache, ch, cl):
    MT = MEM // P
    rows = NS * MH
    scale = P ** -0.5
    with Stage(nc, "smem") as st:
        keys = st.sbuf("keys", [P, 2, MT, MEM_W])
        vals = st.sbuf("vals", [P, 4, MT, MEM_W])
        tok = st.sbuf("tok", [NS, MEM_W])
        sel = st.sbuf("sel", [NS, NS, P])
        prod = st.sbuf("prod", [P, MT, MEM_W])
        score = st.sbuf("score", [P, MT, NS, MH])
        prob = st.sbuf("prob", [rows, MT, P])
        small = st.sbuf("small", [rows, 4])
        p_cols = st.sbuf("p_cols", [P, MT, rows])
        sel_in = st.sem("sel_in")
        key_in = [st.sem(f"key_in{i}") for i in range(2)]
        val_in = [st.sem(f"val_in{i}") for i in range(4)]
        tok_done = st.sem("tok_done")
        tok_taken = st.sem("tok_taken")
        spread = st.sem("spread")
        multiplied = st.sem("multiplied")
        scored = st.sem("scored")
        rowed = st.sem("rowed")
        own = st.sem("own")
        maxed = st.sem("maxed")
        exped = st.sem("exped")
        normal = st.sem("normal")
        coled = st.sem("coled")
        cols_taken = st.sem("cols_taken")
        weighed = st.sem("weighed")
        high = st.sem("high")
        block = st.block()
        c_v = cache.rearrange("a n (t p) c h e -> p (a n) t c (h e)", p=P)

        @block.sync
        def _(sp):
            sp.dma_start(sel[:, :, :], m.sel_in).then_inc(sel_in, 16)
            for n in range(NS):
                if n >= 2:
                    sp.wait_ge(multiplied, n - 1)
                sp.dma_start(keys[:, n % 2, :, :], c_v[:, n, :, 0, :]).then_inc(key_in[n % 2], 16)
                if n < 4:
                    sp.dma_start(vals[:, n, :, :], c_v[:, n, :, 1, :]).then_inc(val_in[n], 16)
            for n in range(4, NS):
                sp.wait_ge(weighed, n - 3)
                sp.dma_start(vals[:, n % 4, :, :], c_v[:, n, :, 1, :]).then_inc(val_in[n % 4], 16)

        @block.tensor
        def _(pe):
            for h in range(MH):
                last = pe.transpose(m.ps[0:NS, 0, h * P:(h + 1) * P], m.s_qm[:, h, :], m.ident[:, :])
            last.then_inc(tok_done, 1)
            pe.wait_ge(tok_taken, 1)
            pe.wait_ge(sel_in, 16)
            for n in range(NS):
                if n >= 2:
                    pe.wait_ge(multiplied, n - 1)
                pe.matmul(m.ps[:, 1 + n % 2, :], sel[:, n, :], tok[:, :], start=True, stop=True).then_inc(spread, 1)
            pe.wait_ge(scored, NS)
            for t in range(MT):
                last = pe.transpose(m.ps[0:rows, 3, t * P:(t + 1) * P], score[:, t, :, :].rearrange("p n h -> p (n h)"),
                                    m.ident[:, :])
            last.then_inc(rowed, 1)
            pe.wait_ge(normal, 1)
            for t in range(MT):
                last = pe.transpose(m.ps[:, 4, t * rows:(t + 1) * rows], prob[:, t, :], m.ident[0:rows, 0:rows])
            last.then_inc(coled, 1)
            pe.wait_ge(cols_taken, 1)
            for n in range(NS):
                pe.wait_ge(val_in[n % 4], 16 * (n // 4 + 1))
                for h in range(MH):
                    col = n * MH + h
                    for t in range(MT):
                        last = pe.matmul(m.ps[:, 5, col:col + 1], vals[:, n % 4, t, h * P:(h + 1) * P],
                                         p_cols[:, t, col:col + 1], start=t == 0, stop=t == MT - 1)
                last.then_inc(weighed, 1)

        @block.vector
        def _(dve):
            order = Count(dve, own)
            dve.wait_ge(tok_done, 1)
            dve.tensor_copy(tok[:, :], m.ps[0:NS, 0, :]).then_inc(tok_taken, 1)
            for n in range(NS):
                dve.wait_ge(spread, n + 1)
                dve.wait_ge(key_in[n % 2], 16 * (n // 2 + 1))
                if n:
                    dve.wait_ge(scored, n)
                dve.tensor_tensor(prod[:, :, :], keys[:, n % 2, :, :],
                                  m.ps[:, 1 + n % 2, :].unsqueeze(1).to_broadcast([P, MT, MEM_W]),
                                  ALU.mult).then_inc(multiplied, 1)
                dve.wait_ge(multiplied, n + 1)
                dve.tensor_reduce(score[:, :, n, :], prod[:, :, :].rearrange("p t (h d) -> p t h d", h=MH), AX_X,
                                  ALU.add).then_inc(scored, 1)
            dve.wait_ge(rowed, 1)
            flat = prob[:, :, :].rearrange("p t r -> p (t r)")
            order.then_wait(dve.tensor_copy(flat, m.ps[0:rows, 3, 0:MEM]))
            order.then_wait(dve.tensor_reduce(small[:, 0:1], flat, AX_X, ALU.max))
            dve.tensor_scalar(small[:, 1:2], small[:, 0:1], -scale, None, ALU.mult).then_inc(maxed, 1)
            dve.wait_ge(exped, 1)
            order.then_wait(dve.reciprocal(small[:, 3:4], small[:, 2:3]))
            dve.tensor_scalar(flat, flat, small[:, 3:4], None, ALU.mult).then_inc(normal, 1)
            dve.wait_ge(coled, 1)
            dve.tensor_copy(p_cols[:, :, :], m.ps[:, 4, 0:MT * rows].rearrange("p (t r) -> p t r", t=MT)
                            ).then_inc(cols_taken, 1)
            dve.wait_ge(high, 1)
            dve.tensor_tensor(cl[:, :, SEQ:T], m.ps[:, 5, 0:rows].rearrange("p (n h) -> p h n", h=MH),
                              ch[:, :, SEQ:T].bitcast(F32), ALU.subtract)

        @block.scalar
        def _(act):
            act.wait_ge(maxed, 1)
            flat = prob[:, :, :].rearrange("p t r -> p (t r)")
            act.activation(flat, flat, ACT.Exp, bias=small[:, 1:2], scale=scale, accum_out=small[:, 2:3]).then_inc(exped, 1)
            act.wait_ge(weighed, NS)
            act.activation(ch[:, :, SEQ:T], m.ps[:, 5, 0:rows].rearrange("p (n h) -> p h n", h=MH),
                           ACT.Copy).then_inc(high, 1)


class Memory:
    pass


def decoder_step(nc, i, o):
    SEMS.clear()
    m = Memory()
    with ExitStack() as ctx:
        def sb(name, shape, dt=F32):
            return ctx.enter_context(nc.sbuf_tensor(name, shape, dt))

        m.x = sb("x", [P, KD, T])
        m.uh = sb("uh", [P, KD, T], F32R)
        m.ul = sb("ul", [P, KD, T], F32R)
        m.ident = sb("ident", [P, P])
        m.mean = sb("mean", [P, P])
        m.gain = sb("gain", [P, GAIN_ROWS + NPOOL])
        m.cache_bias = sb("cache_bias", [P, NG, HG])
        m.new_bias = sb("new_bias", [NS, NG * HG])
        m.s_qkv = sb("s_qkv", [P, 6 * NG, NS])
        m.s_att = sb("s_att", [P, 2, NS])
        m.s_qm = sb("s_qm", [P, MH, NS])
        m.ps = ctx.enter_context(nc.psum_tensor("ps", [P, 8, 512], F32))
        m.bias_rows = nc.dram_tensor("bias_rows", (NG, NG * HG, 384), F32).ap()
        m.group_out = nc.dram_tensor("group_out", (SEQ, NG, RES), F32).ap()
        m.new_scores = nc.dram_tensor("new_scores", (NS, HG, NG), F32).ap()
        m.sel_in, m.own_in, m.inv_in = i["const_sel"], i["const_own"], i["const_inv"]

        gains = [i[n] for n in ("g_ffn1", "g_mix", "g_mem", "g_ffn2", "g_final")]
        w_in = i["w_in"].rearrange("a (k p) f -> p (a k) f", p=P)
        w_out = i["w_out"].rearrange("a (k p) f -> p (a k) f", p=P)
        w_o = [i[n].rearrange("a (k p) f -> p (a k) f", p=P) for n in ("w_oa", "w_ob", "w_oc")]

        load_tokens(nc, m, i["x_prompt"], i["x_sample"], gains, i["pool_scale"], i["const_ident"])
        bias_tables(nc, m, i["rel_bias"], i["const_onehot"])
        ffn(nc, m, "ffn1", G_FFN1, i["w1_gate"], i["w1_up"], i["w1_down"])
        for g in range(NG):
            attention(nc, m, g, w_in, o[f"new_win{g}_kv_prompt"], g == 0)
        sample_attention(nc, m, [i[f"cache_win{g}_kv"] for g in range(NG)],
                         [o[f"new_win{g}_kv_sample"] for g in range(NG)])
        clear_semaphores(nc)
        with ExitStack() as mix:
            with Stage(nc, "c") as c:
                ch, cl = (c.sbuf(n, [P, MH, T], F32R) for n in ("high", "low"))
                memory_attention(nc, m, w_in, i["mem_prompt"], i["w_mem_kv"], o["new_mem_kv_prompt"], ch, cl)
                sample_memory(nc, m, i["cache_mem_kv"], ch, cl)
                m.mix = mix.enter_context(nc.sbuf_tensor("mix", [P, KD, T], F32, side="right"))
                merge(nc, m, "merge_c", 2, True, w_in, w_o[2], ch, cl, MH)
            with Stage(nc, "a") as a:
                ah, al = (a.sbuf(n, [P, 2, T], F32R) for n in ("high", "low"))
                combine(nc, m, ah, al)
                merge(nc, m, "merge_a", 0, False, w_in, w_o[0], ah, al, 2)
            with Stage(nc, "b") as b:
                bh, bl = (b.sbuf(n, [P, NPOOL, T], F32R) for n in ("high", "low"))
                pooling(nc, m, w_in, i["state_pool"], i["w_pool"], o["new_pool_prompt"], o["new_pool_sample"], bh, bl)
                merge(nc, m, "merge_b", 1, False, w_in, w_o[1], bh, bl, NPOOL)
            mix_out(nc, m, w_out)
        clear_semaphores(nc)
        ffn(nc, m, "ffn2", G_FFN2, i["w2_gate"], i["w2_up"], i["w2_down"])
        final(nc, m, o["y_prompt"], o["y_sample"])



N_BUCKETS = 32
MAX_DISTANCE = 2048


def rel_bucket(n):
    exact = N_BUCKETS // 2
    if n < exact:
        return n
    return min(exact + int(np.log(n / exact) / np.log(MAX_DISTANCE / exact) * (N_BUCKETS - exact)), N_BUCKETS - 1)


def constants():
    onehot = np.zeros((N_BUCKETS, 2, NG, REACH + 1), np.float32)
    for g, (_, dil) in enumerate(GROUPS):
        for r in range(REACH + 1):
            onehot[rel_bucket((REACH - r) * dil), 0, g, r] = 1.0
            onehot[rel_bucket(r * dil), 1, g, r] = 1.0
    sel = np.zeros((NS, NS, P), np.float32)
    own = np.zeros((NS * HG, NS), np.float32)
    for n in range(NS):
        sel[n, n, :] = 1.0
        own[n * HG:(n + 1) * HG, n] = 1.0
    inv = np.zeros((P, NPOOL, PAD), np.float32)
    for k, window in enumerate(POOL_WINDOWS):
        inv[:, k, :] = 1.0 / np.minimum(window, np.arange(PAD) + 1)
    return {"const_ident": np.eye(P, dtype=np.float32), "const_onehot": onehot, "const_sel": sel, "const_own": own,
            "const_inv": inv}



_OUTS = [("y_prompt", (1, SEQ, D)), ("y_sample", (NS, 1, D)), ("new_win0_kv_prompt", (1, 1, 128, 2, HG, DH)),
         ("new_win1_kv_prompt", (1, 1, 512, 2, HG, DH)), ("new_win2_kv_prompt", (1, 1, SEQ, 2, HG, DH)),
         ("new_pool_prompt", (1, 1, HIST, POOL_W)), ("new_mem_kv_prompt", (1, 1, MEM, 2, MH, P)),
         ("new_win0_kv_sample", (1, NS, 1, 2, HG, DH)), ("new_win1_kv_sample", (1, NS, 1, 2, HG, DH)),
         ("new_win2_kv_sample", (1, NS, 1, 2, HG, DH)), ("new_pool_sample", (1, NS, 1, POOL_W))]


def kernel(**inputs):
    import concourse.bacc as bacc
    from concourse.bass_utils import run_bass_kernel_spmd as run

    nc = bacc.Bacc("TRN2", target_bir_lowering=False, num_devices=1)
    arrays = {name: np.ascontiguousarray(a) for name, a in inputs.items()} | constants()
    i = {name: nc.dram_tensor(f"in_{name}", a.shape, mybir.dt.from_np(a.dtype), kind="ExternalInput").ap()
         for name, a in arrays.items()}
    o = {name: nc.dram_tensor(f"out_{name}", shape, F32, kind="ExternalOutput").ap() for name, shape in _OUTS}
    decoder_step(nc, i, o)
    r = run(nc, [{f"in_{name}": a for name, a in arrays.items()}], core_ids=[0])
    return tuple(r.results[0][f"out_{name}"] for name, _ in _OUTS)
```

```python
from contextlib import ExitStack

import numpy as np

import concourse.bass as bass
from concourse import mybir

F32 = mybir.dt.float32
F32R = mybir.dt.float32r
ALU = mybir.AluOpType
ACT = mybir.ActivationFunctionType
AX_X = mybir.AxisListType.X

P = 128
D = 1024
SEQ = 1024
NS = 8
T = SEQ + NS
KD = D // P
CHUNKS = ((0, 352), (352, 352), (704, 328))
NCH = len(CHUNKS)
CH = CHUNKS[0][1]
TB = SEQ // P
F = 2816
EPS = 1e-6
G_FFN1, G_MIX, G_MEM, G_FFN2, G_FINAL = range(5)
GAIN_ROWS = 5 * KD
NPOOL = 4


class Count:

    def __init__(self, eng, sem, base=0):
        self.eng, self.sem, self.base, self.n = eng, sem, base, 0

    def then_wait(self, ins):
        self.n += 1
        ins.then_inc(self.sem, 1)
        self.eng.wait_ge(self.sem, self.base + self.n)


SEMS = []


def clear_semaphores(nc):
    nc.clear_and_free_semaphores(SEMS)
    SEMS.clear()
    nc.all_engine_barrier()


class Stage:

    def __init__(self, nc, name):
        self.nc, self.name, self.ctx = nc, name, ExitStack()

    def __enter__(self):
        return self

    def __exit__(self, *e):
        return self.ctx.__exit__(*e)

    def sbuf(self, name, shape, dt=F32):
        return self.ctx.enter_context(self.nc.sbuf_tensor(f"{self.name}_{name}", shape, dt))

    def sem(self, name):
        sem = self.nc.alloc_semaphore(f"{self.name}_{name}")
        SEMS.append(sem)
        return sem

    def block(self):
        return self.ctx.enter_context(self.nc.Block())


def chunk(c):
    return slice(CHUNKS[c][0], CHUNKS[c][0] + CHUNKS[c][1])


def width(c):
    return slice(0, CHUNKS[c][1])


class Stream:

    def __init__(self, nc, ctx):
        self.raw = ctx.enter_context(nc.sbuf_tensor("stream_raw", [P, KD, 2 * P], F32))
        self.high, self.low = ([ctx.enter_context(nc.sbuf_tensor(f"stream_{part}{t}", [P, KD, P], F32R))
                                for t in range(2)] for part in ("high", "low"))
        self.arrived = nc.alloc_semaphore("stream_arrived")
        self.rounded = nc.alloc_semaphore("stream_rounded")
        self.split = nc.alloc_semaphore("stream_split")
        self.base = 0

    def load(self, sp, n, w, col, i=None):
        if not isinstance(n, int) or n > 0:
            sp.wait_ge(self.split, 2 * n)
        first = col if i is None else col(i)
        sp.dma_start(self.raw[:, :, :], w[:, :, bass.ds(first, 2 * P)]).then_inc(self.arrived, 16)

    def load_all(self, sp, pairs, w, cols, then):
        with sp.Fori(1, pairs) as i:
            self.load(sp, self.base + i, w, cols, i)
        if then is not None:
            self.load(sp, self.base + pairs, *then)

    def split_high(self, act, n, t):
        act.wait_ge(self.arrived, 16 * (n + 1))
        act.activation(self.high[t][:, :, :], self.raw[:, :, t * P:(t + 1) * P], ACT.Copy).then_inc(self.rounded, 1)

    def split_low(self, dve, n, t):
        dve.wait_ge(self.rounded, n * 2 + (t + 1))
        dve.tensor_tensor(self.low[t][:, :, :], self.raw[:, :, t * P:(t + 1) * P], self.high[t][:, :, :].bitcast(F32),
                          ALU.subtract).then_inc(self.split, 1)


class Parts:

    def __init__(self, st, m, which):
        self.m, self.which = m, which
        self.high = st.sem("part_high")

    def gain(self, k):
        return self.m.gain[:, self.which * KD + k:self.which * KD + k + 1]

    def scalar_high(self, act, k, c):
        act.activation(self.m.uh[:, k, chunk(c)], self.m.x[:, k, chunk(c)], ACT.Copy,
                       scale=self.gain(k)).then_inc(self.high, 1)

    def vector_low(self, dve, count, k, c):
        dve.wait_ge(self.high, count)
        dve.scalar_tensor_tensor(self.m.ul[:, k, chunk(c)], self.m.x[:, k, chunk(c)], self.gain(k),
                                 self.m.uh[:, k, chunk(c)].bitcast(F32), ALU.mult, ALU.subtract)


def load_tokens(nc, m, i, gains, first):
    with Stage(nc, "load") as st:
        tok = st.sbuf("tok", [P, TB + 1, D])
        junk = st.sbuf("junk", [P, 2, D])
        stat = st.sbuf("stat", [P, 3, TB + 1])
        diag = st.sbuf("diag", [P, 2, P])
        grow = st.sbuf("grow", [GAIN_ROWS + NPOOL, P])
        rel = st.sbuf("rel", [32, NG * HG])
        hot = st.sbuf("hot", [32, 2, NG, REACH + 1])
        rows = st.sbuf("table", [NG * HG, NG, 384])
        parts = Parts(st, m, G_FFN1)
        tok_in = [st.sem(f"tok_in{b}") for b in range(TB + 1)]
        small_in = st.sem("small_in")
        hot_in = st.sem("hot_in")
        small_turned = st.sem("small_turned")
        small_taken = st.sem("small_taken")
        turned = st.sem("turned")
        taken = st.sem("taken")
        ones_set = st.sem("ones_set")
        squared = st.sem("squared")
        shifted = st.sem("shifted")
        rooted = st.sem("rooted")
        inverted = st.sem("inverted")
        diag_made = st.sem("diag_made")
        spread = st.sem("spread")
        bias_made = st.sem("bias_made")
        bias_taken = st.sem("bias_taken")
        stored = st.sem("stored")
        block = st.block()
        xp = i["x_prompt"].rearrange("a (b p) d -> p (a b) d", p=P)
        order_b = [TB] + list(range(TB))

        def size(b):
            return P if b < TB else NS

        @block.sync
        def _(sp):
            sp.dma_start(m.ident[:, :], i["const_ident"]).then_inc(small_in, 16)
            for n, g in enumerate(gains):
                src = g.rearrange("a (k p) -> (a k) p", p=P) if len(g.shape) == 2 else g.rearrange("(k p) -> k p", p=P)
                sp.dma_start(grow[n * KD:(n + 1) * KD, :], src).then_inc(small_in, 16)
            sp.dma_start(grow[GAIN_ROWS:, :], i["pool_scale"].rearrange("a (k p) -> (a k) p", p=P)).then_inc(small_in, 16)
            sp.dma_start(tok[0:NS, TB, :], i["x_sample"].rearrange("n a d -> (n a) d")).then_inc(tok_in[TB], 16)
            for b in range(TB):
                sp.dma_start(tok[:, b, :], xp[:, b, :]).then_inc(tok_in[b], 16)
            sp.dma_start(rel[:, :], i["rel_bias"]).then_inc(hot_in, 16)
            sp.dma_start(hot[:, :, :, :], i["const_onehot"]).then_inc(hot_in, 16)
            m.stream.load(sp, 0, *first)
            sp.wait_ge(bias_taken, 1)
            sp.dma_start(m.bias_rows.rearrange("g h y -> h g y"), rows[:, :, :]).then_inc(stored, 16)
            sp.wait_ge(stored, 16)

        @block.tensor
        def _(pe):
            def spread_rstd(s):
                b = order_b[s]
                pe.wait_ge(diag_made, s + 1)
                bank, at = (5 + b // 4, b % 4 * P) if b < TB else (0, 128)
                pe.matmul(m.ps[:, bank, at:at + size(b)], m.mean[0:size(b), :], diag[0:size(b), s % 2, 0:size(b)],
                          start=True, stop=True).then_inc(spread, 1)

            pe.wait_ge(small_in, 16 * (len(gains) + 2))
            pe.transpose(m.ps[:, 0, 0:GAIN_ROWS + NPOOL], grow[:, :], m.ident[0:GAIN_ROWS + NPOOL, 0:GAIN_ROWS + NPOOL])
            pe.wait_ge(tok_in[TB], 16)
            for k in range(KD):
                last = pe.transpose(m.ps[:, 0, 64 + NS * k:64 + NS * (k + 1)], tok[0:NS, TB, k * P:(k + 1) * P],
                                    m.ident[0:NS, 0:NS])
            last.then_inc(small_turned, 1)
            pe.wait_ge(ones_set, 1)
            for n in range(2 * TB):
                b, half = divmod(n, 2)
                if half == 0:
                    pe.wait_ge(tok_in[b], 16)
                if n >= 4:
                    pe.wait_ge(taken, n - 3)
                for k in range(4):
                    kk = 4 * half + k
                    last = pe.transpose(m.ps[:, 1 + n % 4, k * P:(k + 1) * P], tok[:, b, kk * P:(kk + 1) * P],
                                        m.ident[:, :])
                last.then_inc(turned, 1)
                if half == 1:
                    spread_rstd(b)
            pe.wait_ge(hot_in, 32)
            pe.matmul(m.ps[0:NG * HG, 7, 0:NG * (REACH + 1)], rel[:, :], hot[:, 1, :, :].rearrange("p g r -> p (g r)"),
                      start=True, stop=True)
            for g in range(NG):
                pe.matmul(m.ps[:, 7, 400 + 16 * g:400 + 16 * g + NG * HG], hot[:, 0, g, 0:REACH], rel[:, :], start=True,
                          stop=True)
            pe.matmul(m.ps[0:NS, 7, 448:448 + NG * HG], hot[:, 0, 0, REACH:REACH + 1].to_broadcast([32, NS]), rel[:, :],
                      start=True, stop=True).then_inc(bias_made, 1)
            spread_rstd(TB)

        @block.scalar
        def _(act):
            def square(s):
                b = order_b[s]
                act.wait_ge(tok_in[b], 16)
                if s >= 2:
                    act.wait_ge(squared, s - 1)
                act.activation(junk[0:size(b), s % 2, :], tok[0:size(b), b, :], ACT.Square,
                               accum_out=stat[0:size(b), 0, b:b + 1]).then_inc(squared, 1)

            def root(s):
                b = order_b[s]
                act.wait_ge(shifted, s + 1)
                act.activation(stat[0:size(b), 1, b:b + 1], stat[0:size(b), 1, b:b + 1], ACT.Sqrt).then_inc(rooted, 1)

            def high(c, blocks):
                act.wait_ge(taken, 2 * blocks)
                for k in range(KD):
                    parts.scalar_high(act, k, c)

            square(0)
            for b in range(TB):
                square(b + 1)
                root(b)
                if b == 3:
                    act.wait_ge(small_taken, 2)
                    high(0, 3)
                if b == 6:
                    high(1, 6)
                    act.wait_ge(spread, 5)
                    act.activation(m.rstd[:, 0:512], m.ps[:, 5, :], ACT.Copy)
            root(TB)
            high(2, TB)
            for t in range(2):
                m.stream.split_high(act, 0, t)
            act.wait_ge(spread, TB + 1)
            act.activation(m.rstd[:, 512:SEQ], m.ps[:, 6, :], ACT.Copy)
            act.activation(m.rstd[:, SEQ:T], m.ps[:, 0, 128:128 + NS], ACT.Copy)

        @block.vector
        def _(dve):
            def shift(s):
                b = order_b[s]
                dve.wait_ge(squared, s + 1)
                dve.tensor_scalar(stat[0:size(b), 1, b:b + 1], stat[0:size(b), 0, b:b + 1], 1.0 / D, EPS, ALU.mult,
                                  ALU.add).then_inc(shifted, 1)

            def diagonal(s):
                b = order_b[s]
                dve.wait_ge(rooted, s + 1)
                dve.reciprocal(stat[0:size(b), 2, b:b + 1], stat[0:size(b), 1, b:b + 1]).then_inc(inverted, 1)
                dve.wait_ge(inverted, s + 1)
                if s >= 2:
                    dve.wait_ge(spread, s - 1)
                dve.tensor_scalar(diag[0:size(b), s % 2, 0:size(b)], m.ident[0:size(b), 0:size(b)],
                                  stat[0:size(b), 2, b:b + 1], float(D), ALU.mult, ALU.mult).then_inc(diag_made, 1)

            def low(c):
                for k in range(KD):
                    parts.vector_low(dve, KD * c + k + 1, k, c)

            dve.memset(m.eps[:, :], EPS)
            dve.memset(m.mean[:, :], 1.0 / D).then_inc(ones_set, 1)
            dve.memset(rows[:, :, :], NEG).then_inc(ones_set, 1)
            dve.wait_ge(small_turned, 1)
            dve.tensor_copy(m.gain[:, :], m.ps[:, 0, 0:GAIN_ROWS + NPOOL]).then_inc(small_taken, 1)
            dve.tensor_copy(m.x[:, :, SEQ:T], m.ps[:, 0, 64:128].rearrange("p (k n) -> p k n", k=KD)).then_inc(small_taken, 1)
            shift(0)
            dve.wait_ge(small_taken, 2)
            for b in range(TB):
                diagonal(b)
                for half in range(2):
                    n = 2 * b + half
                    dve.wait_ge(turned, n + 1)
                    dve.tensor_copy(m.x[:, 4 * half:4 * half + 4, b * P:(b + 1) * P],
                                    m.ps[:, 1 + n % 4, :].rearrange("p (k t) -> p k t", k=4)).then_inc(taken, 1)
                shift(b + 1)
                if b == 4:
                    low(0)
            diagonal(TB)
            low(1)
            low(2)
            for t in range(2):
                m.stream.split_low(dve, 0, t)
            dve.wait_ge(bias_made, 1)
            dve.wait_ge(ones_set, 2)
            dve.tensor_copy(rows[:, :, 127:127 + REACH + 1],
                            m.ps[0:NG * HG, 7, 0:NG * (REACH + 1)].rearrange("h (g r) -> h g r", g=NG)).then_inc(bias_taken, 1)
            for g in range(NG):
                dve.tensor_copy(m.cache_bias[:, g, :], m.ps[:, 7, 400 + 16 * g + HG * g:400 + 16 * g + HG * g + HG])
            dve.tensor_copy(m.new_bias[:, :], m.ps[0:NS, 7, 448:448 + NG * HG])


class Norm:

    def __init__(self, st, m, which, banks):
        self.m, self.banks = m, banks
        self.parts = Parts(st, m, which)
        self.sq = st.sbuf("sq", [P, 2, CH])
        self.ssum = st.sbuf("ssum", [P, T])
        self.squared = st.sem("squared")
        self.summed = st.sem("summed")
        self.meaned = st.sem("meaned")
        self.rooted = st.sem("rooted")
        self.inverted = st.sem("inverted")

    def vector_clear(self, dve):
        dve.memset(self.ssum[:, :], 0.0).then_inc(self.summed, 2)

    def scalar_square(self, act, count, parity, x, c):
        act.wait_ge(self.summed, count + 1)
        act.activation(self.sq[:, parity, width(c)], x, ACT.Square).then_inc(self.squared, 1)

    def vector_sum(self, dve, count, parity, c):
        dve.wait_ge(self.squared, count + 1)
        dve.wait_ge(self.summed, count + 2)
        dve.tensor_tensor(self.ssum[:, chunk(c)], self.ssum[:, chunk(c)], self.sq[:, parity, width(c)],
                          ALU.add).then_inc(self.summed, 1)

    def tensor_mean(self, pe, c, count):
        pe.wait_ge(self.summed, count + 2)
        if self.banks[c] in self.banks[:c]:
            pe.wait_ge(self.rooted, c)
        pe.matmul(self.m.ps[:, self.banks[c], width(c)], self.m.mean[:, :], self.ssum[:, chunk(c)],
                  start=True, stop=True).then_inc(self.meaned, 1)

    def scalar_root(self, act, c):
        act.wait_ge(self.meaned, c + 1)
        act.activation(self.m.rstd[:, chunk(c)], self.m.ps[:, self.banks[c], width(c)], ACT.Sqrt,
                       bias=self.m.eps[:, :]).then_inc(self.rooted, 1)

    def vector_invert(self, dve, c):
        dve.wait_ge(self.rooted, c + 1)
        dve.reciprocal(self.m.rstd[:, chunk(c)], self.m.rstd[:, chunk(c)]).then_inc(self.inverted, 1)


FT = F // P
PAIRS = FT // 2
GU_UNITS = 2 * NCH
DOWN_UNITS = NCH * KD


def product(pe, out, w_high, w_low, a_high, a_low, first, last):
    pe.matmul(out, w_high, a_high, start=first, stop=False)
    pe.matmul(out, w_low, a_high, start=False, stop=False)
    return pe.matmul(out, w_high, a_low, start=False, stop=last)


def ffn(nc, m, name, w_gate, w_up, w_down, next_norm, then):
    with Stage(nc, name) as st:
        raw_up = st.sbuf("raw_up", [P, KD, 2 * P])
        up_h = [st.sbuf(f"up_h{t}", [P, KD, P], F32R) for t in range(2)]
        up_l = [st.sbuf(f"up_l{t}", [P, KD, P], F32R) for t in range(2)]
        raw_d = st.sbuf("raw_d", [P, 2, D])
        d_h = st.sbuf("d_h", [P, 2, D], F32R)
        d_l = st.sbuf("d_l", [P, 2, D], F32R)
        hid_h = st.sbuf("hid_h", [P, 2, T], F32R)
        hid_l = st.sbuf("hid_l", [P, 2, T], F32R)
        silu = st.sbuf("silu", [P, 2, CH])
        up = st.sbuf("up", [P, CH])
        norm = Norm(st, m, next_norm, (0, 2, 1)) if next_norm is not None else None
        up_in = st.sem("up_in")
        d_in = st.sem("d_in")
        up_high = st.sem("up_high")
        up_split = st.sem("up_split")
        d_high = st.sem("d_high")
        d_split = st.sem("d_split")
        gu_done = st.sem("gu_done")
        gate_scaled = st.sem("gate_scaled")
        silu_done = st.sem("silu_done")
        hid_done = st.sem("hid_done")
        down_done = st.sem("down_done")
        down_added = st.sem("down_added")
        own = st.sem("own")
        block = st.block()
        stream, base = m.stream, m.stream.base
        wg = w_gate.rearrange("a (k p) f -> p (a k) f", p=P)
        wu = w_up.rearrange("a (k p) f -> p (a k) f", p=P)
        wd = w_down.rearrange("a (t p) d -> p (a t) d", p=P)
        LAST = PAIRS - 1

        @block.sync
        def _(sp):
            def load_up(i):
                sp.dma_start(raw_up[:, :, :], wu[:, :, bass.ts(i, 2 * P)]).then_inc(up_in, 16)

            def load_d(i):
                sp.dma_start(raw_d[:, :, :], wd[:, bass.ts(i, 2), :]).then_inc(d_in, 16)

            load_up(0)
            load_d(0)
            with sp.Fori(1, PAIRS) as i:
                stream.load(sp, base + i, wg, lambda i: i * (2 * P), i)
                sp.wait_ge(up_split, i * 2)
                load_up(i)
                sp.wait_ge(d_split, i)
                load_d(i)
            if then is not None:
                stream.load(sp, base + PAIRS, *then)

        @block.tensor
        def _(pe):
            def pair(i, last_pair):
                for n in range(GU_UNITS):
                    t, c = divmod(n, NCH)
                    if c == 0:
                        pe.wait_ge(stream.split, (base + i) * 2 + (t + 1))
                    pe.wait_ge(hid_done, i * GU_UNITS + (n + 1))
                    for side, w_h, w_l in ((0, stream.high[t], stream.low[t]), (1, up_h[t], up_l[t])):
                        if side == 1 and c == 0:
                            pe.wait_ge(up_split, i * 2 + (t + 1))
                        for k in range(KD):
                            last = product(pe, m.ps[:, 2 * (n % 2) + side, width(c)], w_h[:, k, :], w_l[:, k, :],
                                           m.uh[:, k, chunk(c)], m.ul[:, k, chunk(c)], k == 0, k == KD - 1)
                    last.then_inc(gu_done, 1)
                pe.wait_ge(d_split, i + 1)
                for n in range(DOWN_UNITS):
                    c, o = divmod(n, KD)
                    if o == 0:
                        pe.wait_ge(hid_done, i * GU_UNITS + (NCH + c + 3))
                    pe.wait_ge(down_added, i * DOWN_UNITS + (n + 1))
                    for t in range(2):
                        last = product(pe, m.ps[:, 4 + n % 4, width(c)], d_h[:, t, o * P:(o + 1) * P],
                                       d_l[:, t, o * P:(o + 1) * P], hid_h[:, t, chunk(c)], hid_l[:, t, chunk(c)],
                                       t == 0, t == 1)
                    last.then_inc(down_done, 1)
                    if last_pair and norm and c and o == 5:
                        norm.tensor_mean(pe, c - 1, c * KD)

            with pe.Fori(0, LAST) as i:
                pair(i, False)
            pair(LAST, True)
            if norm:
                norm.tensor_mean(pe, NCH - 1, DOWN_UNITS)

        @block.scalar
        def _(act):
            def high_up(i, t):
                if t == 0:
                    act.wait_ge(up_in, (i + 1) * 16)
                act.activation(up_h[t][:, :, :], raw_up[:, :, t * P:(t + 1) * P], ACT.Copy).then_inc(up_high, 1)

            for t in range(2):
                high_up(0, t)

            def pair(i, more):
                act.wait_ge(d_in, (i + 1) * 16)
                act.wait_ge(down_added, i * DOWN_UNITS + 4)
                act.activation(d_h[:, :, :], raw_d[:, :, :], ACT.Copy).then_inc(d_high, 1)
                for n in range(GU_UNITS):
                    t, c = divmod(n, NCH)
                    act.wait_ge(gate_scaled, i * GU_UNITS + (n + 1))
                    act.activation(silu[:, n % 2, width(c)], silu[:, n % 2, width(c)], ACT.Silu).then_inc(silu_done, 1)
                    if c == NCH - 1:
                        if more or then is not None:
                            stream.split_high(act, base + i + 1, t)
                        if more:
                            high_up(i + 1, t)

            with act.Fori(0, LAST) as i:
                pair(i, True)
            pair(LAST, False)
            if norm:
                for n in range(DOWN_UNITS):
                    c, o = divmod(n, KD)
                    act.wait_ge(down_added, LAST * DOWN_UNITS + (n + 5))
                    norm.parts.scalar_high(act, o, c)
                    norm.scalar_square(act, n, n % 2, m.x[:, o, chunk(c)], c)
                    if c and o == 6:
                        norm.scalar_root(act, c - 1)
                norm.scalar_root(act, NCH - 1)

        @block.vector
        def _(dve):
            def low_up(i, t):
                dve.wait_ge(up_high, i * 2 + (t + 1))
                dve.tensor_tensor(up_l[t][:, :, :], raw_up[:, :, t * P:(t + 1) * P], up_h[t][:, :, :].bitcast(F32),
                                  ALU.subtract).then_inc(up_split, 1)

            dve.sem_inc(hid_done, 2)
            dve.sem_inc(down_added, 4)
            for t in range(2):
                low_up(0, t)
            if norm:
                norm.vector_clear(dve)

            def low(i, t, more):
                if more or then is not None:
                    stream.split_low(dve, base + i + 1, t)
                if more:
                    low_up(i + 1, t)

            def norm_tile(n):
                c, o = divmod(n, KD)
                norm.parts.vector_low(dve, n + 1, o, c)
                norm.vector_sum(dve, n, n % 2, c)

            def pair(i, more):
                dve.wait_ge(d_high, i + 1)
                dve.tensor_tensor(d_l[:, :, :], raw_d[:, :, :], d_h[:, :, :].bitcast(F32),
                                  ALU.subtract).then_inc(d_split, 1)
                order = Count(dve, own, i * (3 * GU_UNITS))
                for n in range(GU_UNITS):
                    t, c = divmod(n, NCH)
                    gate, hid, by = silu[:, n % 2, width(c)], up[:, width(c)], m.rstd[:, chunk(c)]
                    dve.wait_ge(gu_done, i * GU_UNITS + (n + 1))
                    dve.wait_ge(hid_done, i * GU_UNITS + (n + 1))
                    dve.tensor_tensor(gate, m.ps[:, 2 * (n % 2), width(c)], by, ALU.mult).then_inc(gate_scaled, 1)
                    dve.wait_ge(hid_done, i * GU_UNITS + (n + 2))
                    order.then_wait(dve.tensor_tensor(hid, m.ps[:, 2 * (n % 2) + 1, width(c)], by, ALU.mult))
                    dve.wait_ge(silu_done, i * GU_UNITS + (n + 1))
                    order.then_wait(dve.tensor_tensor(hid, gate, hid, ALU.mult))
                    order.then_wait(dve.tensor_copy(hid_h[:, t, chunk(c)], hid))
                    dve.tensor_tensor(hid_l[:, t, chunk(c)], hid, hid_h[:, t, chunk(c)].bitcast(F32),
                                      ALU.subtract).then_inc(hid_done, 1)
                    if n == NCH:
                        low(i, 0, more)
                for n in range(DOWN_UNITS):
                    c, o = divmod(n, KD)
                    dve.wait_ge(down_done, i * DOWN_UNITS + (n + 1))
                    dve.scalar_tensor_tensor(m.x[:, o, chunk(c)], m.ps[:, 4 + n % 4, width(c)], 0.5, m.x[:, o, chunk(c)],
                                             ALU.mult, ALU.add).then_inc(down_added, 1)
                    if n == KD - 1 and (more or not norm):
                        low(i, 1, more)
                    if not more and norm:
                        if n == 0:
                            low(i, 1, more)
                        else:
                            norm_tile(n - 1)
                        if c and o == 7:
                            norm.vector_invert(dve, c - 1)

            with dve.Fori(0, LAST) as i:
                pair(i, True)
            pair(LAST, False)
            if norm:
                norm_tile(DOWN_UNITS - 1)
                norm.vector_invert(dve, NCH - 1)
        stream.base += PAIRS


def final(nc, m, g_final, y_prompt, y_sample):
    BLOCKS = TB + 1
    with Stage(nc, "final") as st:
        tok = st.sbuf("tok", [P, BLOCKS, D])
        junk = st.sbuf("junk", [P, 2, D])
        gain = st.sbuf("gain", [P, D])
        stat = st.sbuf("stat", [P, 3, BLOCKS])
        gain_in = st.sem("gain_in")
        turned = st.sem("turned")
        squared = st.sem("squared")
        shifted = st.sem("shifted")
        rooted = st.sem("rooted")
        inverted = st.sem("inverted")
        normed = st.sem("normed")
        out_done = st.sem("out_done")
        block = st.block()
        yp = y_prompt.rearrange("a (b p) d -> p (a b) d", p=P)

        def rows(b):
            return slice(0, P if b < TB else NS)

        def flat(b):
            return m.ps[rows(b), 2 * (b % 4):2 * (b % 4) + 2, :].rearrange("p a f -> p (a f)")

        @block.tensor
        def _(pe):
            for b in range(BLOCKS):
                if b >= 4:
                    pe.wait_ge(normed, b - 3)
                for k in range(KD):
                    last = pe.transpose(m.ps[rows(b), 2 * (b % 4) + k // 4, (k % 4) * P:(k % 4 + 1) * P],
                                        m.x[:, k, b * P:min((b + 1) * P, T)], m.ident[:, :])
                last.then_inc(turned, 1)

        @block.scalar
        def _(act):
            def square(b):
                act.wait_ge(turned, b + 1)
                if b >= 2:
                    act.wait_ge(squared, b - 1)
                act.activation(junk[rows(b), b % 2, :], flat(b), ACT.Square,
                               accum_out=stat[rows(b), 0, b:b + 1]).then_inc(squared, 1)

            square(0)
            for b in range(BLOCKS):
                if b + 1 < BLOCKS:
                    square(b + 1)
                act.wait_ge(shifted, b + 1)
                act.activation(stat[rows(b), 1, b:b + 1], stat[rows(b), 1, b:b + 1], ACT.Sqrt).then_inc(rooted, 1)

        @block.vector
        def _(dve):
            dve.wait_ge(gain_in, 16)

            def shift(b):
                dve.wait_ge(squared, b + 1)
                dve.tensor_scalar(stat[rows(b), 1, b:b + 1], stat[rows(b), 0, b:b + 1], 1.0 / D, EPS, ALU.mult,
                                  ALU.add).then_inc(shifted, 1)

            shift(0)
            for b in range(BLOCKS):
                if b + 1 < BLOCKS:
                    shift(b + 1)
                dve.wait_ge(rooted, b + 1)
                dve.reciprocal(stat[rows(b), 2, b:b + 1], stat[rows(b), 1, b:b + 1]).then_inc(inverted, 1)
                dve.wait_ge(inverted, b + 1)
                dve.scalar_tensor_tensor(tok[rows(b), b, :], flat(b), stat[rows(b), 2, b:b + 1], gain[rows(b), :],
                                         ALU.mult, ALU.mult).then_inc(normed, 1)

        @block.sync
        def _(sp):
            sp.dma_start(gain[:, :], g_final.partition_broadcast(P)).then_inc(gain_in, 16)
            for b in range(TB):
                sp.wait_ge(normed, b + 1)
                sp.dma_start(yp[:, b, :], tok[:, b, :]).then_inc(out_done, 16)
            sp.wait_ge(normed, BLOCKS)
            sp.dma_start(y_sample.rearrange("n a d -> (n a) d"), tok[0:NS, TB, :]).then_inc(out_done, 16)
            sp.wait_ge(out_done, 16 * BLOCKS)


GROUPS = ((128, 1), (512, 4), (2048, 16))
NG = len(GROUPS)
HG = 4
DH = 64
GW = HG * DH
QKV = NG * GW
NPOOL = 4
POOL_W = NPOOL * P
MH = 4
MEM = 256
MEM_W = MH * P
Z_COL = 3 * QKV
QM_COL = Z_COL + POOL_W
GATE_COL = QM_COL + MEM_W
NEG = -1e30
REACH = 128
RES = GW + 2 * HG


class Product:

    def __init__(self, st, m, w, cols, pairs, then, banks=2 * NCH):
        self.banks = banks
        self.m, self.w, self.cols, self.pairs, self.then = m, w, cols, pairs, then
        self.base = m.stream.base
        self.done = st.sem("product_done")
        self.taken = st.sem("product_taken")

    def load(self, sp):
        self.m.stream.load_all(sp, self.pairs, self.w, self.cols, self.then)

    def tensor_pair(self, pe, i, ready=None, after=None):
        stream = self.m.stream
        for n in range(2 * NCH):
            t, c = divmod(n, NCH)
            if c == 0:
                pe.wait_ge(stream.split, (self.base + i) * 2 + (t + 1))
            pe.wait_ge(self.taken, i * (2 * NCH) + (n + 1))
            for k in range(KD):
                if ready is not None and t == 0:
                    pe.wait_ge(ready, c * KD + (k + 1))
                last = product(pe, self.m.ps[:, n % self.banks, width(c)], stream.high[t][:, k, :], stream.low[t][:, k, :],
                               self.m.uh[:, k, chunk(c)], self.m.ul[:, k, chunk(c)], k == 0, k == KD - 1)
            last.then_inc(self.done, 1)
            if after is not None:
                after(n)

    def tensor(self, pe):
        with pe.Fori(0, self.pairs) as i:
            self.tensor_pair(pe, i)

    def scalar_next(self, act, i, t):
        act.wait_ge(self.done, i * (2 * NCH) + (t + 1) * NCH)
        self.m.stream.split_high(act, self.base + i + 1, t)

    def scalar(self, act):
        with act.Fori(0, self.pairs) as i:
            for t in range(2):
                self.scalar_next(act, i, t)

    def vector_start(self, dve):
        dve.sem_inc(self.taken, self.banks)

    def vector_pair(self, dve, i, take, after=None):
        for n in range(2 * NCH):
            t, c = divmod(n, NCH)
            dve.wait_ge(self.done, i * (2 * NCH) + (n + 1))
            take(dve, i, t, c, self.m.ps[:, n % self.banks, width(c)]).then_inc(self.taken, 1)
            if c == NCH - 1:
                self.m.stream.split_low(dve, self.base + i + 1, t)
            if after is not None:
                after(n)

    def vector(self, dve, take):
        self.vector_start(dve)
        with dve.Fori(0, self.pairs) as i:
            self.vector_pair(dve, i, take)


    def tensor_beside(self, pe, beside):
        for i in range(self.pairs):
            self.tensor_pair(pe, i, after=lambda n: beside(i * (2 * NCH) + n))

    def vector_beside(self, dve, take, beside):
        self.vector_start(dve)
        for i in range(self.pairs):
            self.vector_pair(dve, i, take, after=lambda n: beside(i * (2 * NCH) + n))

    def close(self):
        self.m.stream.base += self.pairs


def scaled(dve, m, c, out, src):
    return dve.tensor_tensor(out, src, m.rstd[:, chunk(c)], ALU.mult)


def blocks_of(g):
    in_residue = SEQ // GROUPS[g][1] // P
    return [(b, in_residue > 1 and b % in_residue != 0) for b in range(TB)]


def attention(nc, m, g, w_in, new_kv, then):
    window, dil = GROUPS[g]
    length = SEQ // dil
    blocks = blocks_of(g)
    with Stage(nc, f"att{g}") as st:
        qkv = st.sbuf("qkv", [P, 6, T])
        with Stage(nc, f"qkv{g}") as pt:
            proj = Product(pt, m, w_in, lambda i: i * QKV + g * GW, 3, then)
            block = pt.block()

            def take(dve, i, t, c, src):
                n_l = (min(CHUNKS[c][0] + CHUNKS[c][1], SEQ) - CHUNKS[c][0]) // dil
                l0 = CHUNKS[c][0] // dil
                if c == NCH - 1:
                    at = i * (2 * NG) + (2 * g + t)
                    dve.tensor_tensor(m.s_qkv[:, bass.ds(at, 1), :], src[:, SEQ - CHUNKS[c][0]:].unsqueeze(1),
                                      m.rstd[:, SEQ:T].unsqueeze(1), ALU.mult)
                out = qkv[:, bass.ds(i * 2 + t, 1), 0:SEQ].rearrange("p a (r l) -> p (a r) l", r=dil)[:, :, l0:l0 + n_l]
                by = m.rstd[:, CHUNKS[c][0]:CHUNKS[c][0] + n_l * dil]
                return dve.tensor_tensor(out, src[:, 0:n_l * dil].rearrange("p (l r) -> p r l", r=dil),
                                         by.rearrange("p (l r) -> p r l", r=dil), ALU.mult)

            @block.sync
            def _(sp):
                proj.load(sp)

            @block.tensor
            def _(pe):
                proj.tensor(pe)

            @block.scalar
            def _(act):
                proj.scalar(act)

            @block.vector
            def _(dve):
                proj.vector(dve, take)
            proj.close()

        kv = st.sbuf("kv", [P, TB, 2 * GW])
        bias = st.sbuf("bias", [P, HG, 2 * P])
        logit = st.sbuf("logit", [P, 2, HG, 2 * P])
        falling = logit[:, 1, :, :]
        prob = st.sbuf("prob", [P, 2, HG, 2 * P])
        turned = st.sbuf("turned", [P, 2, 2, HG, P])
        res = st.sbuf("res", [P, TB, RES])
        neg = st.sbuf("neg", [P, 2, HG])
        bias_in = st.sem("bias_in")
        bias_ready = st.sem("bias_ready")
        kv_turned = st.sem("kv_turned")
        kv_taken = st.sem("kv_taken")
        scored = st.sem("scored")
        logits = st.sem("logits")
        maxed = st.sem("maxed")
        negated = st.sem("negated")
        exped = st.sem("exped")
        p_turned = st.sem("p_turned")
        p_taken_act = st.sem("p_taken_act")
        p_taken_dve = st.sem("p_taken_dve")
        weighed = st.sem("weighed")
        res_taken = st.sem("res_taken")
        stored = st.sem("stored")
        block = st.block()
        head_at = [2 * (i % 2) + i // 2 for i in range(HG)]

        def seen(b):
            return slice(0 if blocks[b][1] else P, 2 * P)

        kv_out = new_kv.rearrange("a n t c h d -> (a n t) (c h d)")
        kept = kv_out.shape[0]

        @block.sync
        def _(sp):
            for i, h in enumerate(head_at):
                row = m.bias_rows[g, g * HG + h, :]
                tile = bass.AP(row.tensor, row.offset, [[1, P], [1, 2 * P]])
                sp.dma_start(falling[:, i, :], tile).then_inc(bias_in, 16)
            n_out = 0
            for b in range(TB):
                for part in range(max(1, P // length)):
                    rows = min(P, length)
                    r, l0 = divmod(b * P + part * rows, length)
                    t_first = l0 * dil + r
                    if t_first >= SEQ - kept or g == 2:
                        n_out += 1
                        if part == 0:
                            sp.wait_ge(kv_taken, b + 1)
                        dst = kv_out.rearrange("(l r) c -> r l c", r=dil)[r, l0 - (SEQ - kept) // dil:l0 - (SEQ - kept) // dil + rows, :]
                        sp.dma_start(dst, kv[part * rows:(part + 1) * rows, b, :]).then_inc(stored, 16)
            for b in range(TB):
                sp.wait_ge(res_taken, b + 1)
                for part in range(max(1, P // length)):
                    rows = min(P, length)
                    r, l0 = divmod(b * P + part * rows, length)
                    dst = m.group_out.rearrange("(l r) g c -> r l g c", r=dil)[r, l0:l0 + rows, g, :]
                    n_out += 1
                    sp.dma_start(dst, res[part * rows:(part + 1) * rows, b, :]).then_inc(stored, 16)
            sp.wait_ge(stored, 16 * n_out)

        @block.tensor
        def _(pe):
            for b in range(TB):
                if b >= 2:
                    pe.wait_ge(kv_taken, b - 1)
                for i in range(4):
                    last = pe.transpose(m.ps[:, 4 + b % 2, i * P:(i + 1) * P], qkv[:, 2 + i, b * P:(b + 1) * P],
                                        m.ident[:, :])
                last.then_inc(kv_turned, 1)

            def scores(b):
                if b >= 2:
                    pe.wait_ge(logits, b - 1)
                for i, h in enumerate(head_at):
                    rows = slice(DH * (h % 2), DH * (h % 2) + DH)
                    bank = 2 * (b % 2) + i // 2
                    w = seen(b)
                    last = pe.matmul(m.ps[:, bank, (i % 2) * 2 * P + w.start:(i % 2 + 1) * 2 * P],
                                     qkv[rows, h // 2, b * P:(b + 1) * P],
                                     qkv[rows, 2 + h // 2, (b - 1) * P + w.start:(b + 1) * P], start=True, stop=True)
                last.then_inc(scored, 1)

            def turn(b):
                pe.wait_ge(exped, HG * (b + 1))
                if b == 0:
                    pe.wait_ge(kv_taken, TB)
                else:
                    pe.wait_ge(p_taken_act, b)
                    pe.wait_ge(p_taken_dve, b)
                for kb in range(0 if blocks[b][1] else 1, 2):
                    for i in range(HG):
                        last = pe.transpose(m.ps[:, 4 + kb, i * P:(i + 1) * P], prob[:, b % 2, i, kb * P:(kb + 1) * P],
                                            m.ident[:, :])
                last.then_inc(p_turned, 1)

            def weigh(b):
                pe.wait_ge(p_taken_act, b + 1)
                pe.wait_ge(p_taken_dve, b + 1)
                if b >= 2:
                    pe.wait_ge(res_taken, b - 1)
                for i, h in enumerate(head_at):
                    first = 0 if blocks[b][1] else 1
                    for kb in range(first, 2):
                        last = pe.matmul(m.ps[:, 6 + b % 2, h * DH:(h + 1) * DH], turned[:, b % 2, kb, i, :],
                                         kv[:, b - 1 + kb, GW + h * DH:GW + (h + 1) * DH],
                                         start=kb == first, stop=kb == 1)
                last.then_inc(weighed, 1)

            scores(0)
            scores(1)
            for b in range(TB):
                turn(b)
                if b + 2 < TB:
                    scores(b + 2)
                weigh(b)

        @block.scalar
        def _(act):
            def exps(b):
                act.wait_ge(negated, b + 1)
                if b >= 2:
                    act.wait_ge(p_turned, b - 1)
                w = seen(b)
                for i in range(HG):
                    act.activation(prob[:, b % 2, i, w], logit[:, b % 2, i, w], ACT.Exp, bias=neg[:, b % 2, i:i + 1],
                                   accum_out=res[:, b, GW + i:GW + i + 1]).then_inc(exped, 1)

            exps(0)
            for b in range(TB):
                if b + 1 < TB:
                    exps(b + 1)
                act.wait_ge(p_turned, b + 1)
                if b >= 2:
                    act.wait_ge(weighed, b - 1)
                act.activation(turned[:, b % 2, 1, :, :], m.ps[:, 5, :].rearrange("p (i q) -> p i q", i=HG),
                               ACT.Copy).then_inc(p_taken_act, 1)

        @block.vector
        def _(dve):
            for b in range(TB):
                dve.wait_ge(kv_turned, b + 1)
                dve.tensor_copy(kv[:, b, :], m.ps[:, 4 + b % 2, :]).then_inc(kv_taken, 1)
            dve.wait_ge(bias_in, 16 * HG)
            dve.tensor_copy(bias[:, :, :], falling[:, :, ::-1]).then_inc(bias_ready, 1)
            dve.wait_ge(bias_ready, 1)
            if length < P:
                dve.memset(bias[length:P, :, P:P + length], NEG).then_inc(bias_ready, 1)
                dve.wait_ge(bias_ready, 2)

            def soft(b):
                w = seen(b)
                dve.wait_ge(scored, b + 1)
                if b >= 2:
                    dve.wait_ge(exped, HG * (b - 1))
                src = m.ps[:, 2 * (b % 2):2 * (b % 2) + 2, :].rearrange("p a (i k) -> p (a i) k", k=2 * P)
                dve.scalar_tensor_tensor(logit[:, b % 2, :, w], src[:, :, w], DH ** -0.5, bias[:, :, w], ALU.mult,
                                         ALU.add).then_inc(logits, 1)
                dve.wait_ge(logits, b + 1)
                dve.tensor_reduce(res[:, b, GW + HG:GW + 2 * HG], logit[:, b % 2, :, w], AX_X,
                                  ALU.max).then_inc(maxed, 1)
                dve.wait_ge(maxed, b + 1)
                dve.tensor_scalar(neg[:, b % 2, :], res[:, b, GW + HG:GW + 2 * HG], -1.0, None,
                                  ALU.mult).then_inc(negated, 1)

            soft(0)
            for b in range(TB):
                if b + 1 < TB:
                    soft(b + 1)
                dve.wait_ge(p_turned, b + 1)
                if b >= 2:
                    dve.wait_ge(weighed, b - 1)
                if blocks[b][1]:
                    dve.tensor_copy(turned[:, b % 2, 0, :, :], m.ps[:, 4, :].rearrange("p (i q) -> p i q", i=HG)
                                    ).then_inc(p_taken_dve, 1)
                else:
                    dve.sem_inc(p_taken_dve, 1)
                if b >= 1:
                    dve.wait_ge(weighed, b)
                    dve.tensor_copy(res[:, b - 1, 0:GW], m.ps[:, 6 + (b - 1) % 2, 0:GW]).then_inc(res_taken, 1)
            dve.wait_ge(weighed, TB)
            dve.tensor_copy(res[:, TB - 1, 0:GW], m.ps[:, 6 + (TB - 1) % 2, 0:GW]).then_inc(res_taken, 1)


def combine(nc, m, ah, al):
    with Stage(nc, "combine") as st:
        part = st.sbuf("part", [P, TB, NG, RES])
        top = st.sbuf("top", [P, TB, HG])
        fall = st.sbuf("fall", [P, NG, TB, HG])
        den = st.sbuf("den", [P, TB, HG])
        whole = part[:, :, 0, 0:GW]
        loaded = st.sem("loaded")
        shifted = st.sem("shifted")
        exped = st.sem("exped")
        summed = st.sem("summed")
        turned = st.sem("turned")
        high = st.sem("high")
        own = st.sem("own")
        block = st.block()

        @block.sync
        def _(sp):
            sp.dma_start(part[:, :, :, :], m.group_out.rearrange("(b p) g c -> p b g c", p=P)).then_inc(loaded, 16)

        @block.vector
        def _(dve):
            order = Count(dve, own)
            dve.wait_ge(loaded, 16)
            maxima = [part[:, :, g, GW + HG:RES] for g in range(NG)]
            order.then_wait(dve.tensor_tensor(top[:, :, :], maxima[0], maxima[1], ALU.max))
            order.then_wait(dve.tensor_tensor(top[:, :, :], top[:, :, :], maxima[2], ALU.max))
            for g in range(NG):
                ins = dve.tensor_tensor(fall[:, g, :, :], maxima[g], top[:, :, :], ALU.subtract)
                ins.then_inc(shifted, 1)
            dve.wait_ge(exped, 1)
            for g in range(NG):
                sums = part[:, :, g, GW:GW + HG]
                order.then_wait(dve.tensor_tensor(sums, sums, fall[:, g, :, :], ALU.mult))
            order.then_wait(dve.tensor_tensor(den[:, :, :], part[:, :, 0, GW:GW + HG], part[:, :, 1, GW:GW + HG], ALU.add))
            order.then_wait(dve.tensor_tensor(den[:, :, :], den[:, :, :], part[:, :, 2, GW:GW + HG], ALU.add))
            order.then_wait(dve.reciprocal(den[:, :, :], den[:, :, :]))
            for g in range(NG):
                order.then_wait(dve.tensor_tensor(fall[:, g, :, :], fall[:, g, :, :], den[:, :, :], ALU.mult))
            for g in range(NG):
                for par in range(2):
                    vals = part[:, :, g, 0:GW].rearrange("p b (hh par d) -> p par b hh d", hh=2, par=2)[:, par]
                    w = fall[:, g, :, 2 * par:2 * par + 2].unsqueeze(3).to_broadcast([P, TB, 2, DH])
                    order.then_wait(dve.tensor_tensor(vals, vals, w, ALU.mult))
            sl = [part[:, :, g, 0:GW] for g in range(NG)]
            order.then_wait(dve.tensor_tensor(whole[:, :, :], sl[0], sl[1], ALU.add))
            dve.tensor_tensor(whole[:, :, :], whole[:, :, :], sl[2], ALU.add).then_inc(summed, 1)
            for n in range(4):
                dve.wait_ge(high, n + 1)
                k, half = divmod(n, 2)
                dve.tensor_tensor(al[:, k, half * 512:(half + 1) * 512], m.ps[:, n, :],
                                  ah[:, k, half * 512:(half + 1) * 512].bitcast(F32), ALU.subtract)
            dve.wait_ge(high, 5)
            dve.tensor_tensor(al[:, :, SEQ:T], m.s_att[:, :, :], ah[:, :, SEQ:T].bitcast(F32), ALU.subtract)

        @block.scalar
        def _(act):
            act.wait_ge(shifted, NG)
            act.activation(fall[:, :, :, :], fall[:, :, :, :], ACT.Exp).then_inc(exped, 1)
            for n in range(4):
                k, half = divmod(n, 2)
                act.wait_ge(turned, n + 1)
                act.activation(ah[:, k, half * 512:(half + 1) * 512], m.ps[:, n, :], ACT.Copy).then_inc(high, 1)
            act.activation(ah[:, :, SEQ:T], m.s_att[:, :, :], ACT.Copy).then_inc(high, 1)

        @block.tensor
        def _(pe):
            pe.wait_ge(summed, 1)
            for n in range(4):
                k, half = divmod(n, 2)
                for b in range(4):
                    last = pe.transpose(m.ps[:, n, b * P:(b + 1) * P], whole[:, 4 * half + b, k * P:(k + 1) * P],
                                        m.ident[:, :])
                last.then_inc(turned, 1)


def merge(nc, m, name, branch, first, w_in, w_o, bh, bl, kt, then, late=None):
    with Stage(nc, name) as st:
        raw_o = st.sbuf("raw_o", [P, kt, 2 * P])
        o_h = [st.sbuf(f"o_h{t}", [P, kt, P], F32R) for t in range(2)]
        o_l = [st.sbuf(f"o_l{t}", [P, kt, P], F32R) for t in range(2)]
        gate = st.sbuf("gate", [P, NCH, CH])
        o_in = st.sem("o_in")
        o_high = st.sem("o_high")
        o_split = st.sem("o_split")
        late_in = [st.sem(f"late_in{i}") for i in range(2)]
        late_high = st.sem("late_high")
        late_split = st.sem("late_split")
        gate_done = st.sem("gate_done")
        scaled_sem = st.sem("scaled")
        gated = st.sem("gated")
        o_done = st.sem("o_done")
        own = st.sem("own")
        mixed = st.sem("mixed")
        block = st.block()
        units = 2 * NCH
        pairs = KD // 2
        stream, base = m.stream, m.stream.base
        halves = gate[:, :, :].rearrange("p c t -> p (c t)")[:, 0:SEQ].rearrange("p (s t) -> p s t", s=2)

        def piece(x, n):
            half, k = divmod(n, kt)
            return x[:, k, half * (SEQ // 2):(half + 1) * (SEQ // 2)]

        @block.sync
        def _(sp):
            def load_o(i):
                sp.dma_start(raw_o[:, :, :], w_o[:, :, bass.ds(i * (2 * P), 2 * P)]).then_inc(o_in, 16)

            load_o(0)
            if late is not None:
                for n in range(2 * kt):
                    if n >= 2:
                        sp.wait_ge(late_split, n - 1)
                    sp.dma_start(halves[:, n % 2, :], piece(late[0], n)).then_inc(late_in[n % 2], 16)
            with sp.Fori(1, pairs) as i:
                sp.wait_ge(o_split, i * 2)
                load_o(i)
                stream.load(sp, base + i, w_in, lambda i: i * (2 * P) + (GATE_COL + branch * D), i)
            stream.load(sp, base + pairs, *then)

        @block.tensor
        def _(pe):
            def pair(i, start):
                for t in range(2):
                    pe.wait_ge(stream.split, (base + i) * 2 + (t + 1))
                    for c in range(NCH):
                        pe.wait_ge(scaled_sem, i * units + (NCH * t + c + 1))
                        for k in range(KD):
                            last = product(pe, m.ps[:, 2 * c, width(c)], stream.high[t][:, k, :], stream.low[t][:, k, :],
                                           m.uh[:, k, chunk(c)], m.ul[:, k, chunk(c)], k == 0, k == KD - 1)
                        last.then_inc(gate_done, 1)
                    pe.wait_ge(o_split, i * 2 + (t + 1))
                    for c in range(NCH):
                        if start and t == 0 and late is not None:
                            pe.wait_ge(late_split, kt if c == 0 else 2 * kt)
                        pe.wait_ge(mixed, i * units + (NCH * t + c + 1))
                        for k in range(kt):
                            last = product(pe, m.ps[:, 2 * c + 1, width(c)], o_h[t][:, k, :], o_l[t][:, k, :],
                                           bh[:, k, chunk(c)], bl[:, k, chunk(c)], k == 0, k == kt - 1)
                        last.then_inc(o_done, 1)

            pair(0, True)
            with pe.Fori(1, pairs) as i:
                pair(i, False)

        @block.scalar
        def _(act):
            def high(i, t):
                if t == 0:
                    act.wait_ge(o_in, (i + 1) * 16)
                act.activation(o_h[t][:, :, :], raw_o[:, :, t * P:(t + 1) * P], ACT.Copy).then_inc(o_high, 1)

            for t in range(2):
                high(0, t)
            if late is not None:
                act.activation(bh[:, :, SEQ:T], late[1], ACT.Copy).then_inc(late_high, 1)
                for n in range(2 * kt):
                    act.wait_ge(late_in[n % 2], 16 * (n // 2 + 1))
                    act.activation(piece(bh, n), halves[:, n % 2, :], ACT.Copy).then_inc(late_high, 1)

            def pair(i, more):
                for t in range(2):
                    for c in range(NCH):
                        act.wait_ge(scaled_sem, i * units + (NCH * t + c + 4))
                        act.activation(gate[:, c, width(c)], gate[:, c, width(c)], ACT.Sigmoid).then_inc(gated, 1)
                    stream.split_high(act, base + i + 1, t)
                    if more:
                        act.wait_ge(o_done, i * units + NCH * (t + 1))
                        high(i + 1, t)

            with act.Fori(0, pairs - 1) as i:
                pair(i, True)
            pair(pairs - 1, False)

        @block.vector
        def _(dve):
            def low(i, t):
                dve.wait_ge(o_high, i * 2 + (t + 1))
                dve.tensor_tensor(o_l[t][:, :, :], raw_o[:, :, t * P:(t + 1) * P], o_h[t][:, :, :].bitcast(F32),
                                  ALU.subtract).then_inc(o_split, 1)

            dve.sem_inc(mixed, NCH)
            dve.sem_inc(scaled_sem, NCH)
            for t in range(2):
                low(0, t)
            if late is not None:
                dve.wait_ge(late_high, 1)
                dve.tensor_tensor(bl[:, :, SEQ:T], late[1], bh[:, :, SEQ:T].bitcast(F32), ALU.subtract)
                for n in range(2 * kt):
                    dve.wait_ge(late_high, n + 2)
                    dve.tensor_tensor(piece(bl, n), halves[:, n % 2, :], piece(bh, n).bitcast(F32),
                                      ALU.subtract).then_inc(late_split, 1)
                dve.wait_ge(late_split, 2 * kt)

            def pair(i, more):
                order = Count(dve, own, i * units)
                for t in range(2):
                    for c in range(NCH):
                        dve.wait_ge(gate_done, i * units + (NCH * t + c + 1))
                        dve.wait_ge(mixed, i * units + (NCH * t + c + 1))
                        scaled(dve, m, c, gate[:, c, width(c)], m.ps[:, 2 * c, width(c)]).then_inc(scaled_sem, 1)
                    stream.split_low(dve, base + i + 1, t)
                    for c in range(NCH):
                        n = NCH * t + c
                        dve.wait_ge(o_done, i * units + (n + 1))
                        dve.wait_ge(gated, i * units + (n + 1))
                        g, proj = gate[:, c, width(c)], m.ps[:, 2 * c + 1, width(c)]
                        mix = m.mix[:, bass.ds(i * 2 + t, 1), chunk(c)].rearrange("p a t -> p (a t)")
                        if first:
                            dve.tensor_tensor(mix, g, proj, ALU.mult).then_inc(mixed, 1)
                        else:
                            order.then_wait(dve.tensor_tensor(g, g, proj, ALU.mult))
                            dve.tensor_tensor(mix, mix, g, ALU.add).then_inc(mixed, 1)
                    if more:
                        low(i + 1, t)

            with dve.Fori(0, pairs - 1) as i:
                pair(i, True)
            pair(pairs - 1, False)
        stream.base += pairs


def mix_out(nc, m, w_out, next_norm, then):
    with Stage(nc, "mix_out") as st:
        pairs = KD // 2
        proj = Product(st, m, w_out, lambda i: i * (2 * P), pairs, then)
        norm = Norm(st, m, next_norm, (6, 7, 6))
        mix_high = st.sem("mix_high")
        mix_low = st.sem("mix_low")
        block = st.block()
        units = 2 * NCH

        def tile_of_x(i, t, c):
            return m.x[:, bass.ds(i * 2 + t, 1), chunk(c)].rearrange("p a t -> p (a t)")

        @block.sync
        def _(sp):
            proj.load(sp)

        @block.tensor
        def _(pe):
            def mean(n):
                if n > NCH:
                    norm.tensor_mean(pe, n - NCH - 1, (pairs - 1) * units + n)

            proj.tensor_pair(pe, 0, ready=mix_low)
            with pe.Fori(1, pairs - 1) as i:
                proj.tensor_pair(pe, i)
            proj.tensor_pair(pe, pairs - 1, after=mean)
            norm.tensor_mean(pe, NCH - 1, pairs * units)

        @block.scalar
        def _(act):
            for c in range(NCH):
                for k in range(KD):
                    act.activation(m.uh[:, k, chunk(c)], m.mix[:, k, chunk(c)], ACT.Copy).then_inc(mix_high, 1)

            def pair(i, last):
                for n in range(units):
                    t, c = divmod(n, NCH)
                    act.wait_ge(proj.taken, (i + 1) * units + (n + 1))
                    norm.scalar_square(act, i * units + n, n % 2, tile_of_x(i, t, c), c)
                    if last and t == 1:
                        for k in range(KD):
                            norm.parts.scalar_high(act, k, c)
                        if c:
                            norm.scalar_root(act, c - 1)
                    if c == NCH - 1:
                        proj.scalar_next(act, i, t)
                if last:
                    norm.scalar_root(act, NCH - 1)

            with act.Fori(0, pairs - 1) as i:
                pair(i, False)
            pair(pairs - 1, True)

        @block.vector
        def _(dve):
            proj.vector_start(dve)
            for n in range(NCH * KD):
                c, k = divmod(n, KD)
                dve.wait_ge(mix_high, n + 1)
                dve.tensor_tensor(m.ul[:, k, chunk(c)], m.mix[:, k, chunk(c)], m.uh[:, k, chunk(c)].bitcast(F32),
                                  ALU.subtract).then_inc(mix_low, 1)
            norm.vector_clear(dve)

            def add(dve, i, t, c, src):
                x = tile_of_x(i, t, c)
                return dve.tensor_tensor(x, x, src, ALU.add)

            def pair(i, last):
                def norm_tile(n):
                    t, c = divmod(n, NCH)
                    norm.vector_sum(dve, i * units + n, n % 2, c)
                    if last and t == 1:
                        for k in range(KD):
                            norm.parts.vector_low(dve, KD * c + k + 1, k, c)
                        if c:
                            norm.vector_invert(dve, c - 1)
                proj.vector_pair(dve, i, add, norm_tile)

            with dve.Fori(0, pairs - 1) as i:
                pair(i, False)
            pair(pairs - 1, True)
            norm.vector_invert(dve, NCH - 1)
        proj.close()


POOL_WINDOWS = (2, 4, 8, 16)
HIST = 15
PAD = 16


def pool_values(nc, m, z, w_in, then, caches, new_kv):
    rows = NS * HG
    with Stage(nc, "samp") as st:
        proj = Product(st, m, w_in, lambda i: i * (2 * P) + Z_COL, NPOOL // 2, then, banks=NCH)
        cache = [st.sbuf(f"cache{g}", [REACH, NS, 2 * GW]) for g in range(NG)]
        tok = st.sbuf("tok", [NS, 3 * QKV])
        own_of = st.sbuf("own_of", [rows, NS])
        prod = st.sbuf("prod", [P, QKV])
        score = st.sbuf("score", [P, NG, NS, HG])
        new_prod = prod[0:NS, :]
        new_score = st.sbuf("new_score", [NS, NG, HG])
        prob = st.sbuf("prob", [rows, NG, REACH + 1])
        small = st.sbuf("small", [rows, 4])
        diag = st.sbuf("diag", [rows, NG, rows])
        p_cols = st.sbuf("p_cols", [P, NG, rows])
        new_p = st.sbuf("new_p", [NS, NG, rows])
        cleared = st.sem("cleared")
        cache_in = [st.sem(f"cache_in{g}") for g in range(NG)]
        own_of_in = st.sem("own_of_in")
        stored = st.sem("stored")
        new_out = st.sem("new_out")
        new_back = st.sem("new_back")
        tok_turned = st.sem("tok_turned")
        tok_taken = st.sem("tok_taken")
        spread = st.sem("spread")
        multiplied = st.sem("multiplied")
        scored = st.sem("scored")
        own = st.sem("own")
        logits = st.sem("logits")
        new_scored = st.sem("new_scored")
        rowed = st.sem("rowed")
        maxed = st.sem("maxed")
        exped = st.sem("exped")
        normal = st.sem("normal")
        coled = st.sem("coled")
        cols_taken = st.sem("cols_taken")
        weighed = st.sem("weighed")
        block = st.block()
        flat = prob[:, :, :].rearrange("p g r -> p (g r)")

        def take(dve, i, t, c, src):
            out = z[:, i * 2 + t, PAD + CHUNKS[c][0]:PAD + CHUNKS[c][0] + CHUNKS[c][1]]
            return scaled(dve, m, c, out, src)

        def spread_queries(n, g):
            at = g * GW
            return m.ps[:, 3 + 2 * (n % 2) + at // 512, at % 512:at % 512 + GW]

        @block.sync
        def _(sp):
            for g in range(NG):
                src = caches[g].rearrange("a n (r d) c h e -> r d (a n) (c h e)", d=GROUPS[g][1])[:, 0]
                sp.dma_start(cache[g][:, :, :], src).then_inc(cache_in[g], 16)
            sp.dma_start(own_of[:, :], m.own_in).then_inc(own_of_in, 16)
            proj.load(sp)
            sp.wait_ge(tok_taken, 5)
            for g in range(NG):
                dst = new_kv[g].rearrange("a n t c h e -> (a n t) c (h e)")
                for side in range(2):
                    sp.dma_start(dst[:, side, :], tok[:, (1 + side) * QKV + g * GW:(1 + side) * QKV + (g + 1) * GW]
                                 ).then_inc(stored, 16)
            sp.wait_ge(new_scored, 1)
            with nc.allow_non_contiguous_dma(reason="96 scores"):
                for g in range(NG):
                    sp.dma_start(m.new_scores[:, :, g], new_score[:, g, :]).then_inc(new_out, 16)
                sp.wait_ge(new_out, 16 * NG)
                sp.dma_start(prob[:, :, REACH], m.new_scores.rearrange("n h g -> (n h) g")).then_inc(new_back, 16)
            sp.wait_ge(stored, 16 * 2 * NG)

        @block.tensor
        def _(pe):
            def beside(u):
                if u == 0:
                    for i in range(2 * NG * 3):
                        last = pe.transpose(m.ps[0:NS, 3 + i // 4, (i % 4) * P:(i % 4 + 1) * P], m.s_qkv[:, i, :],
                                            m.ident[:, :])
                    last.then_inc(tok_turned, 1)
                if 1 <= u <= 4:
                    pe.wait_ge(tok_taken, 5)
                    for n in range(2 * (u - 1), 2 * u):
                        if n >= 2:
                            pe.wait_ge(multiplied, n - 1)
                        for g in range(NG):
                            last = pe.matmul(spread_queries(n, g), m.ident[0:NS, n:n + 1].to_broadcast([NS, P]),
                                             tok[:, g * GW:(g + 1) * GW], start=True, stop=True)
                        last.then_inc(spread, 1)
                if u == 6:
                    pe.wait_ge(logits, 1)
                    for g in range(NG):
                        last = pe.transpose(m.ps[0:rows, 7, g * P:(g + 1) * P],
                                            score[:, g, :, :].rearrange("p n h -> p (n h)"), m.ident[:, :])
                    last.then_inc(rowed, 1)
                if u == 9:
                    pe.wait_ge(normal, 2)
                    pe.wait_ge(own_of_in, 16)
                    for g in range(NG):
                        pe.transpose(m.ps[:, 3, g * rows:(g + 1) * rows], prob[:, g, 0:REACH], m.ident[0:rows, 0:rows])
                    pe.matmul(m.ps[0:NS, 4, 0:NG * rows], own_of[:, :], diag[:, :, :].rearrange("p g r -> p (g r)"),
                              start=True, stop=True).then_inc(coled, 1)
                if u == 10:
                    pe.wait_ge(cols_taken, 2)
                    for c in range(2):
                        for g in range(NG):
                            v = 2 * QKV + g * GW + c * P
                            pe.matmul(m.ps[:, 5 + c, 0:rows], tok[:, v:v + P], new_p[:, g, :], start=g == 0, stop=False,
                                      skip_group_check=True)
                        for n in range(NS):
                            for g in range(NG):
                                last = pe.matmul(m.ps[:, 5 + c, n * HG:(n + 1) * HG],
                                                 cache[g][:, n, GW + c * P:GW + (c + 1) * P],
                                                 p_cols[:, g, n * HG:(n + 1) * HG], start=False,
                                                 stop=n == NS - 1 and g == NG - 1, skip_group_check=True)
                    last.then_inc(weighed, 1)

            proj.tensor_beside(pe, beside)

        @block.vector
        def _(dve):
            order = Count(dve, own)

            def beside(u):
                if u == 0:
                    dve.wait_ge(tok_turned, 1)
                    for b in range(5):
                        w = min(512, 3 * QKV - b * 512)
                        dve.tensor_copy(tok[:, b * 512:b * 512 + w], m.ps[0:NS, 3 + b, 0:w]).then_inc(tok_taken, 1)
                if u == 1:
                    for g in range(NG):
                        dve.wait_ge(cache_in[g], 16)
                if 1 <= u <= 4:
                    for n in range(2 * (u - 1), 2 * u):
                        dve.wait_ge(spread, n + 1)
                        if n >= 1:
                            dve.wait_ge(scored, n)
                        for g in range(NG):
                            ins = dve.tensor_tensor(prod[:, g * GW:(g + 1) * GW], cache[g][:, n, 0:GW],
                                                    spread_queries(n, g), ALU.mult)
                        ins.then_inc(multiplied, 1)
                        dve.wait_ge(multiplied, n + 1)
                        dve.tensor_reduce(score[:, :, n, :], prod[:, :].rearrange("p (g h d) -> p g h d", g=NG, h=HG),
                                          AX_X, ALU.add).then_inc(scored, 1)
                if u == 5:
                    dve.wait_ge(scored, NS)
                    for g in range(NG):
                        ins = dve.scalar_tensor_tensor(score[:, g, :, :], score[:, g, :, :], DH ** -0.5,
                                                       m.cache_bias[:, g, :].unsqueeze(1).to_broadcast([P, NS, HG]),
                                                       ALU.mult, ALU.add)
                    ins.then_inc(logits, 1)
                    dve.wait_ge(tok_taken, 5)
                    order.then_wait(dve.tensor_tensor(new_prod, tok[:, 0:QKV], tok[:, QKV:2 * QKV], ALU.mult))
                    new = new_score[:, :, :].rearrange("n g h -> n (g h)")
                    order.then_wait(dve.tensor_reduce(new, new_prod.rearrange("n (s d) -> n s d", d=DH), AX_X, ALU.add))
                    dve.scalar_tensor_tensor(new, new, DH ** -0.5, m.new_bias[:, :], ALU.mult,
                                             ALU.add).then_inc(new_scored, 1)
                if u == 7:
                    dve.wait_ge(rowed, 1)
                    order.then_wait(dve.tensor_copy(prob[:, :, 0:REACH],
                                                    m.ps[0:rows, 7, 0:NG * P].rearrange("p (g r) -> p g r", g=NG)))
                    dve.wait_ge(new_back, 16)
                    order.then_wait(dve.tensor_reduce(small[:, 0:1], flat, AX_X, ALU.max))
                    dve.tensor_scalar(small[:, 1:2], small[:, 0:1], -1.0, None, ALU.mult).then_inc(maxed, 1)
                if u == 8:
                    dve.wait_ge(exped, 1)
                    order.then_wait(dve.reciprocal(small[:, 3:4], small[:, 2:3]))
                    dve.tensor_scalar(flat, flat, small[:, 3:4], None, ALU.mult).then_inc(normal, 1)
                    dve.wait_ge(normal, 1)
                    for g in range(NG):
                        ins = dve.tensor_scalar(diag[:, g, :], m.ident[0:rows, 0:rows], prob[:, g, REACH:REACH + 1],
                                                None, ALU.mult)
                    ins.then_inc(normal, 1)
                if u == 9:
                    dve.wait_ge(coled, 1)
                    dve.tensor_copy(p_cols[:, :, :], m.ps[:, 3, 0:NG * rows].rearrange("p (g r) -> p g r", g=NG)
                                    ).then_inc(cols_taken, 1)
                    dve.tensor_copy(new_p[:, :, :], m.ps[0:NS, 4, 0:NG * rows].rearrange("p (g r) -> p g r", g=NG)
                                    ).then_inc(cols_taken, 1)
                if u == 11:
                    dve.wait_ge(weighed, 1)
                    for c in range(2):
                        for half in range(2):
                            part = slice(half * DH, (half + 1) * DH)
                            src = m.ps[part, 5 + c, 0:rows].rearrange("p (n h) -> p h n", h=HG)[:, 2 * c + half, :]
                            dve.tensor_copy(m.s_att[part, c, :], src)

            dve.memset(z[:, :, 0:PAD], 0.0).then_inc(cleared, 1)
            proj.vector_beside(dve, take, beside)

        @block.scalar
        def _(act):
            for t in range(2):
                proj.scalar_next(act, 0, t)
            act.wait_ge(maxed, 1)
            act.activation(flat, flat, ACT.Exp, bias=small[:, 1:2], accum_out=small[:, 2:3]).then_inc(exped, 1)
            for t in range(2):
                proj.scalar_next(act, 1, t)
        proj.close()


def pooling(nc, m, z, state_pool, w_pool, new_pool_prompt, new_pool_sample, bh, bl):
    with Stage(nc, "pool") as st:
        sums = st.sbuf("sums", [P, 2, PAD + SEQ])
        hist = st.sbuf("hist", [NS * HIST, POOL_W])
        w = st.sbuf("w", [P, NPOOL, P])
        inv = st.sbuf("inv", [P, NPOOL, PAD])
        first = st.sbuf("first", [P, PAD])
        past = st.sbuf("past", [P, NPOOL, NS])
        ztok = st.sbuf("ztok", [HIST, POOL_W])
        zstok = st.sbuf("zstok", [NS, POOL_W])
        loaded = st.sem("loaded")
        turned = st.sem("turned")
        taken = st.sem("taken")
        stored = st.sem("stored")
        own = st.sem("own")
        ready = st.sem("ready")
        mapped = st.sem("mapped")
        high = st.sem("high")
        split = st.sem("split")
        block = st.block()

        @block.sync
        def _(sp):
            sp.dma_start(hist[:, :], state_pool.rearrange("a n r c -> (a n r) c")).then_inc(loaded, 16)
            sp.dma_start(w[:, :, :], w_pool.rearrange("a g c d -> c (a g) d")).then_inc(loaded, 16)
            sp.dma_start(inv[:, :, :], m.inv_in).then_inc(loaded, 16)
            sp.wait_ge(taken, 2)
            sp.dma_start(new_pool_prompt.rearrange("a n r c -> (a n r) c"), ztok[:, :]).then_inc(stored, 16)
            sp.dma_start(new_pool_sample.rearrange("a n r c -> (a n r) c"), zstok[:, :]).then_inc(stored, 16)
            sp.wait_ge(stored, 32)

        @block.tensor
        def _(pe):
            for k in range(NPOOL):
                pe.transpose(m.ps[0:HIST, 0, k * P:(k + 1) * P], z[:, k, PAD + SEQ - HIST:PAD + SEQ], m.ident[:, :])
                pe.transpose(m.ps[0:NS, 1, k * P:(k + 1) * P], z[:, k, PAD + SEQ:PAD + T], m.ident[:, :])
            pe.wait_ge(loaded, 48)
            for k in range(NPOOL):
                last = pe.transpose(m.ps[:, 2, k * NS * HIST:(k + 1) * NS * HIST], hist[:, k * P:(k + 1) * P],
                                    m.ident[0:NS * HIST, 0:NS * HIST])
            last.then_inc(turned, 1)
            for k in range(NPOOL):
                pe.wait_ge(ready, k + 1)
                for c in range(NCH):
                    n = k * NCH + c
                    if n >= 5:
                        pe.wait_ge(split, n - 4)
                    pe.matmul(m.ps[:, 3 + n % 5, width(c)], w[:, k, :], z[:, k, PAD + CHUNKS[c][0]:PAD + CHUNKS[c][0] + CHUNKS[c][1]], start=True,
                              stop=True).then_inc(mapped, 1)

        @block.scalar
        def _(act):
            for n in range(NPOOL * NCH):
                k, c = divmod(n, NCH)
                act.wait_ge(mapped, n + 1)
                act.activation(bh[:, k, chunk(c)], m.ps[:, 3 + n % 5, width(c)], ACT.Copy,
                               scale=m.gain[:, GAIN_ROWS + k:GAIN_ROWS + k + 1]).then_inc(high, 1)

        @block.vector
        def _(dve):
            order = Count(dve, own)
            order.then_wait(dve.memset(sums[:, :, 0:PAD], 0.0))
            dve.wait_ge(turned, 1)
            dve.tensor_copy(ztok[:, :], m.ps[0:HIST, 0, :]).then_inc(taken, 1)
            dve.tensor_copy(zstok[:, :], m.ps[0:NS, 1, :]).then_inc(taken, 1)
            dve.wait_ge(loaded, 48)
            for k, window in enumerate(POOL_WINDOWS):
                past_rows = m.ps[:, 2, k * NS * HIST:(k + 1) * NS * HIST].rearrange("p (n r) -> p n r", n=NS)
                dve.tensor_reduce(past[:, k, :], past_rows[:, :, HIST + 1 - window:HIST], AX_X, ALU.add).then_inc(own, 1)
                order.n += 1
                src = z[:, k, :]
                for j in range(k + 1):
                    dst = sums[:, j % 2, :]
                    order.then_wait(dve.tensor_tensor(dst[:, PAD:PAD + SEQ], src[:, PAD:PAD + SEQ],
                                                      src[:, PAD - 2 ** j:PAD + SEQ - 2 ** j], ALU.add))
                    src = dst
                zk = z[:, k, PAD:PAD + SEQ]
                dve.scalar_tensor_tensor(zk[:, PAD:SEQ], src[:, 2 * PAD:PAD + SEQ], 1.0 / window,
                                         zk[:, PAD:SEQ], ALU.mult, ALU.subtract)
                order.then_wait(dve.tensor_tensor(first[:, :], src[:, PAD:2 * PAD], inv[:, k, :], ALU.mult))
                order.then_wait(dve.tensor_tensor(zk[:, 0:PAD], first[:, :], zk[:, 0:PAD], ALU.subtract))
                zs = z[:, k, PAD + SEQ:PAD + T]
                order.then_wait(dve.tensor_tensor(past[:, k, :], past[:, k, :], zs, ALU.add))
                dve.scalar_tensor_tensor(zs, past[:, k, :], 1.0 / window, zs, ALU.mult,
                                         ALU.subtract).then_inc(ready, 1)
                dve.wait_ge(ready, k + 1)
            for n in range(NPOOL * NCH):
                k, c = divmod(n, NCH)
                dve.wait_ge(high, n + 1)
                dve.scalar_tensor_tensor(bl[:, k, chunk(c)], m.ps[:, 3 + n % 5, width(c)],
                                         m.gain[:, GAIN_ROWS + k:GAIN_ROWS + k + 1], bh[:, k, chunk(c)].bitcast(F32),
                                         ALU.mult, ALU.subtract).then_inc(split, 1)


def memory_attention(nc, m, w_in, mem_prompt, w_mem_kv, new_mem_kv, then):
    MT = MEM // P
    scale = P ** -0.5
    with Stage(nc, "mem") as st:
        kv = st.sbuf("kv", [P, MT, 2 * MEM_W])
        kt = st.sbuf("kt", [P, MH, MEM])
        with Stage(nc, "memkv") as kt_st:
            tok = kt_st.sbuf("tok", [P, MT, D])
            w = kt_st.sbuf("w", [P, KD, D // 2])
            turned_m = kt_st.sbuf("turned", [P, KD, MEM])
            stat = kt_st.sbuf("stat", [P, MT])
            tok_in = kt_st.sem("tok_in")
            w_arrived = kt_st.sem("w_arrived")
            squared = kt_st.sem("squared")
            own = kt_st.sem("own")
            rooted = kt_st.sem("rooted")
            normed = kt_st.sem("normed")
            turned = kt_st.sem("turned_sem")
            gained = kt_st.sem("gained")
            done = kt_st.sem("done")
            taken = kt_st.sem("taken")
            kt_done = kt_st.sem("kt_done")
            stored = kt_st.sem("stored")
            block = kt_st.block()
            out = new_mem_kv.rearrange("a n (t p) c h e -> p (a n t) (c h e)", p=P)
            w_v = w_mem_kv.rearrange("a (k p) f -> p (a k) f", p=P)

            @block.sync
            def _(sp):
                sp.dma_start(tok[:, :, :], mem_prompt.rearrange("a (t p) d -> p (a t) d", p=P)).then_inc(tok_in, 16)
                sp.dma_start(w[:, :, :], w_v[:, :, 0:D // 2]).then_inc(w_arrived, 16)
                sp.wait_ge(done, MT)
                sp.dma_start(w[:, :, :], w_v[:, :, D // 2:D]).then_inc(w_arrived, 16)
                sp.wait_ge(taken, 2 * MT)
                sp.dma_start(out, kv[:, :, :]).then_inc(stored, 16)
                sp.wait_ge(stored, 16)

            @block.scalar
            def _(act):
                act.wait_ge(tok_in, 16)
                for t in range(MT):
                    if t:
                        act.wait_ge(squared, t)
                    act.activation(m.ps[:, 6:8, :].rearrange("p a f -> p (a f)"), tok[:, t, :], ACT.Square, accum_out=stat[:, t:t + 1]).then_inc(squared, 1)
                act.wait_ge(own, 1)
                act.activation(stat[:, :], stat[:, :], ACT.Sqrt).then_inc(rooted, 1)
                for k in range(KD):
                    act.wait_ge(turned, k // 2 + 1)
                    act.activation(turned_m[:, k, :], m.ps[:, k // 2, (k % 2) * MEM:(k % 2 + 1) * MEM], ACT.Copy,
                                   scale=m.gain[:, G_MEM * KD + k:G_MEM * KD + k + 1]).then_inc(gained, 1)
                for h in range(MH):
                    act.wait_ge(kt_done, 1)
                    act.activation(kt[:, h, :], m.ps[:, h // 2, (h % 2) * MEM:(h % 2 + 1) * MEM], ACT.Copy)

            @block.vector
            def _(dve):
                order = Count(dve, own)
                dve.wait_ge(squared, MT)
                order.then_wait(dve.tensor_scalar(stat[:, :], stat[:, :], 1.0 / D, EPS, ALU.mult, ALU.add))
                dve.wait_ge(rooted, 1)
                order.then_wait(dve.reciprocal(stat[:, :], stat[:, :]))
                for t in range(MT):
                    dve.tensor_scalar(tok[:, t, :], tok[:, t, :], stat[:, t:t + 1], None, ALU.mult).then_inc(normed, 1)
                for n in range(2 * MT):
                    half, t = divmod(n, MT)
                    dve.wait_ge(done, n + 1)
                    dve.tensor_copy(kv[:, t, half * 512:(half + 1) * 512], m.ps[:, 4 + n, :]).then_inc(taken, 1)

            @block.tensor
            def _(pe):
                pe.wait_ge(normed, MT)
                for k in range(KD):
                    for t in range(MT):
                        last = pe.transpose(m.ps[:, k // 2, (k % 2) * MEM + t * P:(k % 2) * MEM + (t + 1) * P],
                                            tok[:, t, k * P:(k + 1) * P], m.ident[:, :])
                    if k % 2:
                        last.then_inc(turned, 1)
                pe.wait_ge(gained, KD)
                for half in range(2):
                    pe.wait_ge(w_arrived, 16 * (half + 1))
                    for t in range(MT):
                        for k in range(KD):
                            last = pe.matmul(m.ps[:, 4 + half * MT + t, :], turned_m[:, k, t * P:(t + 1) * P], w[:, k, :],
                                             start=k == 0, stop=k == KD - 1)
                        last.then_inc(done, 1)
                pe.wait_ge(taken, MT)
                for h in range(MH):
                    for t in range(MT):
                        last = pe.transpose(m.ps[:, h // 2, (h % 2) * MEM + t * P:(h % 2) * MEM + (t + 1) * P],
                                            kv[:, t, h * P:(h + 1) * P], m.ident[:, :])
                last.then_inc(kt_done, 1)

        q = st.sbuf("q", [P, MH, T])
        with Stage(nc, "qm") as pt:
            proj = Product(pt, m, w_in, lambda i: i * (2 * P) + QM_COL, MH // 2, then)
            block = pt.block()

            def take(dve, i, t, c, src):
                return scaled(dve, m, c, q[:, bass.ds(i * 2 + t, 1), chunk(c)].rearrange("p a t -> p (a t)"), src)

            @block.sync
            def _(sp):
                proj.load(sp)

            @block.tensor
            def _(pe):
                proj.tensor(pe)

            @block.scalar
            def _(act):
                proj.scalar(act)

            @block.vector
            def _(dve):
                proj.vector(dve, take)
            proj.close()

        prob = st.sbuf("prob", [P, 2, MH, MEM])
        turned_p = st.sbuf("turned_p", [P, 2, MT, MH, P])
        stat = st.sbuf("stat", [P, 2, 4, MH])
        scored = st.sem("scored")
        own = st.sem("own")
        negated = st.sem("negated")
        exped = st.sem("exped")
        normal = st.sem("normal")
        p_turned = st.sem("p_turned")
        p_taken_act = st.sem("p_taken_act")
        p_taken_dve = st.sem("p_taken_dve")
        weighed = st.sem("weighed")
        res_taken = st.sem("res_taken")
        stored = st.sem("stored")
        sampled = st.sem("sampled")
        block = st.block()

        @block.sync
        def _(sp):
            for b in range(TB):
                sp.wait_ge(res_taken, b + 1)
                sp.dma_start(m.mem_out[:, :, b * P:(b + 1) * P], q[:, :, b * P:(b + 1) * P]).then_inc(stored, 16)
            sp.wait_ge(stored, 16 * TB)

        @block.tensor
        def _(pe):
            def scores(b):
                if b >= 2:
                    pe.wait_ge(exped, MH * (b - 1))
                for h in range(MH):
                    last = pe.matmul(m.ps[:, 2 * (b % 2) + h // 2, (h % 2) * MEM:(h % 2 + 1) * MEM],
                                     q[:, h, b * P:(b + 1) * P], kt[:, h, :], start=True, stop=True)
                last.then_inc(scored, 1)

            def turn(b):
                pe.wait_ge(normal, b + 1)
                if b >= 1:
                    pe.wait_ge(p_taken_act, b)
                    pe.wait_ge(p_taken_dve, b)
                for t in range(MT):
                    for h in range(MH):
                        last = pe.transpose(m.ps[:, 4 + t, h * P:(h + 1) * P], prob[:, b % 2, h, t * P:(t + 1) * P],
                                            m.ident[:, :])
                last.then_inc(p_turned, 1)

            def weigh(b):
                pe.wait_ge(p_taken_act, b + 1)
                pe.wait_ge(p_taken_dve, b + 1)
                if b >= 2:
                    pe.wait_ge(res_taken, b - 1)
                for h in range(MH):
                    for t in range(MT):
                        last = pe.matmul(m.ps[:, 6 + b % 2, h * P:(h + 1) * P], kv[:, t, MEM_W + h * P:MEM_W + (h + 1) * P],
                                         turned_p[:, b % 2, t, h, :], start=t == 0, stop=t == MT - 1)
                last.then_inc(weighed, 1)

            scores(0)
            scores(1)
            for b in range(TB):
                turn(b)
                if b + 2 < TB:
                    scores(b + 2)
                weigh(b)

        @block.scalar
        def _(act):
            act.activation(m.s_qm[:, :, :], q[:, :, SEQ:T], ACT.Copy).then_inc(sampled, 1)

            def exps(b):
                act.wait_ge(negated, b + 1)
                if b >= 2:
                    act.wait_ge(p_turned, b - 1)
                for h in range(MH):
                    act.activation(prob[:, b % 2, h, :], m.ps[:, 2 * (b % 2) + h // 2, (h % 2) * MEM:(h % 2 + 1) * MEM],
                                   ACT.Exp, bias=stat[:, b % 2, 1, h:h + 1], scale=scale,
                                   accum_out=stat[:, b % 2, 2, h:h + 1]).then_inc(exped, 1)

            def result(b):
                act.wait_ge(weighed, b + 1)
                act.activation(q[:, :, b * P:(b + 1) * P], m.ps[:, 6 + b % 2, :].rearrange("p (h q) -> p h q", h=MH),
                               ACT.Copy).then_inc(res_taken, 1)

            exps(0)
            for b in range(TB):
                if b + 1 < TB:
                    exps(b + 1)
                act.wait_ge(p_turned, b + 1)
                if b >= 2:
                    act.wait_ge(weighed, b - 1)
                act.activation(turned_p[:, b % 2, 1, :, :], m.ps[:, 5, :].rearrange("p (h q) -> p h q", h=MH),
                               ACT.Copy).then_inc(p_taken_act, 1)
                if b >= 1:
                    result(b - 1)
            result(TB - 1)

        @block.vector
        def _(dve):
            order = Count(dve, own)

            def top(b):
                dve.wait_ge(scored, b + 1)
                if b >= 2:
                    dve.wait_ge(normal, b - 1)
                src = m.ps[:, 2 * (b % 2):2 * (b % 2) + 2, :].rearrange("p a (i k) -> p (a i) k", k=MEM)
                order.then_wait(dve.tensor_reduce(stat[:, b % 2, 0, :], src, AX_X, ALU.max))
                dve.tensor_scalar(stat[:, b % 2, 1, :], stat[:, b % 2, 0, :], -scale, None, ALU.mult).then_inc(negated, 1)

            def normalise(b):
                dve.wait_ge(exped, MH * (b + 1))
                order.then_wait(dve.reciprocal(stat[:, b % 2, 3, :], stat[:, b % 2, 2, :]))
                dve.tensor_tensor(prob[:, b % 2, :, :], prob[:, b % 2, :, :],
                                  stat[:, b % 2, 3, :].unsqueeze(2).to_broadcast([P, MH, MEM]), ALU.mult).then_inc(normal, 1)

            top(0)
            for b in range(TB):
                normalise(b)
                if b + 1 < TB:
                    top(b + 1)
                dve.wait_ge(p_turned, b + 1)
                if b >= 2:
                    dve.wait_ge(weighed, b - 1)
                dve.tensor_copy(turned_p[:, b % 2, 0, :, :], m.ps[:, 4, :].rearrange("p (h q) -> p h q", h=MH)
                                ).then_inc(p_taken_dve, 1)


def sample_memory(nc, m, cache):
    MT = MEM // P
    rows = NS * MH
    scale = P ** -0.5
    with Stage(nc, "smem") as st:
        keys = st.sbuf("keys", [P, 2, MT, MEM_W])
        vals = st.sbuf("vals", [P, 4, MT, MEM_W])
        tok = st.sbuf("tok", [NS, MEM_W])
        sel = st.sbuf("sel", [NS, NS, P])
        prod = st.sbuf("prod", [P, MT, MEM_W])
        score = st.sbuf("score", [P, MT, NS, MH])
        prob = st.sbuf("prob", [rows, MT, P])
        small = st.sbuf("small", [rows, 4])
        p_cols = st.sbuf("p_cols", [P, MT, rows])
        sel_in = st.sem("sel_in")
        key_in = [st.sem(f"key_in{i}") for i in range(2)]
        val_in = [st.sem(f"val_in{i}") for i in range(4)]
        tok_done = st.sem("tok_done")
        tok_taken = st.sem("tok_taken")
        spread = st.sem("spread")
        multiplied = st.sem("multiplied")
        scored = st.sem("scored")
        rowed = st.sem("rowed")
        own = st.sem("own")
        maxed = st.sem("maxed")
        exped = st.sem("exped")
        normal = st.sem("normal")
        coled = st.sem("coled")
        cols_taken = st.sem("cols_taken")
        weighed = st.sem("weighed")
        block = st.block()
        c_v = cache.rearrange("a n (t p) c h e -> p (a n) t c (h e)", p=P)

        @block.sync
        def _(sp):
            sp.dma_start(sel[:, :, :], m.sel_in).then_inc(sel_in, 16)
            for n in range(NS):
                if n >= 2:
                    sp.wait_ge(multiplied, n - 1)
                sp.dma_start(keys[:, n % 2, :, :], c_v[:, n, :, 0, :]).then_inc(key_in[n % 2], 16)
                if n < 4:
                    sp.dma_start(vals[:, n, :, :], c_v[:, n, :, 1, :]).then_inc(val_in[n], 16)
            for n in range(4, NS):
                sp.wait_ge(weighed, n - 3)
                sp.dma_start(vals[:, n % 4, :, :], c_v[:, n, :, 1, :]).then_inc(val_in[n % 4], 16)

        @block.tensor
        def _(pe):
            for h in range(MH):
                last = pe.transpose(m.ps[0:NS, 0, h * P:(h + 1) * P], m.s_qm[:, h, :], m.ident[:, :])
            last.then_inc(tok_done, 1)
            pe.wait_ge(tok_taken, 1)
            pe.wait_ge(sel_in, 16)
            for n in range(NS):
                if n >= 2:
                    pe.wait_ge(multiplied, n - 1)
                pe.matmul(m.ps[:, 1 + n % 2, :], sel[:, n, :], tok[:, :], start=True, stop=True).then_inc(spread, 1)
            pe.wait_ge(scored, NS)
            for t in range(MT):
                last = pe.transpose(m.ps[0:rows, 3, t * P:(t + 1) * P], score[:, t, :, :].rearrange("p n h -> p (n h)"),
                                    m.ident[:, :])
            last.then_inc(rowed, 1)
            pe.wait_ge(normal, 1)
            for t in range(MT):
                last = pe.transpose(m.ps[:, 4, t * rows:(t + 1) * rows], prob[:, t, :], m.ident[0:rows, 0:rows])
            last.then_inc(coled, 1)
            pe.wait_ge(cols_taken, 1)
            for n in range(NS):
                pe.wait_ge(val_in[n % 4], 16 * (n // 4 + 1))
                for h in range(MH):
                    col = n * MH + h
                    for t in range(MT):
                        last = pe.matmul(m.ps[:, 5, col:col + 1], vals[:, n % 4, t, h * P:(h + 1) * P],
                                         p_cols[:, t, col:col + 1], start=t == 0, stop=t == MT - 1)
                last.then_inc(weighed, 1)

        @block.vector
        def _(dve):
            order = Count(dve, own)
            dve.wait_ge(tok_done, 1)
            dve.tensor_copy(tok[:, :], m.ps[0:NS, 0, :]).then_inc(tok_taken, 1)
            for n in range(NS):
                dve.wait_ge(spread, n + 1)
                dve.wait_ge(key_in[n % 2], 16 * (n // 2 + 1))
                if n:
                    dve.wait_ge(scored, n)
                dve.tensor_tensor(prod[:, :, :], keys[:, n % 2, :, :],
                                  m.ps[:, 1 + n % 2, :].unsqueeze(1).to_broadcast([P, MT, MEM_W]),
                                  ALU.mult).then_inc(multiplied, 1)
                dve.wait_ge(multiplied, n + 1)
                dve.tensor_reduce(score[:, :, n, :], prod[:, :, :].rearrange("p t (h d) -> p t h d", h=MH), AX_X,
                                  ALU.add).then_inc(scored, 1)
            dve.wait_ge(rowed, 1)
            flat = prob[:, :, :].rearrange("p t r -> p (t r)")
            order.then_wait(dve.tensor_copy(flat, m.ps[0:rows, 3, 0:MEM]))
            order.then_wait(dve.tensor_reduce(small[:, 0:1], flat, AX_X, ALU.max))
            dve.tensor_scalar(small[:, 1:2], small[:, 0:1], -scale, None, ALU.mult).then_inc(maxed, 1)
            dve.wait_ge(exped, 1)
            order.then_wait(dve.reciprocal(small[:, 3:4], small[:, 2:3]))
            dve.tensor_scalar(flat, flat, small[:, 3:4], None, ALU.mult).then_inc(normal, 1)
            dve.wait_ge(coled, 1)
            dve.tensor_copy(p_cols[:, :, :], m.ps[:, 4, 0:MT * rows].rearrange("p (t r) -> p t r", t=MT)
                            ).then_inc(cols_taken, 1)
            dve.wait_ge(weighed, NS)
            dve.tensor_copy(m.s_mem[:, :, :], m.ps[:, 5, 0:rows].rearrange("p (n h) -> p h n", h=MH))

        @block.scalar
        def _(act):
            act.wait_ge(maxed, 1)
            flat = prob[:, :, :].rearrange("p t r -> p (t r)")
            act.activation(flat, flat, ACT.Exp, bias=small[:, 1:2], scale=scale, accum_out=small[:, 2:3]).then_inc(exped, 1)


class Memory:
    pass


def decoder_step(nc, i, o):
    SEMS.clear()
    m = Memory()
    with ExitStack() as ctx:
        def sb(name, shape, dt=F32):
            return ctx.enter_context(nc.sbuf_tensor(name, shape, dt))

        m.x = sb("x", [P, KD, T])
        m.uh = sb("uh", [P, KD, T], F32R)
        m.ul = sb("ul", [P, KD, T], F32R)
        m.rstd = sb("rstd", [P, T])
        m.ident = sb("ident", [P, P])
        m.mean = sb("mean", [P, P])
        m.eps = sb("eps", [P, 1])
        m.gain = sb("gain", [P, GAIN_ROWS + NPOOL])
        m.cache_bias = sb("cache_bias", [P, NG, HG])
        m.new_bias = sb("new_bias", [NS, NG * HG])
        m.s_qkv = sb("s_qkv", [P, 6 * NG, NS])
        m.s_att = sb("s_att", [P, 2, NS])
        m.s_mem = sb("s_mem", [P, MH, NS])
        m.s_qm = sb("s_qm", [P, MH, NS])
        m.stream = Stream(nc, ctx)
        m.ps = ctx.enter_context(nc.psum_tensor("ps", [P, 8, 512], F32))
        m.bias_rows = nc.dram_tensor("bias_rows", (NG, NG * HG, 384), F32).ap()
        m.group_out = nc.dram_tensor("group_out", (SEQ, NG, RES), F32).ap()
        m.mem_out = nc.dram_tensor("mem_out", (P, MH, SEQ), F32).ap()
        m.new_scores = nc.dram_tensor("new_scores", (NS, HG, NG), F32).ap()
        m.sel_in, m.own_in, m.inv_in = i["const_sel"], i["const_own"], i["const_inv"]

        gains = [i[n] for n in ("g_ffn1", "g_mix", "g_mem", "g_ffn2", "g_final")]
        w_in = i["w_in"].rearrange("a (k p) f -> p (a k) f", p=P)
        w_out = i["w_out"].rearrange("a (k p) f -> p (a k) f", p=P)
        w_o = [i[n].rearrange("a (k p) f -> p (a k) f", p=P) for n in ("w_oa", "w_ob", "w_oc")]

        def gates(branch):
            return w_in, GATE_COL + branch * D

        w_gate1, w_gate2 = (i[n].rearrange("a (k p) f -> p (a k) f", p=P) for n in ("w1_gate", "w2_gate"))
        load_tokens(nc, m, i, gains, (w_gate1, 0))
        ffn(nc, m, "ffn1", i["w1_gate"], i["w1_up"], i["w1_down"], G_MIX, (w_in, 0))
        for g in range(NG):
            attention(nc, m, g, w_in, o[f"new_win{g}_kv_prompt"], (w_in, (g + 1) * GW if g + 1 < NG else Z_COL))
        clear_semaphores(nc)
        with ExitStack() as mix:
            with Stage(nc, "b") as b:
                with ExitStack() as pool:
                    z = pool.enter_context(nc.sbuf_tensor("z", [P, NPOOL, PAD + T], F32, side="right"))
                    pool_values(nc, m, z, w_in, gates(1), [i[f"cache_win{g}_kv"] for g in range(NG)],
                                [o[f"new_win{g}_kv_sample"] for g in range(NG)])
                    bh, bl = (b.sbuf(n, [P, NPOOL, T], F32R) for n in ("high", "low"))
                    pooling(nc, m, z, i["state_pool"], i["w_pool"], o["new_pool_prompt"], o["new_pool_sample"], bh, bl)
                m.mix = mix.enter_context(nc.sbuf_tensor("mix", [P, KD, T], F32, side="right"))
                merge(nc, m, "merge_b", 1, True, w_in, w_o[1], bh, bl, NPOOL, gates(0))
            with Stage(nc, "a") as a:
                ah, al = (a.sbuf(n, [P, 2, T], F32R) for n in ("high", "low"))
                combine(nc, m, ah, al)
                merge(nc, m, "merge_a", 0, False, w_in, w_o[0], ah, al, 2, (w_in, QM_COL))
            memory_attention(nc, m, w_in, i["mem_prompt"], i["w_mem_kv"], o["new_mem_kv_prompt"], gates(2))
            sample_memory(nc, m, i["cache_mem_kv"])
            with Stage(nc, "c") as c:
                ch, cl = (c.sbuf(n, [P, MH, T], F32R) for n in ("high", "low"))
                merge(nc, m, "merge_c", 2, False, w_in, w_o[2], ch, cl, MH, (w_out, 0), late=(m.mem_out, m.s_mem[:, :, :]))
            mix_out(nc, m, w_out, G_FFN2, (w_gate2, 0))
        clear_semaphores(nc)
        ffn(nc, m, "ffn2", i["w2_gate"], i["w2_up"], i["w2_down"], None, None)
        final(nc, m, i["g_final"], o["y_prompt"], o["y_sample"])



N_BUCKETS = 32
MAX_DISTANCE = 2048


def rel_bucket(n):
    exact = N_BUCKETS // 2
    if n < exact:
        return n
    return min(exact + int(np.log(n / exact) / np.log(MAX_DISTANCE / exact) * (N_BUCKETS - exact)), N_BUCKETS - 1)


def constants():
    onehot = np.zeros((N_BUCKETS, 2, NG, REACH + 1), np.float32)
    for g, (_, dil) in enumerate(GROUPS):
        for r in range(REACH + 1):
            onehot[rel_bucket((REACH - r) * dil), 0, g, r] = 1.0
            onehot[rel_bucket(r * dil), 1, g, r] = 1.0
    sel = np.zeros((NS, NS, P), np.float32)
    own = np.zeros((NS * HG, NS), np.float32)
    for n in range(NS):
        sel[n, n, :] = 1.0
        own[n * HG:(n + 1) * HG, n] = 1.0
    inv = np.zeros((P, NPOOL, PAD), np.float32)
    for k, window in enumerate(POOL_WINDOWS):
        inv[:, k, :] = 1.0 / np.minimum(window, np.arange(PAD) + 1)
    return {"const_ident": np.eye(P, dtype=np.float32), "const_onehot": onehot, "const_sel": sel, "const_own": own,
            "const_inv": inv}



_OUTS = [("y_prompt", (1, SEQ, D)), ("y_sample", (NS, 1, D)), ("new_win0_kv_prompt", (1, 1, 128, 2, HG, DH)),
         ("new_win1_kv_prompt", (1, 1, 512, 2, HG, DH)), ("new_win2_kv_prompt", (1, 1, SEQ, 2, HG, DH)),
         ("new_pool_prompt", (1, 1, HIST, POOL_W)), ("new_mem_kv_prompt", (1, 1, MEM, 2, MH, P)),
         ("new_win0_kv_sample", (1, NS, 1, 2, HG, DH)), ("new_win1_kv_sample", (1, NS, 1, 2, HG, DH)),
         ("new_win2_kv_sample", (1, NS, 1, 2, HG, DH)), ("new_pool_sample", (1, NS, 1, POOL_W))]


def kernel(**inputs):
    import concourse.bacc as bacc
    from concourse.bass_utils import run_bass_kernel_spmd as run

    nc = bacc.Bacc("TRN2", target_bir_lowering=False, num_devices=1)
    arrays = {name: np.ascontiguousarray(a) for name, a in inputs.items()} | constants()
    i = {name: nc.dram_tensor(f"in_{name}", a.shape, mybir.dt.from_np(a.dtype), kind="ExternalInput").ap()
         for name, a in arrays.items()}
    o = {name: nc.dram_tensor(f"out_{name}", shape, F32, kind="ExternalOutput").ap() for name, shape in _OUTS}
    decoder_step(nc, i, o)
    r = run(nc, [{f"in_{name}": a for name, a in arrays.items()}], core_ids=[0])
    return tuple(r.results[0][f"out_{name}"] for name, _ in _OUTS)
```

```python
from contextlib import ExitStack

import numpy as np

import concourse.bass as bass
from concourse import mybir

F32 = mybir.dt.float32
F32R = mybir.dt.float32r
ALU = mybir.AluOpType
ACT = mybir.ActivationFunctionType
AX_X = mybir.AxisListType.X

P = 128
D = 1024
SEQ = 1024
NS = 8
T = SEQ + NS
KD = D // P
CHUNKS = ((0, 352), (352, 352), (704, 328))
NCH = len(CHUNKS)
CH = CHUNKS[0][1]
TB = SEQ // P
F = 2816
EPS = 1e-6
G_FFN1, G_MIX, G_MEM, G_FFN2, G_FINAL = range(5)
GAIN_ROWS = 5 * KD
NPOOL = 4


class Count:

    def __init__(self, eng, sem, base=0):
        self.eng, self.sem, self.base, self.n = eng, sem, base, 0

    def then_wait(self, ins):
        self.n += 1
        ins.then_inc(self.sem, 1)
        self.eng.wait_ge(self.sem, self.base + self.n)


SEMS = []


def clear_semaphores(nc):
    nc.clear_and_free_semaphores(SEMS)
    SEMS.clear()
    nc.all_engine_barrier()


class Stage:

    def __init__(self, nc, name):
        self.nc, self.name, self.ctx = nc, name, ExitStack()

    def __enter__(self):
        return self

    def __exit__(self, *e):
        return self.ctx.__exit__(*e)

    def sbuf(self, name, shape, dt=F32):
        return self.ctx.enter_context(self.nc.sbuf_tensor(f"{self.name}_{name}", shape, dt))

    def sem(self, name):
        sem = self.nc.alloc_semaphore(f"{self.name}_{name}")
        SEMS.append(sem)
        return sem

    def block(self):
        return self.ctx.enter_context(self.nc.Block())


def chunk(c):
    return slice(CHUNKS[c][0], CHUNKS[c][0] + CHUNKS[c][1])


def width(c):
    return slice(0, CHUNKS[c][1])


class Stream:

    def __init__(self, nc, ctx):
        self.raw = ctx.enter_context(nc.sbuf_tensor("stream_raw", [P, KD, 2 * P], F32))
        self.high, self.low = ([ctx.enter_context(nc.sbuf_tensor(f"stream_{part}{t}", [P, KD, P], F32R))
                                for t in range(2)] for part in ("high", "low"))
        self.arrived = nc.alloc_semaphore("stream_arrived")
        self.rounded = nc.alloc_semaphore("stream_rounded")
        self.split = nc.alloc_semaphore("stream_split")
        self.base = 0

    def load(self, sp, n, w, col, i=None):
        if not isinstance(n, int) or n > 0:
            sp.wait_ge(self.split, 2 * n)
        first = col if i is None else col(i)
        sp.dma_start(self.raw[:, :, :], w[:, :, bass.ds(first, 2 * P)]).then_inc(self.arrived, 16)

    def load_all(self, sp, pairs, w, cols, then):
        with sp.Fori(1, pairs) as i:
            self.load(sp, self.base + i, w, cols, i)
        if then is not None:
            self.load(sp, self.base + pairs, *then)

    def split_high(self, act, n, t):
        act.wait_ge(self.arrived, 16 * (n + 1))
        act.activation(self.high[t][:, :, :], self.raw[:, :, t * P:(t + 1) * P], ACT.Copy).then_inc(self.rounded, 1)

    def split_low(self, dve, n, t):
        dve.wait_ge(self.rounded, n * 2 + (t + 1))
        dve.tensor_tensor(self.low[t][:, :, :], self.raw[:, :, t * P:(t + 1) * P], self.high[t][:, :, :].bitcast(F32),
                          ALU.subtract).then_inc(self.split, 1)


class Parts:

    def __init__(self, st, m, which):
        self.m, self.which = m, which
        self.high = st.sem("part_high")

    def gain(self, k):
        return self.m.gain[:, self.which * KD + k:self.which * KD + k + 1]

    def scalar_high(self, act, k, c):
        act.activation(self.m.uh[:, k, chunk(c)], self.m.x[:, k, chunk(c)], ACT.Copy,
                       scale=self.gain(k)).then_inc(self.high, 1)

    def vector_low(self, dve, count, k, c):
        dve.wait_ge(self.high, count)
        dve.scalar_tensor_tensor(self.m.ul[:, k, chunk(c)], self.m.x[:, k, chunk(c)], self.gain(k),
                                 self.m.uh[:, k, chunk(c)].bitcast(F32), ALU.mult, ALU.subtract)


def load_tokens(nc, m, i, gains, first):
    with Stage(nc, "load") as st:
        tok = st.sbuf("tok", [P, TB + 1, D])
        junk = st.sbuf("junk", [P, 2, D])
        stat = st.sbuf("stat", [P, 3, TB + 1])
        diag = st.sbuf("diag", [P, 2, P])
        grow = st.sbuf("grow", [GAIN_ROWS + NPOOL, P])
        rel = st.sbuf("rel", [32, NG * HG])
        hot = st.sbuf("hot", [32, 2, NG, REACH + 1])
        rows = st.sbuf("table", [NG * HG, NG, 384])
        parts = Parts(st, m, G_FFN1)
        tok_in = [st.sem(f"tok_in{b}") for b in range(TB + 1)]
        small_in = st.sem("small_in")
        hot_in = st.sem("hot_in")
        small_turned = st.sem("small_turned")
        small_taken = st.sem("small_taken")
        turned = st.sem("turned")
        taken = st.sem("taken")
        ones_set = st.sem("ones_set")
        squared = st.sem("squared")
        shifted = st.sem("shifted")
        rooted = st.sem("rooted")
        inverted = st.sem("inverted")
        diag_made = st.sem("diag_made")
        spread = st.sem("spread")
        bias_made = st.sem("bias_made")
        bias_taken = st.sem("bias_taken")
        stored = st.sem("stored")
        block = st.block()
        xp = i["x_prompt"].rearrange("a (b p) d -> p (a b) d", p=P)
        order_b = [TB] + list(range(TB))

        def size(b):
            return P if b < TB else NS

        @block.sync
        def _(sp):
            sp.dma_start(m.ident[:, :], i["const_ident"]).then_inc(small_in, 16)
            for n, g in enumerate(gains):
                src = g.rearrange("a (k p) -> (a k) p", p=P) if len(g.shape) == 2 else g.rearrange("(k p) -> k p", p=P)
                sp.dma_start(grow[n * KD:(n + 1) * KD, :], src).then_inc(small_in, 16)
            sp.dma_start(grow[GAIN_ROWS:, :], i["pool_scale"].rearrange("a (k p) -> (a k) p", p=P)).then_inc(small_in, 16)
            sp.dma_start(tok[0:NS, TB, :], i["x_sample"].rearrange("n a d -> (n a) d")).then_inc(tok_in[TB], 16)
            for b in range(TB):
                sp.dma_start(tok[:, b, :], xp[:, b, :]).then_inc(tok_in[b], 16)
            sp.dma_start(rel[:, :], i["rel_bias"]).then_inc(hot_in, 16)
            sp.dma_start(hot[:, :, :, :], i["const_onehot"]).then_inc(hot_in, 16)
            m.stream.load(sp, 0, *first)
            sp.wait_ge(bias_taken, 1)
            sp.dma_start(m.bias_rows.rearrange("g h y -> h g y"), rows[:, :, :]).then_inc(stored, 16)
            sp.wait_ge(stored, 16)

        @block.tensor
        def _(pe):
            def spread_rstd(s):
                b = order_b[s]
                pe.wait_ge(diag_made, s + 1)
                bank, at = (5 + b // 4, b % 4 * P) if b < TB else (0, 128)
                pe.matmul(m.ps[:, bank, at:at + size(b)], m.mean[0:size(b), :], diag[0:size(b), s % 2, 0:size(b)],
                          start=True, stop=True).then_inc(spread, 1)

            pe.wait_ge(small_in, 16 * (len(gains) + 2))
            pe.transpose(m.ps[:, 0, 0:GAIN_ROWS + NPOOL], grow[:, :], m.ident[0:GAIN_ROWS + NPOOL, 0:GAIN_ROWS + NPOOL])
            pe.wait_ge(tok_in[TB], 16)
            for k in range(KD):
                last = pe.transpose(m.ps[:, 0, 64 + NS * k:64 + NS * (k + 1)], tok[0:NS, TB, k * P:(k + 1) * P],
                                    m.ident[0:NS, 0:NS])
            last.then_inc(small_turned, 1)
            pe.wait_ge(ones_set, 1)
            for n in range(2 * TB):
                b, half = divmod(n, 2)
                if half == 0:
                    pe.wait_ge(tok_in[b], 16)
                if n >= 4:
                    pe.wait_ge(taken, n - 3)
                for k in range(4):
                    kk = 4 * half + k
                    last = pe.transpose(m.ps[:, 1 + n % 4, k * P:(k + 1) * P], tok[:, b, kk * P:(kk + 1) * P],
                                        m.ident[:, :])
                last.then_inc(turned, 1)
                if half == 1:
                    spread_rstd(b)
            pe.wait_ge(hot_in, 32)
            pe.matmul(m.ps[0:NG * HG, 7, 0:NG * (REACH + 1)], rel[:, :], hot[:, 1, :, :].rearrange("p g r -> p (g r)"),
                      start=True, stop=True)
            for g in range(NG):
                pe.matmul(m.ps[:, 7, 400 + 16 * g:400 + 16 * g + NG * HG], hot[:, 0, g, 0:REACH], rel[:, :], start=True,
                          stop=True)
            pe.matmul(m.ps[0:NS, 7, 448:448 + NG * HG], hot[:, 0, 0, REACH:REACH + 1].to_broadcast([32, NS]), rel[:, :],
                      start=True, stop=True).then_inc(bias_made, 1)
            spread_rstd(TB)

        @block.scalar
        def _(act):
            def square(s):
                b = order_b[s]
                act.wait_ge(tok_in[b], 16)
                if s >= 2:
                    act.wait_ge(squared, s - 1)
                act.activation(junk[0:size(b), s % 2, :], tok[0:size(b), b, :], ACT.Square,
                               accum_out=stat[0:size(b), 0, b:b + 1]).then_inc(squared, 1)

            def root(s):
                b = order_b[s]
                act.wait_ge(shifted, s + 1)
                act.activation(stat[0:size(b), 1, b:b + 1], stat[0:size(b), 1, b:b + 1], ACT.Sqrt).then_inc(rooted, 1)

            def high(c, blocks):
                act.wait_ge(taken, 2 * blocks)
                for k in range(KD):
                    parts.scalar_high(act, k, c)

            square(0)
            for b in range(TB):
                square(b + 1)
                root(b)
                if b == 3:
                    act.wait_ge(small_taken, 2)
                    high(0, 3)
                if b == 6:
                    high(1, 6)
                    act.wait_ge(spread, 5)
                    act.activation(m.rstd[:, 0:512], m.ps[:, 5, :], ACT.Copy)
            root(TB)
            high(2, TB)
            for t in range(2):
                m.stream.split_high(act, 0, t)
            act.wait_ge(spread, TB + 1)
            act.activation(m.rstd[:, 512:SEQ], m.ps[:, 6, :], ACT.Copy)
            act.activation(m.rstd[:, SEQ:T], m.ps[:, 0, 128:128 + NS], ACT.Copy)

        @block.vector
        def _(dve):
            def shift(s):
                b = order_b[s]
                dve.wait_ge(squared, s + 1)
                dve.tensor_scalar(stat[0:size(b), 1, b:b + 1], stat[0:size(b), 0, b:b + 1], 1.0 / D, EPS, ALU.mult,
                                  ALU.add).then_inc(shifted, 1)

            def diagonal(s):
                b = order_b[s]
                dve.wait_ge(rooted, s + 1)
                dve.reciprocal(stat[0:size(b), 2, b:b + 1], stat[0:size(b), 1, b:b + 1]).then_inc(inverted, 1)
                dve.wait_ge(inverted, s + 1)
                if s >= 2:
                    dve.wait_ge(spread, s - 1)
                dve.tensor_scalar(diag[0:size(b), s % 2, 0:size(b)], m.ident[0:size(b), 0:size(b)],
                                  stat[0:size(b), 2, b:b + 1], float(D), ALU.mult, ALU.mult).then_inc(diag_made, 1)

            def low(c):
                for k in range(KD):
                    parts.vector_low(dve, KD * c + k + 1, k, c)

            dve.memset(m.eps[:, :], EPS)
            dve.memset(m.mean[:, :], 1.0 / D).then_inc(ones_set, 1)
            dve.memset(rows[:, :, :], NEG).then_inc(ones_set, 1)
            dve.wait_ge(small_turned, 1)
            dve.tensor_copy(m.gain[:, :], m.ps[:, 0, 0:GAIN_ROWS + NPOOL]).then_inc(small_taken, 1)
            dve.tensor_copy(m.x[:, :, SEQ:T], m.ps[:, 0, 64:128].rearrange("p (k n) -> p k n", k=KD)).then_inc(small_taken, 1)
            shift(0)
            dve.wait_ge(small_taken, 2)
            for b in range(TB):
                diagonal(b)
                for half in range(2):
                    n = 2 * b + half
                    dve.wait_ge(turned, n + 1)
                    dve.tensor_copy(m.x[:, 4 * half:4 * half + 4, b * P:(b + 1) * P],
                                    m.ps[:, 1 + n % 4, :].rearrange("p (k t) -> p k t", k=4)).then_inc(taken, 1)
                shift(b + 1)
                if b == 4:
                    low(0)
            diagonal(TB)
            low(1)
            low(2)
            for t in range(2):
                m.stream.split_low(dve, 0, t)
            dve.wait_ge(bias_made, 1)
            dve.wait_ge(ones_set, 2)
            dve.tensor_copy(rows[:, :, 127:127 + REACH + 1],
                            m.ps[0:NG * HG, 7, 0:NG * (REACH + 1)].rearrange("h (g r) -> h g r", g=NG)).then_inc(bias_taken, 1)
            for g in range(NG):
                dve.tensor_copy(m.cache_bias[:, g, :], m.ps[:, 7, 400 + 16 * g + HG * g:400 + 16 * g + HG * g + HG])
            dve.tensor_copy(m.new_bias[:, :], m.ps[0:NS, 7, 448:448 + NG * HG])


class Norm:

    def __init__(self, st, m, which, banks):
        self.m, self.banks = m, banks
        self.parts = Parts(st, m, which)
        self.sq = st.sbuf("sq", [P, 2, CH])
        self.ssum = st.sbuf("ssum", [P, T])
        self.squared = st.sem("squared")
        self.summed = st.sem("summed")
        self.meaned = st.sem("meaned")
        self.rooted = st.sem("rooted")
        self.inverted = st.sem("inverted")

    def vector_clear(self, dve):
        dve.memset(self.ssum[:, :], 0.0).then_inc(self.summed, 2)

    def scalar_square(self, act, count, parity, x, c):
        act.wait_ge(self.summed, count + 1)
        act.activation(self.sq[:, parity, width(c)], x, ACT.Square).then_inc(self.squared, 1)

    def vector_sum(self, dve, count, parity, c):
        dve.wait_ge(self.squared, count + 1)
        dve.wait_ge(self.summed, count + 2)
        dve.tensor_tensor(self.ssum[:, chunk(c)], self.ssum[:, chunk(c)], self.sq[:, parity, width(c)],
                          ALU.add).then_inc(self.summed, 1)

    def tensor_mean(self, pe, c, count):
        pe.wait_ge(self.summed, count + 2)
        if self.banks[c] in self.banks[:c]:
            pe.wait_ge(self.rooted, c)
        pe.matmul(self.m.ps[:, self.banks[c], width(c)], self.m.mean[:, :], self.ssum[:, chunk(c)],
                  start=True, stop=True).then_inc(self.meaned, 1)

    def scalar_root(self, act, c):
        act.wait_ge(self.meaned, c + 1)
        act.activation(self.m.rstd[:, chunk(c)], self.m.ps[:, self.banks[c], width(c)], ACT.Sqrt,
                       bias=self.m.eps[:, :]).then_inc(self.rooted, 1)

    def vector_invert(self, dve, c):
        dve.wait_ge(self.rooted, c + 1)
        dve.reciprocal(self.m.rstd[:, chunk(c)], self.m.rstd[:, chunk(c)]).then_inc(self.inverted, 1)


FT = F // P
PAIRS = FT // 2
GU_UNITS = 2 * NCH
DOWN_UNITS = NCH * KD


def product(pe, out, w_high, w_low, a_high, a_low, first, last):
    pe.matmul(out, w_high, a_high, start=first, stop=False)
    pe.matmul(out, w_low, a_high, start=False, stop=False)
    return pe.matmul(out, w_high, a_low, start=False, stop=last)


def ffn(nc, m, name, w_gate, w_up, w_down, next_norm, then):
    with Stage(nc, name) as st:
        raw_up = st.sbuf("raw_up", [P, KD, 2 * P])
        up_h = [st.sbuf(f"up_h{t}", [P, KD, P], F32R) for t in range(2)]
        up_l = [st.sbuf(f"up_l{t}", [P, KD, P], F32R) for t in range(2)]
        raw_d = st.sbuf("raw_d", [P, 2, D])
        d_h = st.sbuf("d_h", [P, 2, D], F32R)
        d_l = st.sbuf("d_l", [P, 2, D], F32R)
        hid_h = st.sbuf("hid_h", [P, 2, T], F32R)
        hid_l = st.sbuf("hid_l", [P, 2, T], F32R)
        silu = st.sbuf("silu", [P, 2, CH])
        up = st.sbuf("up", [P, CH])
        norm = Norm(st, m, next_norm, (0, 2, 1)) if next_norm is not None else None
        up_in = st.sem("up_in")
        d_in = st.sem("d_in")
        up_high = st.sem("up_high")
        up_split = st.sem("up_split")
        d_high = st.sem("d_high")
        d_split = st.sem("d_split")
        gu_done = st.sem("gu_done")
        gate_scaled = st.sem("gate_scaled")
        silu_done = st.sem("silu_done")
        hid_done = st.sem("hid_done")
        down_done = st.sem("down_done")
        down_added = st.sem("down_added")
        own = st.sem("own")
        block = st.block()
        stream, base = m.stream, m.stream.base
        wg = w_gate.rearrange("a (k p) f -> p (a k) f", p=P)
        wu = w_up.rearrange("a (k p) f -> p (a k) f", p=P)
        wd = w_down.rearrange("a (t p) d -> p (a t) d", p=P)
        LAST = PAIRS - 1

        @block.sync
        def _(sp):
            def load_up(i):
                sp.dma_start(raw_up[:, :, :], wu[:, :, bass.ts(i, 2 * P)]).then_inc(up_in, 16)

            def load_d(i):
                sp.dma_start(raw_d[:, :, :], wd[:, bass.ts(i, 2), :]).then_inc(d_in, 16)

            load_up(0)
            load_d(0)
            with sp.Fori(1, PAIRS) as i:
                stream.load(sp, base + i, wg, lambda i: i * (2 * P), i)
                sp.wait_ge(up_split, i * 2)
                load_up(i)
                sp.wait_ge(d_split, i)
                load_d(i)
            if then is not None:
                stream.load(sp, base + PAIRS, *then)

        @block.tensor
        def _(pe):
            def pair(i, last_pair):
                for n in range(GU_UNITS):
                    t, c = divmod(n, NCH)
                    if c == 0:
                        pe.wait_ge(stream.split, (base + i) * 2 + (t + 1))
                    pe.wait_ge(hid_done, i * GU_UNITS + (n + 1))
                    for side, w_h, w_l in ((0, stream.high[t], stream.low[t]), (1, up_h[t], up_l[t])):
                        if side == 1 and c == 0:
                            pe.wait_ge(up_split, i * 2 + (t + 1))
                        for k in range(KD):
                            last = product(pe, m.ps[:, 2 * (n % 2) + side, width(c)], w_h[:, k, :], w_l[:, k, :],
                                           m.uh[:, k, chunk(c)], m.ul[:, k, chunk(c)], k == 0, k == KD - 1)
                    last.then_inc(gu_done, 1)
                pe.wait_ge(d_split, i + 1)
                for n in range(DOWN_UNITS):
                    c, o = divmod(n, KD)
                    if o == 0:
                        pe.wait_ge(hid_done, i * GU_UNITS + (NCH + c + 3))
                    pe.wait_ge(down_added, i * DOWN_UNITS + (n + 1))
                    for t in range(2):
                        last = product(pe, m.ps[:, 4 + n % 4, width(c)], d_h[:, t, o * P:(o + 1) * P],
                                       d_l[:, t, o * P:(o + 1) * P], hid_h[:, t, chunk(c)], hid_l[:, t, chunk(c)],
                                       t == 0, t == 1)
                    last.then_inc(down_done, 1)
                    if last_pair and norm and c and o == 5:
                        norm.tensor_mean(pe, c - 1, c * KD)

            with pe.Fori(0, LAST) as i:
                pair(i, False)
            pair(LAST, True)
            if norm:
                norm.tensor_mean(pe, NCH - 1, DOWN_UNITS)

        @block.scalar
        def _(act):
            def high_up(i, t):
                if t == 0:
                    act.wait_ge(up_in, (i + 1) * 16)
                act.activation(up_h[t][:, :, :], raw_up[:, :, t * P:(t + 1) * P], ACT.Copy).then_inc(up_high, 1)

            for t in range(2):
                high_up(0, t)

            def pair(i, more):
                act.wait_ge(d_in, (i + 1) * 16)
                act.wait_ge(down_added, i * DOWN_UNITS + 4)
                act.activation(d_h[:, :, :], raw_d[:, :, :], ACT.Copy).then_inc(d_high, 1)
                for n in range(GU_UNITS):
                    t, c = divmod(n, NCH)
                    act.wait_ge(gate_scaled, i * GU_UNITS + (n + 1))
                    act.activation(silu[:, n % 2, width(c)], silu[:, n % 2, width(c)], ACT.Silu).then_inc(silu_done, 1)
                    if c == NCH - 1:
                        if more or then is not None:
                            stream.split_high(act, base + i + 1, t)
                        if more:
                            high_up(i + 1, t)

            with act.Fori(0, LAST) as i:
                pair(i, True)
            pair(LAST, False)
            if norm:
                for n in range(DOWN_UNITS):
                    c, o = divmod(n, KD)
                    act.wait_ge(down_added, LAST * DOWN_UNITS + (n + 5))
                    norm.parts.scalar_high(act, o, c)
                    norm.scalar_square(act, n, n % 2, m.x[:, o, chunk(c)], c)
                    if c and o == 6:
                        norm.scalar_root(act, c - 1)
                norm.scalar_root(act, NCH - 1)

        @block.vector
        def _(dve):
            def low_up(i, t):
                dve.wait_ge(up_high, i * 2 + (t + 1))
                dve.tensor_tensor(up_l[t][:, :, :], raw_up[:, :, t * P:(t + 1) * P], up_h[t][:, :, :].bitcast(F32),
                                  ALU.subtract).then_inc(up_split, 1)

            dve.sem_inc(hid_done, 2)
            dve.sem_inc(down_added, 4)
            for t in range(2):
                low_up(0, t)
            if norm:
                norm.vector_clear(dve)

            def low(i, t, more):
                if more or then is not None:
                    stream.split_low(dve, base + i + 1, t)
                if more:
                    low_up(i + 1, t)

            def norm_tile(n):
                c, o = divmod(n, KD)
                norm.parts.vector_low(dve, n + 1, o, c)
                norm.vector_sum(dve, n, n % 2, c)

            def pair(i, more):
                dve.wait_ge(d_high, i + 1)
                dve.tensor_tensor(d_l[:, :, :], raw_d[:, :, :], d_h[:, :, :].bitcast(F32),
                                  ALU.subtract).then_inc(d_split, 1)
                order = Count(dve, own, i * (3 * GU_UNITS))
                for n in range(GU_UNITS):
                    t, c = divmod(n, NCH)
                    gate, hid, by = silu[:, n % 2, width(c)], up[:, width(c)], m.rstd[:, chunk(c)]
                    dve.wait_ge(gu_done, i * GU_UNITS + (n + 1))
                    dve.wait_ge(hid_done, i * GU_UNITS + (n + 1))
                    dve.tensor_tensor(gate, m.ps[:, 2 * (n % 2), width(c)], by, ALU.mult).then_inc(gate_scaled, 1)
                    dve.wait_ge(hid_done, i * GU_UNITS + (n + 2))
                    order.then_wait(dve.tensor_tensor(hid, m.ps[:, 2 * (n % 2) + 1, width(c)], by, ALU.mult))
                    dve.wait_ge(silu_done, i * GU_UNITS + (n + 1))
                    order.then_wait(dve.tensor_tensor(hid, gate, hid, ALU.mult))
                    order.then_wait(dve.tensor_copy(hid_h[:, t, chunk(c)], hid))
                    dve.tensor_tensor(hid_l[:, t, chunk(c)], hid, hid_h[:, t, chunk(c)].bitcast(F32),
                                      ALU.subtract).then_inc(hid_done, 1)
                    if n == NCH:
                        low(i, 0, more)
                for n in range(DOWN_UNITS):
                    c, o = divmod(n, KD)
                    dve.wait_ge(down_done, i * DOWN_UNITS + (n + 1))
                    dve.scalar_tensor_tensor(m.x[:, o, chunk(c)], m.ps[:, 4 + n % 4, width(c)], 0.5, m.x[:, o, chunk(c)],
                                             ALU.mult, ALU.add).then_inc(down_added, 1)
                    if n == KD - 1 and (more or not norm):
                        low(i, 1, more)
                    if not more and norm:
                        if n == 0:
                            low(i, 1, more)
                        else:
                            norm_tile(n - 1)
                        if c and o == 7:
                            norm.vector_invert(dve, c - 1)

            with dve.Fori(0, LAST) as i:
                pair(i, True)
            pair(LAST, False)
            if norm:
                norm_tile(DOWN_UNITS - 1)
                norm.vector_invert(dve, NCH - 1)
        stream.base += PAIRS


def final(nc, m, g_final, y_prompt, y_sample):
    BLOCKS = TB + 1
    with Stage(nc, "final") as st:
        tok = st.sbuf("tok", [P, BLOCKS, D])
        junk = st.sbuf("junk", [P, 2, D])
        gain = st.sbuf("gain", [P, D])
        stat = st.sbuf("stat", [P, 3, BLOCKS])
        gain_in = st.sem("gain_in")
        turned = st.sem("turned")
        squared = st.sem("squared")
        shifted = st.sem("shifted")
        rooted = st.sem("rooted")
        inverted = st.sem("inverted")
        normed = st.sem("normed")
        out_done = st.sem("out_done")
        block = st.block()
        yp = y_prompt.rearrange("a (b p) d -> p (a b) d", p=P)

        def rows(b):
            return slice(0, P if b < TB else NS)

        def flat(b):
            return m.ps[rows(b), 2 * (b % 4):2 * (b % 4) + 2, :].rearrange("p a f -> p (a f)")

        @block.tensor
        def _(pe):
            for b in range(BLOCKS):
                if b >= 4:
                    pe.wait_ge(normed, b - 3)
                for k in range(KD):
                    last = pe.transpose(m.ps[rows(b), 2 * (b % 4) + k // 4, (k % 4) * P:(k % 4 + 1) * P],
                                        m.x[:, k, b * P:min((b + 1) * P, T)], m.ident[:, :])
                last.then_inc(turned, 1)

        @block.scalar
        def _(act):
            def square(b):
                act.wait_ge(turned, b + 1)
                if b >= 2:
                    act.wait_ge(squared, b - 1)
                act.activation(junk[rows(b), b % 2, :], flat(b), ACT.Square,
                               accum_out=stat[rows(b), 0, b:b + 1]).then_inc(squared, 1)

            square(0)
            for b in range(BLOCKS):
                if b + 1 < BLOCKS:
                    square(b + 1)
                act.wait_ge(shifted, b + 1)
                act.activation(stat[rows(b), 1, b:b + 1], stat[rows(b), 1, b:b + 1], ACT.Sqrt).then_inc(rooted, 1)

        @block.vector
        def _(dve):
            dve.wait_ge(gain_in, 16)

            def shift(b):
                dve.wait_ge(squared, b + 1)
                dve.tensor_scalar(stat[rows(b), 1, b:b + 1], stat[rows(b), 0, b:b + 1], 1.0 / D, EPS, ALU.mult,
                                  ALU.add).then_inc(shifted, 1)

            shift(0)
            for b in range(BLOCKS):
                if b + 1 < BLOCKS:
                    shift(b + 1)
                dve.wait_ge(rooted, b + 1)
                dve.reciprocal(stat[rows(b), 2, b:b + 1], stat[rows(b), 1, b:b + 1]).then_inc(inverted, 1)
                dve.wait_ge(inverted, b + 1)
                dve.scalar_tensor_tensor(tok[rows(b), b, :], flat(b), stat[rows(b), 2, b:b + 1], gain[rows(b), :],
                                         ALU.mult, ALU.mult).then_inc(normed, 1)

        @block.sync
        def _(sp):
            sp.dma_start(gain[:, :], g_final.partition_broadcast(P)).then_inc(gain_in, 16)
            for b in range(TB):
                sp.wait_ge(normed, b + 1)
                sp.dma_start(yp[:, b, :], tok[:, b, :]).then_inc(out_done, 16)
            sp.wait_ge(normed, BLOCKS)
            sp.dma_start(y_sample.rearrange("n a d -> (n a) d"), tok[0:NS, TB, :]).then_inc(out_done, 16)
            sp.wait_ge(out_done, 16 * BLOCKS)


GROUPS = ((128, 1), (512, 4), (2048, 16))
NG = len(GROUPS)
HG = 4
DH = 64
GW = HG * DH
QKV = NG * GW
NPOOL = 4
POOL_W = NPOOL * P
MH = 4
MEM = 256
MEM_W = MH * P
Z_COL = 3 * QKV
QM_COL = Z_COL + POOL_W
GATE_COL = QM_COL + MEM_W
NEG = -1e30
REACH = 128
RES = GW + 2 * HG


class Product:

    def __init__(self, st, m, w, cols, pairs, then, banks=2 * NCH):
        self.banks = banks
        self.m, self.w, self.cols, self.pairs, self.then = m, w, cols, pairs, then
        self.base = m.stream.base
        self.done = st.sem("product_done")
        self.taken = st.sem("product_taken")

    def load(self, sp):
        self.m.stream.load_all(sp, self.pairs, self.w, self.cols, self.then)

    def tensor_pair(self, pe, i, ready=None, after=None):
        stream = self.m.stream
        for n in range(2 * NCH):
            t, c = divmod(n, NCH)
            if c == 0:
                pe.wait_ge(stream.split, (self.base + i) * 2 + (t + 1))
            pe.wait_ge(self.taken, i * (2 * NCH) + (n + 1))
            for k in range(KD):
                if ready is not None and t == 0:
                    pe.wait_ge(ready, c * KD + (k + 1))
                last = product(pe, self.m.ps[:, n % self.banks, width(c)], stream.high[t][:, k, :], stream.low[t][:, k, :],
                               self.m.uh[:, k, chunk(c)], self.m.ul[:, k, chunk(c)], k == 0, k == KD - 1)
            last.then_inc(self.done, 1)
            if after is not None:
                after(n)

    def tensor(self, pe):
        with pe.Fori(0, self.pairs) as i:
            self.tensor_pair(pe, i)

    def scalar_next(self, act, i, t):
        act.wait_ge(self.done, i * (2 * NCH) + (t + 1) * NCH)
        self.m.stream.split_high(act, self.base + i + 1, t)

    def scalar(self, act):
        with act.Fori(0, self.pairs) as i:
            for t in range(2):
                self.scalar_next(act, i, t)

    def vector_start(self, dve):
        dve.sem_inc(self.taken, self.banks)

    def vector_pair(self, dve, i, take, after=None):
        for n in range(2 * NCH):
            t, c = divmod(n, NCH)
            dve.wait_ge(self.done, i * (2 * NCH) + (n + 1))
            take(dve, i, t, c, self.m.ps[:, n % self.banks, width(c)]).then_inc(self.taken, 1)
            if c == NCH - 1:
                self.m.stream.split_low(dve, self.base + i + 1, t)
            if after is not None:
                after(n)

    def vector(self, dve, take):
        self.vector_start(dve)
        with dve.Fori(0, self.pairs) as i:
            self.vector_pair(dve, i, take)


    def tensor_beside(self, pe, beside):
        for i in range(self.pairs):
            self.tensor_pair(pe, i, after=lambda n: beside(i * (2 * NCH) + n))

    def vector_beside(self, dve, take, beside):
        self.vector_start(dve)
        for i in range(self.pairs):
            self.vector_pair(dve, i, take, after=lambda n: beside(i * (2 * NCH) + n))

    def close(self):
        self.m.stream.base += self.pairs


def scaled(dve, m, c, out, src):
    return dve.tensor_tensor(out, src, m.rstd[:, chunk(c)], ALU.mult)


def blocks_of(g):
    in_residue = SEQ // GROUPS[g][1] // P
    return [(b, in_residue > 1 and b % in_residue != 0) for b in range(TB)]


def attention(nc, m, g, w_in, new_kv, then, side_job=None):
    window, dil = GROUPS[g]
    length = SEQ // dil
    blocks = blocks_of(g)
    with Stage(nc, f"att{g}") as st:
        qkv = st.sbuf("qkv", [P, 6, T])
        with Stage(nc, f"qkv{g}") as pt:
            proj = Product(pt, m, w_in, lambda i: i * QKV + g * GW, 3, then, banks=NCH if side_job else 2 * NCH)
            side = side_job(pt) if side_job else None
            block = pt.block()

            def take(dve, i, t, c, src):
                n_l = (min(CHUNKS[c][0] + CHUNKS[c][1], SEQ) - CHUNKS[c][0]) // dil
                l0 = CHUNKS[c][0] // dil
                if c == NCH - 1:
                    at = i * (2 * NG) + (2 * g + t)
                    dve.tensor_tensor(m.s_qkv[:, bass.ds(at, 1), :], src[:, SEQ - CHUNKS[c][0]:].unsqueeze(1),
                                      m.rstd[:, SEQ:T].unsqueeze(1), ALU.mult)
                out = qkv[:, bass.ds(i * 2 + t, 1), 0:SEQ].rearrange("p a (r l) -> p (a r) l", r=dil)[:, :, l0:l0 + n_l]
                by = m.rstd[:, CHUNKS[c][0]:CHUNKS[c][0] + n_l * dil]
                return dve.tensor_tensor(out, src[:, 0:n_l * dil].rearrange("p (l r) -> p r l", r=dil),
                                         by.rearrange("p (l r) -> p r l", r=dil), ALU.mult)

            @block.sync
            def _(sp):
                proj.load(sp)

            @block.tensor
            def _(pe):
                if side:
                    proj.tensor_beside(pe, lambda u: side.tensor(pe, u))
                else:
                    proj.tensor(pe)

            @block.scalar
            def _(act):
                if side:
                    side.scalar(act, proj)
                else:
                    proj.scalar(act)

            @block.vector
            def _(dve):
                if side:
                    proj.vector_beside(dve, take, lambda u: side.vector(dve, u))
                else:
                    proj.vector(dve, take)

            if side:
                @block.gpsimd
                def _(gp):
                    side.gpsimd(gp)
            proj.close()

        kv = st.sbuf("kv", [P, TB, 2 * GW])
        bias = st.sbuf("bias", [P, HG, 2 * P])
        logit = st.sbuf("logit", [P, 2, HG, 2 * P])
        falling = logit[:, 1, :, :]
        prob = st.sbuf("prob", [P, 2, HG, 2 * P])
        turned = st.sbuf("turned", [P, 2, 2, HG, P])
        res = st.sbuf("res", [P, TB, RES])
        neg = st.sbuf("neg", [P, 2, HG])
        bias_in = st.sem("bias_in")
        bias_ready = st.sem("bias_ready")
        kv_turned = st.sem("kv_turned")
        kv_taken = st.sem("kv_taken")
        scored = st.sem("scored")
        logits = st.sem("logits")
        maxed = st.sem("maxed")
        negated = st.sem("negated")
        exped = st.sem("exped")
        p_turned = st.sem("p_turned")
        p_taken_act = st.sem("p_taken_act")
        p_taken_dve = st.sem("p_taken_dve")
        weighed = st.sem("weighed")
        res_taken = st.sem("res_taken")
        stored = st.sem("stored")
        block = st.block()
        head_at = [2 * (i % 2) + i // 2 for i in range(HG)]

        def seen(b):
            return slice(0 if blocks[b][1] else P, 2 * P)

        kv_out = new_kv.rearrange("a n t c h d -> (a n t) (c h d)")
        kept = kv_out.shape[0]

        @block.sync
        def _(sp):
            for i, h in enumerate(head_at):
                row = m.bias_rows[g, g * HG + h, :]
                tile = bass.AP(row.tensor, row.offset, [[1, P], [1, 2 * P]])
                sp.dma_start(falling[:, i, :], tile).then_inc(bias_in, 16)
            n_out = 0
            for b in range(TB):
                for part in range(max(1, P // length)):
                    rows = min(P, length)
                    r, l0 = divmod(b * P + part * rows, length)
                    t_first = l0 * dil + r
                    if t_first >= SEQ - kept or g == 2:
                        n_out += 1
                        if part == 0:
                            sp.wait_ge(kv_taken, b + 1)
                        dst = kv_out.rearrange("(l r) c -> r l c", r=dil)[r, l0 - (SEQ - kept) // dil:l0 - (SEQ - kept) // dil + rows, :]
                        sp.dma_start(dst, kv[part * rows:(part + 1) * rows, b, :]).then_inc(stored, 16)
            for b in range(TB):
                sp.wait_ge(res_taken, b + 1)
                for part in range(max(1, P // length)):
                    rows = min(P, length)
                    r, l0 = divmod(b * P + part * rows, length)
                    dst = m.group_out.rearrange("(l r) g c -> r l g c", r=dil)[r, l0:l0 + rows, g, :]
                    n_out += 1
                    sp.dma_start(dst, res[part * rows:(part + 1) * rows, b, :]).then_inc(stored, 16)
            sp.wait_ge(stored, 16 * n_out)

        @block.tensor
        def _(pe):
            for b in range(TB):
                if b >= 2:
                    pe.wait_ge(kv_taken, b - 1)
                for i in range(4):
                    last = pe.transpose(m.ps[:, 4 + b % 2, i * P:(i + 1) * P], qkv[:, 2 + i, b * P:(b + 1) * P],
                                        m.ident[:, :])
                last.then_inc(kv_turned, 1)

            def scores(b):
                if b >= 2:
                    pe.wait_ge(logits, b - 1)
                for i, h in enumerate(head_at):
                    rows = slice(DH * (h % 2), DH * (h % 2) + DH)
                    bank = 2 * (b % 2) + i // 2
                    w = seen(b)
                    last = pe.matmul(m.ps[:, bank, (i % 2) * 2 * P + w.start:(i % 2 + 1) * 2 * P],
                                     qkv[rows, h // 2, b * P:(b + 1) * P],
                                     qkv[rows, 2 + h // 2, (b - 1) * P + w.start:(b + 1) * P], start=True, stop=True)
                last.then_inc(scored, 1)

            def turn(b):
                pe.wait_ge(exped, HG * (b + 1))
                if b == 0:
                    pe.wait_ge(kv_taken, TB)
                else:
                    pe.wait_ge(p_taken_act, b)
                    pe.wait_ge(p_taken_dve, b)
                for kb in range(0 if blocks[b][1] else 1, 2):
                    for i in range(HG):
                        last = pe.transpose(m.ps[:, 4 + kb, i * P:(i + 1) * P], prob[:, b % 2, i, kb * P:(kb + 1) * P],
                                            m.ident[:, :])
                last.then_inc(p_turned, 1)

            def weigh(b):
                pe.wait_ge(p_taken_act, b + 1)
                pe.wait_ge(p_taken_dve, b + 1)
                if b >= 2:
                    pe.wait_ge(res_taken, b - 1)
                for i, h in enumerate(head_at):
                    first = 0 if blocks[b][1] else 1
                    for kb in range(first, 2):
                        last = pe.matmul(m.ps[:, 6 + b % 2, h * DH:(h + 1) * DH], turned[:, b % 2, kb, i, :],
                                         kv[:, b - 1 + kb, GW + h * DH:GW + (h + 1) * DH],
                                         start=kb == first, stop=kb == 1)
                last.then_inc(weighed, 1)

            scores(0)
            scores(1)
            for b in range(TB):
                turn(b)
                if b + 2 < TB:
                    scores(b + 2)
                weigh(b)

        @block.scalar
        def _(act):
            def exps(b):
                act.wait_ge(negated, b + 1)
                if b >= 2:
                    act.wait_ge(p_turned, b - 1)
                w = seen(b)
                for i in range(HG):
                    act.activation(prob[:, b % 2, i, w], logit[:, b % 2, i, w], ACT.Exp, bias=neg[:, b % 2, i:i + 1],
                                   accum_out=res[:, b, GW + i:GW + i + 1]).then_inc(exped, 1)

            exps(0)
            for b in range(TB):
                if b + 1 < TB:
                    exps(b + 1)
                act.wait_ge(p_turned, b + 1)
                if b >= 2:
                    act.wait_ge(weighed, b - 1)
                act.activation(turned[:, b % 2, 1, :, :], m.ps[:, 5, :].rearrange("p (i q) -> p i q", i=HG),
                               ACT.Copy).then_inc(p_taken_act, 1)

        @block.vector
        def _(dve):
            for b in range(TB):
                dve.wait_ge(kv_turned, b + 1)
                dve.tensor_copy(kv[:, b, :], m.ps[:, 4 + b % 2, :]).then_inc(kv_taken, 1)
            dve.wait_ge(bias_in, 16 * HG)
            dve.tensor_copy(bias[:, :, :], falling[:, :, ::-1]).then_inc(bias_ready, 1)
            dve.wait_ge(bias_ready, 1)
            if length < P:
                dve.memset(bias[length:P, :, P:P + length], NEG).then_inc(bias_ready, 1)
                dve.wait_ge(bias_ready, 2)

            def soft(b):
                w = seen(b)
                dve.wait_ge(scored, b + 1)
                if b >= 2:
                    dve.wait_ge(exped, HG * (b - 1))
                src = m.ps[:, 2 * (b % 2):2 * (b % 2) + 2, :].rearrange("p a (i k) -> p (a i) k", k=2 * P)
                dve.scalar_tensor_tensor(logit[:, b % 2, :, w], src[:, :, w], DH ** -0.5, bias[:, :, w], ALU.mult,
                                         ALU.add).then_inc(logits, 1)
                dve.wait_ge(logits, b + 1)
                dve.tensor_reduce(res[:, b, GW + HG:GW + 2 * HG], logit[:, b % 2, :, w], AX_X,
                                  ALU.max).then_inc(maxed, 1)
                dve.wait_ge(maxed, b + 1)
                dve.tensor_scalar(neg[:, b % 2, :], res[:, b, GW + HG:GW + 2 * HG], -1.0, None,
                                  ALU.mult).then_inc(negated, 1)

            soft(0)
            for b in range(TB):
                if b + 1 < TB:
                    soft(b + 1)
                dve.wait_ge(p_turned, b + 1)
                if b >= 2:
                    dve.wait_ge(weighed, b - 1)
                if blocks[b][1]:
                    dve.tensor_copy(turned[:, b % 2, 0, :, :], m.ps[:, 4, :].rearrange("p (i q) -> p i q", i=HG)
                                    ).then_inc(p_taken_dve, 1)
                else:
                    dve.sem_inc(p_taken_dve, 1)
                if b >= 1:
                    dve.wait_ge(weighed, b)
                    dve.tensor_copy(res[:, b - 1, 0:GW], m.ps[:, 6 + (b - 1) % 2, 0:GW]).then_inc(res_taken, 1)
            dve.wait_ge(weighed, TB)
            dve.tensor_copy(res[:, TB - 1, 0:GW], m.ps[:, 6 + (TB - 1) % 2, 0:GW]).then_inc(res_taken, 1)


class MemoryKeys:

    MT = MEM // P

    def __init__(self, st, nc, m, mem_prompt, w_mem_kv, new_mem_kv):
        self.nc, self.m, self.mem_prompt = nc, m, mem_prompt
        self.out = new_mem_kv.rearrange("a n (t p) c h e -> p (a n t) (c h e)", p=P)
        self.w_v = w_mem_kv.rearrange("a (k p) f -> p (a k) f", p=P)
        self.kv = st.sbuf("kv", [P, self.MT, 2 * MEM_W])
        self.kt = st.sbuf("kt", [P, MH, MEM])
        self.tok = st.sbuf("tok", [P, self.MT, D])
        self.w = st.sbuf("w", [P, KD, D // 2])
        self.turned_m = st.sbuf("turned", [P, KD, MEM])
        self.stat = st.sbuf("stat", [P, 2, self.MT])
        self.tok_in = st.sem("tok_in")
        self.w_arrived = st.sem("w_arrived")
        self.squared = st.sem("squared")
        self.shifted = st.sem("shifted")
        self.rooted = st.sem("rooted")
        self.inverted = st.sem("inverted")
        self.normed = st.sem("normed")
        self.turned = st.sem("turned_sem")
        self.gained = st.sem("gained")
        self.done = st.sem("done")
        self.taken = st.sem("taken")
        self.kt_done = st.sem("kt_done")
        self.kt_taken = st.sem("kt_taken")
        self.stored = st.sem("stored")

    def product_bank(self, n):
        return (7, 3, 4, 5)[n]

    def gpsimd(self, gp):
        gp.dma_start(self.tok[:, :, :], self.mem_prompt.rearrange("a (t p) d -> p (a t) d", p=P)).then_inc(self.tok_in, 16)
        gp.dma_start(self.w[:, :, :], self.w_v[:, :, 0:D // 2]).then_inc(self.w_arrived, 16)
        gp.wait_ge(self.done, self.MT)
        gp.dma_start(self.w[:, :, :], self.w_v[:, :, D // 2:D]).then_inc(self.w_arrived, 16)
        gp.wait_ge(self.taken, 2 * self.MT)
        gp.dma_start(self.out, self.kv[:, :, :]).then_inc(self.stored, 16)
        gp.dma_start(self.m.mem_v, self.kv[:, :, MEM_W:]).then_inc(self.stored, 16)
        gp.wait_ge(self.kt_taken, 1)
        gp.dma_start(self.m.mem_kt, self.kt[:, :, :]).then_inc(self.stored, 16)
        gp.wait_ge(self.stored, 48)

    def scalar(self, act, proj):
        act.wait_ge(self.tok_in, 16)
        for t in range(self.MT):
            act.activation(self.turned_m[:, 4 * t:4 * t + 4, :].rearrange("p a f -> p (a f)"), self.tok[:, t, :], ACT.Square,
                           accum_out=self.stat[:, 0, t:t + 1]).then_inc(self.squared, 1)
        act.wait_ge(self.shifted, 1)
        act.activation(self.stat[:, 1, :], self.stat[:, 1, :], ACT.Sqrt).then_inc(self.rooted, 1)
        proj.scalar_next(act, 0, 0)
        act.wait_ge(self.squared, self.MT)
        for k in range(KD):
            act.wait_ge(self.turned, k // 2 + 1)
            act.activation(self.turned_m[:, k, :], self.m.ps[:, 3 + k // 2, (k % 2) * MEM:(k % 2 + 1) * MEM], ACT.Copy,
                           scale=self.m.gain[:, G_MEM * KD + k:G_MEM * KD + k + 1]).then_inc(self.gained, 1)
        proj.scalar_next(act, 0, 1)
        for t in range(2):
            proj.scalar_next(act, 1, t)
        act.wait_ge(self.kt_done, 1)
        act.activation(self.kt[:, :, :], self.m.ps[:, 6:8, :].rearrange("p a (h t) -> p (a h) t", h=2),
                       ACT.Copy).then_inc(self.kt_taken, 1)
        for t in range(2):
            proj.scalar_next(act, 2, t)

    def vector(self, dve, u):
        if u == 0:
            dve.wait_ge(self.squared, self.MT)
            dve.tensor_scalar(self.stat[:, 1, :], self.stat[:, 0, :], 1.0 / D, EPS, ALU.mult, ALU.add).then_inc(self.shifted, 1)
            dve.wait_ge(self.rooted, 1)
            dve.reciprocal(self.stat[:, 0, :], self.stat[:, 1, :]).then_inc(self.inverted, 1)
            dve.wait_ge(self.inverted, 1)
            for t in range(self.MT):
                dve.tensor_scalar(self.tok[:, t, :], self.tok[:, t, :], self.stat[:, 0, t:t + 1], None,
                                  ALU.mult).then_inc(self.normed, 1)
        if u in (4, 5, 9, 10):
            n = (4, 5, 9, 10).index(u)
            half, t = divmod(n, self.MT)
            dve.wait_ge(self.done, n + 1)
            dve.tensor_copy(self.kv[:, t, half * 512:(half + 1) * 512], self.m.ps[:, self.product_bank(n), :]
                            ).then_inc(self.taken, 1)

    def tensor(self, pe, u):
        m = self.m
        if u == 1:
            pe.wait_ge(self.normed, self.MT)
            for k in range(KD):
                for t in range(self.MT):
                    last = pe.transpose(m.ps[:, 3 + k // 2, (k % 2) * MEM + t * P:(k % 2) * MEM + (t + 1) * P],
                                        self.tok[:, t, k * P:(k + 1) * P], m.ident[:, :])
                if k % 2:
                    last.then_inc(self.turned, 1)
        if u in (3, 4, 8, 9):
            n = (3, 4, 8, 9).index(u)
            half, t = divmod(n, self.MT)
            pe.wait_ge(self.gained, KD)
            pe.wait_ge(self.w_arrived, 16 * (half + 1))
            for k in range(KD):
                last = pe.matmul(m.ps[:, self.product_bank(n), :], self.turned_m[:, k, t * P:(t + 1) * P], self.w[:, k, :],
                                 start=k == 0, stop=k == KD - 1)
            last.then_inc(self.done, 1)
        if u == 11:
            pe.wait_ge(self.taken, self.MT)
            for h in range(MH):
                for t in range(self.MT):
                    last = pe.transpose(m.ps[:, 6 + h // 2, (h % 2) * MEM + t * P:(h % 2) * MEM + (t + 1) * P],
                                        self.kv[:, t, h * P:(h + 1) * P], m.ident[:, :])
            last.then_inc(self.kt_done, 1)


SIDE_PAIR = 1


def merge(nc, m, name, branch, first, w_in, w_o, bh, bl, kt, then, late, side_job=None):
    with Stage(nc, name) as st:
        raw_o = st.sbuf("raw_o", [P, kt, 2 * P])
        o_h = [st.sbuf(f"o_h{t}", [P, kt, P], F32R) for t in range(2)]
        o_l = [st.sbuf(f"o_l{t}", [P, kt, P], F32R) for t in range(2)]
        gate = st.sbuf("gate", [P, NCH, CH])
        side = side_job(st) if side_job else None
        o_in = st.sem("o_in")
        o_high = st.sem("o_high")
        o_split = st.sem("o_split")
        late_in = [st.sem(f"late_in{i}") for i in range(2)]
        late_high = st.sem("late_high")
        late_split = st.sem("late_split")
        gate_done = st.sem("gate_done")
        scaled_sem = st.sem("scaled")
        gated = st.sem("gated")
        o_done = st.sem("o_done")
        own = st.sem("own")
        mixed = st.sem("mixed")
        block = st.block()
        units = 2 * NCH
        pairs = KD // 2
        stream, base = m.stream, m.stream.base
        halves = gate[:, :, :].rearrange("p c t -> p (c t)")[:, 0:SEQ].rearrange("p (s t) -> p s t", s=2)

        def piece(x, n):
            half, k = divmod(n, kt)
            return x[:, k, half * (SEQ // 2):(half + 1) * (SEQ // 2)]

        @block.sync
        def _(sp):
            def load_o(i):
                sp.dma_start(raw_o[:, :, :], w_o[:, :, bass.ds(i * (2 * P), 2 * P)]).then_inc(o_in, 16)

            load_o(0)
            for n in range(2 * kt):
                if n >= 2:
                    sp.wait_ge(late_split, n - 1)
                sp.dma_start(halves[:, n % 2, :], piece(late[0], n)).then_inc(late_in[n % 2], 16)
            with sp.Fori(1, pairs) as i:
                sp.wait_ge(o_split, i * 2)
                load_o(i)
                stream.load(sp, base + i, w_in, lambda i: i * (2 * P) + (GATE_COL + branch * D), i)
            stream.load(sp, base + pairs, *then)

        @block.tensor
        def _(pe):
            def pair(i, start):
                for t in range(2):
                    pe.wait_ge(stream.split, (base + i) * 2 + (t + 1))
                    for c in range(NCH):
                        pe.wait_ge(scaled_sem, i * units + (NCH * t + c + 1))
                        for k in range(KD):
                            last = product(pe, m.ps[:, 2 * c, width(c)], stream.high[t][:, k, :], stream.low[t][:, k, :],
                                           m.uh[:, k, chunk(c)], m.ul[:, k, chunk(c)], k == 0, k == KD - 1)
                        last.then_inc(gate_done, 1)
                        if side and start:
                            side.tensor(pe, 2 * units * i + 2 * NCH * t + c)
                    pe.wait_ge(o_split, i * 2 + (t + 1))
                    for c in range(NCH):
                        if start and i == 0 and t == 0:
                            pe.wait_ge(late_split, kt if c == 0 else 2 * kt)
                        pe.wait_ge(mixed, i * units + (NCH * t + c + 1))
                        for k in range(kt):
                            last = product(pe, m.ps[:, 2 * c + 1, width(c)], o_h[t][:, k, :], o_l[t][:, k, :],
                                           bh[:, k, chunk(c)], bl[:, k, chunk(c)], k == 0, k == kt - 1)
                        last.then_inc(o_done, 1)
                        if side and start:
                            side.tensor(pe, 2 * units * i + 2 * NCH * t + NCH + c)

            peeled = pairs if side else 1
            for i in range(peeled):
                pair(i, True)
            if peeled < pairs:
                with pe.Fori(peeled, pairs) as i:
                    pair(i, False)

        @block.scalar
        def _(act):
            def high(i, t):
                if t == 0:
                    act.wait_ge(o_in, (i + 1) * 16)
                act.activation(o_h[t][:, :, :], raw_o[:, :, t * P:(t + 1) * P], ACT.Copy).then_inc(o_high, 1)

            for t in range(2):
                high(0, t)
            act.activation(bh[:, :, SEQ:T], late[1], ACT.Copy).then_inc(late_high, 1)
            for n in range(2 * kt):
                act.wait_ge(late_in[n % 2], 16 * (n // 2 + 1))
                act.activation(piece(bh, n), halves[:, n % 2, :], ACT.Copy).then_inc(late_high, 1)

            def pair(i, more):
                for t in range(2):
                    for c in range(NCH):
                        act.wait_ge(scaled_sem, i * units + (NCH * t + c + 4))
                        act.activation(gate[:, c, width(c)], gate[:, c, width(c)], ACT.Sigmoid).then_inc(gated, 1)
                    stream.split_high(act, base + i + 1, t)
                    if more:
                        act.wait_ge(o_done, i * units + NCH * (t + 1))
                        high(i + 1, t)

            if side:
                for i in range(pairs):
                    pair(i, i < pairs - 1)
                    if i == SIDE_PAIR:
                        side.scalar(act)
            else:
                with act.Fori(0, pairs - 1) as i:
                    pair(i, True)
                pair(pairs - 1, False)

        @block.vector
        def _(dve):
            def low(i, t):
                dve.wait_ge(o_high, i * 2 + (t + 1))
                dve.tensor_tensor(o_l[t][:, :, :], raw_o[:, :, t * P:(t + 1) * P], o_h[t][:, :, :].bitcast(F32),
                                  ALU.subtract).then_inc(o_split, 1)

            dve.sem_inc(mixed, NCH)
            dve.sem_inc(scaled_sem, NCH)
            for t in range(2):
                low(0, t)
            dve.wait_ge(late_high, 1)
            dve.tensor_tensor(bl[:, :, SEQ:T], late[1], bh[:, :, SEQ:T].bitcast(F32), ALU.subtract)
            for n in range(2 * kt):
                dve.wait_ge(late_high, n + 2)
                dve.tensor_tensor(piece(bl, n), halves[:, n % 2, :], piece(bh, n).bitcast(F32),
                                  ALU.subtract).then_inc(late_split, 1)
            dve.wait_ge(late_split, 2 * kt)

            def pair(i, more):
                order = Count(dve, own, i * units)
                for t in range(2):
                    for c in range(NCH):
                        dve.wait_ge(gate_done, i * units + (NCH * t + c + 1))
                        dve.wait_ge(mixed, i * units + (NCH * t + c + 1))
                        scaled(dve, m, c, gate[:, c, width(c)], m.ps[:, 2 * c, width(c)]).then_inc(scaled_sem, 1)
                        if side:
                            side.vector(dve, 2 * units * i + 2 * NCH * t + c)
                    stream.split_low(dve, base + i + 1, t)
                    for c in range(NCH):
                        n = NCH * t + c
                        dve.wait_ge(o_done, i * units + (n + 1))
                        dve.wait_ge(gated, i * units + (n + 1))
                        g, proj = gate[:, c, width(c)], m.ps[:, 2 * c + 1, width(c)]
                        mix = m.mix[:, bass.ds(i * 2 + t, 1), chunk(c)].rearrange("p a t -> p (a t)")
                        if first:
                            dve.tensor_tensor(mix, g, proj, ALU.mult).then_inc(mixed, 1)
                        else:
                            order.then_wait(dve.tensor_tensor(g, g, proj, ALU.mult))
                            dve.tensor_tensor(mix, mix, g, ALU.add).then_inc(mixed, 1)
                        if side:
                            side.vector(dve, 2 * units * i + 2 * NCH * t + NCH + c)
                    if more:
                        low(i + 1, t)

            if side:
                for i in range(pairs):
                    pair(i, i < pairs - 1)
            else:
                with dve.Fori(0, pairs - 1) as i:
                    pair(i, True)
                pair(pairs - 1, False)

        if side:
            @block.gpsimd
            def _(gp):
                side.gpsimd(gp)
        stream.base += pairs


def mix_out(nc, m, w_out, next_norm, then):
    with Stage(nc, "mix_out") as st:
        pairs = KD // 2
        proj = Product(st, m, w_out, lambda i: i * (2 * P), pairs, then)
        norm = Norm(st, m, next_norm, (6, 7, 6))
        mix_high = st.sem("mix_high")
        mix_low = st.sem("mix_low")
        block = st.block()
        units = 2 * NCH

        def tile_of_x(i, t, c):
            return m.x[:, bass.ds(i * 2 + t, 1), chunk(c)].rearrange("p a t -> p (a t)")

        @block.sync
        def _(sp):
            proj.load(sp)

        @block.tensor
        def _(pe):
            def mean(n):
                if n > NCH:
                    norm.tensor_mean(pe, n - NCH - 1, (pairs - 1) * units + n)

            proj.tensor_pair(pe, 0, ready=mix_low)
            with pe.Fori(1, pairs - 1) as i:
                proj.tensor_pair(pe, i)
            proj.tensor_pair(pe, pairs - 1, after=mean)
            norm.tensor_mean(pe, NCH - 1, pairs * units)

        @block.scalar
        def _(act):
            for c in range(NCH):
                for k in range(KD):
                    act.activation(m.uh[:, k, chunk(c)], m.mix[:, k, chunk(c)], ACT.Copy).then_inc(mix_high, 1)

            def pair(i, last):
                for n in range(units):
                    t, c = divmod(n, NCH)
                    act.wait_ge(proj.taken, (i + 1) * units + (n + 1))
                    norm.scalar_square(act, i * units + n, n % 2, tile_of_x(i, t, c), c)
                    if last and t == 1:
                        for k in range(KD):
                            norm.parts.scalar_high(act, k, c)
                        if c:
                            norm.scalar_root(act, c - 1)
                    if c == NCH - 1:
                        proj.scalar_next(act, i, t)
                if last:
                    norm.scalar_root(act, NCH - 1)

            with act.Fori(0, pairs - 1) as i:
                pair(i, False)
            pair(pairs - 1, True)

        @block.vector
        def _(dve):
            proj.vector_start(dve)
            for n in range(NCH * KD):
                c, k = divmod(n, KD)
                dve.wait_ge(mix_high, n + 1)
                dve.tensor_tensor(m.ul[:, k, chunk(c)], m.mix[:, k, chunk(c)], m.uh[:, k, chunk(c)].bitcast(F32),
                                  ALU.subtract).then_inc(mix_low, 1)
            norm.vector_clear(dve)

            def add(dve, i, t, c, src):
                x = tile_of_x(i, t, c)
                return dve.tensor_tensor(x, x, src, ALU.add)

            def pair(i, last):
                def norm_tile(n):
                    t, c = divmod(n, NCH)
                    norm.vector_sum(dve, i * units + n, n % 2, c)
                    if last and t == 1:
                        for k in range(KD):
                            norm.parts.vector_low(dve, KD * c + k + 1, k, c)
                        if c:
                            norm.vector_invert(dve, c - 1)
                proj.vector_pair(dve, i, add, norm_tile)

            with dve.Fori(0, pairs - 1) as i:
                pair(i, False)
            pair(pairs - 1, True)
            norm.vector_invert(dve, NCH - 1)
        proj.close()


POOL_WINDOWS = (2, 4, 8, 16)
HIST = 15
PAD = 16


def pool_values(nc, m, z, w_in, then, caches, new_kv):
    rows = NS * HG
    with Stage(nc, "samp") as st:
        proj = Product(st, m, w_in, lambda i: i * (2 * P) + Z_COL, NPOOL // 2, then, banks=NCH)
        cache = [st.sbuf(f"cache{g}", [REACH, NS, 2 * GW]) for g in range(NG)]
        tok = st.sbuf("tok", [NS, 3 * QKV])
        own_of = st.sbuf("own_of", [rows, NS])
        prod = st.sbuf("prod", [P, QKV])
        score = st.sbuf("score", [P, NG, NS, HG])
        new_prod = prod[0:NS, :]
        new_score = st.sbuf("new_score", [NS, NG, HG])
        prob = st.sbuf("prob", [rows, NG, REACH + 1])
        small = st.sbuf("small", [rows, 4])
        diag = st.sbuf("diag", [rows, NG, rows])
        p_cols = st.sbuf("p_cols", [P, NG, rows])
        new_p = st.sbuf("new_p", [NS, NG, rows])
        cleared = st.sem("cleared")
        cache_in = [st.sem(f"cache_in{g}") for g in range(NG)]
        own_of_in = st.sem("own_of_in")
        stored = st.sem("stored")
        new_out = st.sem("new_out")
        new_back = st.sem("new_back")
        tok_turned = st.sem("tok_turned")
        tok_taken = st.sem("tok_taken")
        spread = st.sem("spread")
        multiplied = st.sem("multiplied")
        scored = st.sem("scored")
        own = st.sem("own")
        logits = st.sem("logits")
        new_scored = st.sem("new_scored")
        rowed = st.sem("rowed")
        maxed = st.sem("maxed")
        exped = st.sem("exped")
        normal = st.sem("normal")
        coled = st.sem("coled")
        cols_taken = st.sem("cols_taken")
        weighed = st.sem("weighed")
        block = st.block()
        flat = prob[:, :, :].rearrange("p g r -> p (g r)")

        def take(dve, i, t, c, src):
            out = z[:, i * 2 + t, PAD + CHUNKS[c][0]:PAD + CHUNKS[c][0] + CHUNKS[c][1]]
            return scaled(dve, m, c, out, src)

        def spread_queries(n, g):
            at = g * GW
            return m.ps[:, 3 + 2 * (n % 2) + at // 512, at % 512:at % 512 + GW]

        @block.sync
        def _(sp):
            for g in range(NG):
                src = caches[g].rearrange("a n (r d) c h e -> r d (a n) (c h e)", d=GROUPS[g][1])[:, 0]
                sp.dma_start(cache[g][:, :, :], src).then_inc(cache_in[g], 16)
            sp.dma_start(own_of[:, :], m.own_in).then_inc(own_of_in, 16)
            proj.load(sp)
            sp.wait_ge(tok_taken, 5)
            for g in range(NG):
                dst = new_kv[g].rearrange("a n t c h e -> (a n t) c (h e)")
                for side in range(2):
                    sp.dma_start(dst[:, side, :], tok[:, (1 + side) * QKV + g * GW:(1 + side) * QKV + (g + 1) * GW]
                                 ).then_inc(stored, 16)
            sp.wait_ge(new_scored, 1)
            with nc.allow_non_contiguous_dma(reason="96 scores"):
                for g in range(NG):
                    sp.dma_start(m.new_scores[:, :, g], new_score[:, g, :]).then_inc(new_out, 16)
                sp.wait_ge(new_out, 16 * NG)
                sp.dma_start(prob[:, :, REACH], m.new_scores.rearrange("n h g -> (n h) g")).then_inc(new_back, 16)
            sp.wait_ge(stored, 16 * 2 * NG)

        @block.tensor
        def _(pe):
            def beside(u):
                if u == 0:
                    for i in range(2 * NG * 3):
                        last = pe.transpose(m.ps[0:NS, 3 + i // 4, (i % 4) * P:(i % 4 + 1) * P], m.s_qkv[:, i, :],
                                            m.ident[:, :])
                    last.then_inc(tok_turned, 1)
                if 1 <= u <= 4:
                    pe.wait_ge(tok_taken, 5)
                    for n in range(2 * (u - 1), 2 * u):
                        if n >= 2:
                            pe.wait_ge(multiplied, n - 1)
                        for g in range(NG):
                            last = pe.matmul(spread_queries(n, g), m.ident[0:NS, n:n + 1].to_broadcast([NS, P]),
                                             tok[:, g * GW:(g + 1) * GW], start=True, stop=True)
                        last.then_inc(spread, 1)
                if u == 6:
                    pe.wait_ge(logits, 1)
                    for g in range(NG):
                        last = pe.transpose(m.ps[0:rows, 7, g * P:(g + 1) * P],
                                            score[:, g, :, :].rearrange("p n h -> p (n h)"), m.ident[:, :])
                    last.then_inc(rowed, 1)
                if u == 9:
                    pe.wait_ge(normal, 2)
                    pe.wait_ge(own_of_in, 16)
                    for g in range(NG):
                        pe.transpose(m.ps[:, 3, g * rows:(g + 1) * rows], prob[:, g, 0:REACH], m.ident[0:rows, 0:rows])
                    pe.matmul(m.ps[0:NS, 4, 0:NG * rows], own_of[:, :], diag[:, :, :].rearrange("p g r -> p (g r)"),
                              start=True, stop=True).then_inc(coled, 1)
                if u == 10:
                    pe.wait_ge(cols_taken, 2)
                    for c in range(2):
                        for g in range(NG):
                            v = 2 * QKV + g * GW + c * P
                            pe.matmul(m.ps[:, 5 + c, 0:rows], tok[:, v:v + P], new_p[:, g, :], start=g == 0, stop=False,
                                      skip_group_check=True)
                        for n in range(NS):
                            for g in range(NG):
                                last = pe.matmul(m.ps[:, 5 + c, n * HG:(n + 1) * HG],
                                                 cache[g][:, n, GW + c * P:GW + (c + 1) * P],
                                                 p_cols[:, g, n * HG:(n + 1) * HG], start=False,
                                                 stop=n == NS - 1 and g == NG - 1, skip_group_check=True)
                    last.then_inc(weighed, 1)

            proj.tensor_beside(pe, beside)

        @block.vector
        def _(dve):
            order = Count(dve, own)

            def beside(u):
                if u == 0:
                    dve.wait_ge(tok_turned, 1)
                    for b in range(5):
                        w = min(512, 3 * QKV - b * 512)
                        dve.tensor_copy(tok[:, b * 512:b * 512 + w], m.ps[0:NS, 3 + b, 0:w]).then_inc(tok_taken, 1)
                if u == 1:
                    for g in range(NG):
                        dve.wait_ge(cache_in[g], 16)
                if 1 <= u <= 4:
                    for n in range(2 * (u - 1), 2 * u):
                        dve.wait_ge(spread, n + 1)
                        if n >= 1:
                            dve.wait_ge(scored, n)
                        for g in range(NG):
                            ins = dve.tensor_tensor(prod[:, g * GW:(g + 1) * GW], cache[g][:, n, 0:GW],
                                                    spread_queries(n, g), ALU.mult)
                        ins.then_inc(multiplied, 1)
                        dve.wait_ge(multiplied, n + 1)
                        dve.tensor_reduce(score[:, :, n, :], prod[:, :].rearrange("p (g h d) -> p g h d", g=NG, h=HG),
                                          AX_X, ALU.add).then_inc(scored, 1)
                if u == 5:
                    dve.wait_ge(scored, NS)
                    for g in range(NG):
                        ins = dve.scalar_tensor_tensor(score[:, g, :, :], score[:, g, :, :], DH ** -0.5,
                                                       m.cache_bias[:, g, :].unsqueeze(1).to_broadcast([P, NS, HG]),
                                                       ALU.mult, ALU.add)
                    ins.then_inc(logits, 1)
                    dve.wait_ge(tok_taken, 5)
                    order.then_wait(dve.tensor_tensor(new_prod, tok[:, 0:QKV], tok[:, QKV:2 * QKV], ALU.mult))
                    new = new_score[:, :, :].rearrange("n g h -> n (g h)")
                    order.then_wait(dve.tensor_reduce(new, new_prod.rearrange("n (s d) -> n s d", d=DH), AX_X, ALU.add))
                    dve.scalar_tensor_tensor(new, new, DH ** -0.5, m.new_bias[:, :], ALU.mult,
                                             ALU.add).then_inc(new_scored, 1)
                if u == 7:
                    dve.wait_ge(rowed, 1)
                    order.then_wait(dve.tensor_copy(prob[:, :, 0:REACH],
                                                    m.ps[0:rows, 7, 0:NG * P].rearrange("p (g r) -> p g r", g=NG)))
                    dve.wait_ge(new_back, 16)
                    order.then_wait(dve.tensor_reduce(small[:, 0:1], flat, AX_X, ALU.max))
                    dve.tensor_scalar(small[:, 1:2], small[:, 0:1], -1.0, None, ALU.mult).then_inc(maxed, 1)
                if u == 8:
                    dve.wait_ge(exped, 1)
                    order.then_wait(dve.reciprocal(small[:, 3:4], small[:, 2:3]))
                    dve.tensor_scalar(flat, flat, small[:, 3:4], None, ALU.mult).then_inc(normal, 1)
                    dve.wait_ge(normal, 1)
                    for g in range(NG):
                        ins = dve.tensor_scalar(diag[:, g, :], m.ident[0:rows, 0:rows], prob[:, g, REACH:REACH + 1],
                                                None, ALU.mult)
                    ins.then_inc(normal, 1)
                if u == 9:
                    dve.wait_ge(coled, 1)
                    dve.tensor_copy(p_cols[:, :, :], m.ps[:, 3, 0:NG * rows].rearrange("p (g r) -> p g r", g=NG)
                                    ).then_inc(cols_taken, 1)
                    dve.tensor_copy(new_p[:, :, :], m.ps[0:NS, 4, 0:NG * rows].rearrange("p (g r) -> p g r", g=NG)
                                    ).then_inc(cols_taken, 1)
                if u == 11:
                    dve.wait_ge(weighed, 1)
                    for c in range(2):
                        for half in range(2):
                            part = slice(half * DH, (half + 1) * DH)
                            src = m.ps[part, 5 + c, 0:rows].rearrange("p (n h) -> p h n", h=HG)[:, 2 * c + half, :]
                            dve.tensor_copy(m.s_att[part, c, :], src)

            dve.memset(z[:, :, 0:PAD], 0.0).then_inc(cleared, 1)
            proj.vector_beside(dve, take, beside)

        @block.scalar
        def _(act):
            for t in range(2):
                proj.scalar_next(act, 0, t)
            act.wait_ge(maxed, 1)
            act.activation(flat, flat, ACT.Exp, bias=small[:, 1:2], accum_out=small[:, 2:3]).then_inc(exped, 1)
            for t in range(2):
                proj.scalar_next(act, 1, t)
        proj.close()


def memory_queries(nc, m, q, z, w_in, then, state_pool, w_pool, new_pool_prompt, new_pool_sample):
    with Stage(nc, "qm") as st:
        proj = Product(st, m, w_in, lambda i: i * (2 * P) + QM_COL, MH // 2, then, banks=NCH)
        sums = st.sbuf("sums", [P, 2, PAD + SEQ])
        hist = st.sbuf("hist", [NS * HIST, POOL_W])
        w = st.sbuf("w", [P, NPOOL, P])
        inv = st.sbuf("inv", [P, NPOOL, PAD])
        first = st.sbuf("first", [P, PAD])
        past = st.sbuf("past", [P, NPOOL, NS])
        ztok = st.sbuf("ztok", [HIST, POOL_W])
        zstok = st.sbuf("zstok", [NS, POOL_W])
        part = st.sbuf("part", [P, TB, NG, RES])
        top = st.sbuf("top", [P, TB, HG])
        fall = st.sbuf("fall", [P, NG, TB, HG])
        den = st.sbuf("den", [P, TB, HG])
        whole = part[:, :, 0, 0:GW]
        attended = sums[:, :, PAD:PAD + SEQ]
        pool_in = st.sem("pool_in")
        part_in = st.sem("part_in")
        turned = st.sem("turned")
        past_summed = st.sem("past_summed")
        taken = st.sem("taken")
        own = st.sem("own")
        ready = st.sem("ready")
        mapped = st.sem("mapped")
        copied = st.sem("copied")
        shifted = st.sem("shifted")
        exped = st.sem("exped")
        summed = st.sem("summed")
        att_turned = st.sem("att_turned")
        att_copied = st.sem("att_copied")
        stored = st.sem("stored")
        block = st.block()
        maxima = [part[:, :, g, GW + HG:RES] for g in range(NG)]

        def take(dve, i, t, c, src):
            return scaled(dve, m, c, q[:, i * 2 + t, chunk(c)], src)

        def map_bank(n):
            return m.ps[:, 3 + n % 5, width(n % NCH)]

        @block.gpsimd
        def _(gp):
            gp.dma_start(hist[:, :], state_pool.rearrange("a n r c -> (a n r) c")).then_inc(pool_in, 16)
            gp.dma_start(w[:, :, :], w_pool.rearrange("a g c d -> c (a g) d")).then_inc(pool_in, 16)
            gp.dma_start(inv[:, :, :], m.inv_in).then_inc(pool_in, 16)
            gp.dma_start(part[:, :, :, :], m.group_out.rearrange("(b p) g c -> p b g c", p=P)).then_inc(part_in, 16)
            gp.wait_ge(taken, 2)
            gp.dma_start(new_pool_prompt.rearrange("a n r c -> (a n r) c"), ztok[:, :]).then_inc(stored, 16)
            gp.dma_start(new_pool_sample.rearrange("a n r c -> (a n r) c"), zstok[:, :]).then_inc(stored, 16)
            for k in range(NPOOL):
                gp.wait_ge(copied, NCH * (k + 1))
                gp.dma_start(m.pool_out[:, k, :], z[:, k, PAD:PAD + SEQ]).then_inc(stored, 16)
            gp.wait_ge(att_copied, 4)
            gp.dma_start(m.att_out, attended).then_inc(stored, 16)
            gp.wait_ge(stored, 16 * (3 + NPOOL))

        @block.sync
        def _(sp):
            proj.load(sp)

        @block.tensor
        def _(pe):
            def map_group(k):
                pe.wait_ge(ready, k + 1)
                for c in range(NCH):
                    n = k * NCH + c
                    if n >= 5:
                        pe.wait_ge(copied, n - 4)
                    pe.matmul(map_bank(n), w[:, k, :], z[:, k, PAD + CHUNKS[c][0]:PAD + CHUNKS[c][0] + CHUNKS[c][1]],
                              start=True, stop=True).then_inc(mapped, 1)

            def beside(u):
                if u == 0:
                    for k in range(NPOOL):
                        pe.transpose(m.ps[0:HIST, 3, k * P:(k + 1) * P], z[:, k, PAD + SEQ - HIST:PAD + SEQ], m.ident[:, :])
                        pe.transpose(m.ps[0:NS, 4, k * P:(k + 1) * P], z[:, k, PAD + SEQ:PAD + T], m.ident[:, :])
                    pe.wait_ge(pool_in, 48)
                    for k in range(NPOOL):
                        last = pe.transpose(m.ps[:, 5, k * NS * HIST:(k + 1) * NS * HIST], hist[:, k * P:(k + 1) * P],
                                            m.ident[0:NS * HIST, 0:NS * HIST])
                    last.then_inc(turned, 1)
                if u in (1, 2, 4, 5):
                    map_group((1, 2, 4, 5).index(u))
                if u == 11:
                    pe.wait_ge(summed, 1)
                    pe.wait_ge(copied, NCH * NPOOL)
                    for n in range(4):
                        k, half = divmod(n, 2)
                        for b in range(4):
                            last = pe.transpose(m.ps[:, 3 + n, b * P:(b + 1) * P], whole[:, 4 * half + b, k * P:(k + 1) * P],
                                                m.ident[:, :])
                        last.then_inc(att_turned, 1)

            proj.tensor_beside(pe, beside)

        @block.scalar
        def _(act):
            def copy_group(k):
                act.wait_ge(mapped, NCH * (k + 1))
                for c in range(NCH):
                    act.activation(z[:, k, PAD + CHUNKS[c][0]:PAD + CHUNKS[c][0] + CHUNKS[c][1]], map_bank(k * NCH + c),
                                   ACT.Copy, scale=m.gain[:, GAIN_ROWS + k:GAIN_ROWS + k + 1]).then_inc(copied, 1)

            copy_group(0)
            proj.scalar_next(act, 0, 0)
            copy_group(1)
            copy_group(2)
            proj.scalar_next(act, 0, 1)
            copy_group(3)
            act.wait_ge(shifted, NG)
            act.activation(fall[:, :, :, :], fall[:, :, :, :], ACT.Exp).then_inc(exped, 1)
            for t in range(2):
                proj.scalar_next(act, 1, t)
            act.wait_ge(copied, NCH * NPOOL)
            act.activation(m.s_pool[:, :, :], z[:, :, PAD + SEQ:PAD + T], ACT.Copy)
            act.wait_ge(proj.taken, 2 * 2 * NCH + NCH)
            act.activation(m.s_qm[:, :, :], q[:, :, SEQ:T], ACT.Copy)
            for n in range(4):
                k, half = divmod(n, 2)
                act.wait_ge(att_turned, n + 1)
                act.activation(attended[:, k, half * 512:(half + 1) * 512], m.ps[:, 3 + n, :], ACT.Copy).then_inc(att_copied, 1)

        @block.vector
        def _(dve):
            order = Count(dve, own)

            def pool_group(k):
                window = POOL_WINDOWS[k]
                src = z[:, k, :]
                for j in range(k + 1):
                    dst = sums[:, j % 2, :]
                    order.then_wait(dve.tensor_tensor(dst[:, PAD:PAD + SEQ], src[:, PAD:PAD + SEQ],
                                                      src[:, PAD - 2 ** j:PAD + SEQ - 2 ** j], ALU.add))
                    src = dst
                zk = z[:, k, PAD:PAD + SEQ]
                dve.scalar_tensor_tensor(zk[:, PAD:SEQ], src[:, 2 * PAD:PAD + SEQ], 1.0 / window,
                                         zk[:, PAD:SEQ], ALU.mult, ALU.subtract)
                order.then_wait(dve.tensor_tensor(first[:, :], src[:, PAD:2 * PAD], inv[:, k, :], ALU.mult))
                order.then_wait(dve.tensor_tensor(zk[:, 0:PAD], first[:, :], zk[:, 0:PAD], ALU.subtract))
                zs = z[:, k, PAD + SEQ:PAD + T]
                order.then_wait(dve.tensor_tensor(past[:, k, :], past[:, k, :], zs, ALU.add))
                dve.scalar_tensor_tensor(zs, past[:, k, :], 1.0 / window, zs, ALU.mult,
                                         ALU.subtract).then_inc(ready, 1)

            def beside(u):
                if u == 0:
                    order.then_wait(dve.memset(sums[:, :, 0:PAD], 0.0))
                    dve.wait_ge(turned, 1)
                    dve.wait_ge(pool_in, 48)
                    dve.tensor_copy(ztok[:, :], m.ps[0:HIST, 3, :]).then_inc(taken, 1)
                    dve.tensor_copy(zstok[:, :], m.ps[0:NS, 4, :]).then_inc(taken, 1)
                    for k, window in enumerate(POOL_WINDOWS):
                        past_rows = m.ps[:, 5, k * NS * HIST:(k + 1) * NS * HIST].rearrange("p (n r) -> p n r", n=NS)
                        dve.tensor_reduce(past[:, k, :], past_rows[:, :, HIST + 1 - window:HIST], AX_X,
                                          ALU.add).then_inc(past_summed, 1)
                    dve.wait_ge(taken, 2)
                    dve.wait_ge(past_summed, NPOOL)
                if u < NPOOL:
                    if u:
                        dve.wait_ge(ready, u)
                    pool_group(u)
                if u == 4:
                    dve.wait_ge(ready, NPOOL)
                    dve.wait_ge(part_in, 16)
                    order.then_wait(dve.tensor_tensor(top[:, :, :], maxima[0], maxima[1], ALU.max))
                    order.then_wait(dve.tensor_tensor(top[:, :, :], top[:, :, :], maxima[2], ALU.max))
                    for g in range(NG):
                        dve.tensor_tensor(fall[:, g, :, :], maxima[g], top[:, :, :], ALU.subtract).then_inc(shifted, 1)
                if u == 5:
                    dve.wait_ge(exped, 1)
                    for g in range(NG):
                        group_sums = part[:, :, g, GW:GW + HG]
                        order.then_wait(dve.tensor_tensor(group_sums, group_sums, fall[:, g, :, :], ALU.mult))
                    order.then_wait(dve.tensor_tensor(den[:, :, :], part[:, :, 0, GW:GW + HG], part[:, :, 1, GW:GW + HG],
                                                      ALU.add))
                    order.then_wait(dve.tensor_tensor(den[:, :, :], den[:, :, :], part[:, :, 2, GW:GW + HG], ALU.add))
                    order.then_wait(dve.reciprocal(den[:, :, :], den[:, :, :]))
                    for g in range(NG):
                        order.then_wait(dve.tensor_tensor(fall[:, g, :, :], fall[:, g, :, :], den[:, :, :], ALU.mult))
                if u in (6, 7, 8):
                    g = u - 6
                    for par in range(2):
                        vals = part[:, :, g, 0:GW].rearrange("p b (hh par d) -> p par b hh d", hh=2, par=2)[:, par]
                        weight = fall[:, g, :, 2 * par:2 * par + 2].unsqueeze(3).to_broadcast([P, TB, 2, DH])
                        order.then_wait(dve.tensor_tensor(vals, vals, weight, ALU.mult))
                if u == 9:
                    order.then_wait(dve.tensor_tensor(whole, whole, part[:, :, 1, 0:GW], ALU.add))
                if u == 10:
                    dve.tensor_tensor(whole, whole, part[:, :, 2, 0:GW], ALU.add).then_inc(summed, 1)

            proj.vector_beside(dve, take, beside)
        proj.close()


def memory_attention(nc, m, q):
    MT = MEM // P
    scale = P ** -0.5
    with Stage(nc, "mematt") as st:
        v = st.sbuf("v", [P, MT, MEM_W])
        kt = st.sbuf("kt", [P, MH, MEM])
        kt_in = st.sem("kt_in")
        v_in = st.sem("v_in")
        prob = st.sbuf("prob", [P, 2, MH, MEM])
        turned_p = st.sbuf("turned_p", [P, 2, MT, MH, P])
        stat = st.sbuf("stat", [P, 2, 4, MH])
        scored = st.sem("scored")
        own = st.sem("own")
        negated = st.sem("negated")
        exped = st.sem("exped")
        normal = st.sem("normal")
        p_turned = st.sem("p_turned")
        p_taken_act = st.sem("p_taken_act")
        p_taken_dve = st.sem("p_taken_dve")
        weighed = st.sem("weighed")
        res_taken = st.sem("res_taken")
        stored = st.sem("stored")
        block = st.block()

        @block.sync
        def _(sp):
            sp.dma_start(kt[:, :, :], m.mem_kt).then_inc(kt_in, 16)
            sp.dma_start(v[:, :, :], m.mem_v).then_inc(v_in, 16)
            for b in range(TB):
                sp.wait_ge(res_taken, b + 1)
                sp.dma_start(m.mem_out[:, :, b * P:(b + 1) * P], q[:, :, b * P:(b + 1) * P]).then_inc(stored, 16)
            sp.wait_ge(stored, 16 * TB)

        @block.tensor
        def _(pe):
            def scores(b):
                if b >= 2:
                    pe.wait_ge(exped, MH * (b - 1))
                for h in range(MH):
                    last = pe.matmul(m.ps[:, 2 * (b % 2) + h // 2, (h % 2) * MEM:(h % 2 + 1) * MEM],
                                     q[:, h, b * P:(b + 1) * P], kt[:, h, :], start=True, stop=True)
                last.then_inc(scored, 1)

            def turn(b):
                pe.wait_ge(normal, b + 1)
                if b >= 1:
                    pe.wait_ge(p_taken_act, b)
                    pe.wait_ge(p_taken_dve, b)
                for t in range(MT):
                    for h in range(MH):
                        last = pe.transpose(m.ps[:, 4 + t, h * P:(h + 1) * P], prob[:, b % 2, h, t * P:(t + 1) * P],
                                            m.ident[:, :])
                last.then_inc(p_turned, 1)

            def weigh(b):
                pe.wait_ge(p_taken_act, b + 1)
                pe.wait_ge(p_taken_dve, b + 1)
                if b >= 2:
                    pe.wait_ge(res_taken, b - 1)
                for h in range(MH):
                    for t in range(MT):
                        last = pe.matmul(m.ps[:, 6 + b % 2, h * P:(h + 1) * P], v[:, t, h * P:(h + 1) * P],
                                         turned_p[:, b % 2, t, h, :], start=t == 0, stop=t == MT - 1)
                last.then_inc(weighed, 1)

            pe.wait_ge(kt_in, 16)
            scores(0)
            scores(1)
            for b in range(TB):
                turn(b)
                if b + 2 < TB:
                    scores(b + 2)
                if b == 0:
                    pe.wait_ge(v_in, 16)
                weigh(b)

        @block.scalar
        def _(act):
            def exps(b):
                act.wait_ge(negated, b + 1)
                if b >= 2:
                    act.wait_ge(p_turned, b - 1)
                for h in range(MH):
                    act.activation(prob[:, b % 2, h, :], m.ps[:, 2 * (b % 2) + h // 2, (h % 2) * MEM:(h % 2 + 1) * MEM],
                                   ACT.Exp, bias=stat[:, b % 2, 1, h:h + 1], scale=scale,
                                   accum_out=stat[:, b % 2, 2, h:h + 1]).then_inc(exped, 1)

            def result(b):
                act.wait_ge(weighed, b + 1)
                act.activation(q[:, :, b * P:(b + 1) * P], m.ps[:, 6 + b % 2, :].rearrange("p (h q) -> p h q", h=MH),
                               ACT.Copy).then_inc(res_taken, 1)

            exps(0)
            for b in range(TB):
                if b + 1 < TB:
                    exps(b + 1)
                act.wait_ge(p_turned, b + 1)
                if b >= 2:
                    act.wait_ge(weighed, b - 1)
                act.activation(turned_p[:, b % 2, 1, :, :], m.ps[:, 5, :].rearrange("p (h q) -> p h q", h=MH),
                               ACT.Copy).then_inc(p_taken_act, 1)
                if b >= 1:
                    result(b - 1)
            result(TB - 1)

        @block.vector
        def _(dve):
            order = Count(dve, own)

            def top(b):
                dve.wait_ge(scored, b + 1)
                if b >= 2:
                    dve.wait_ge(normal, b - 1)
                src = m.ps[:, 2 * (b % 2):2 * (b % 2) + 2, :].rearrange("p a (i k) -> p (a i) k", k=MEM)
                order.then_wait(dve.tensor_reduce(stat[:, b % 2, 0, :], src, AX_X, ALU.max))
                dve.tensor_scalar(stat[:, b % 2, 1, :], stat[:, b % 2, 0, :], -scale, None, ALU.mult).then_inc(negated, 1)

            def normalise(b):
                dve.wait_ge(exped, MH * (b + 1))
                order.then_wait(dve.reciprocal(stat[:, b % 2, 3, :], stat[:, b % 2, 2, :]))
                dve.tensor_tensor(prob[:, b % 2, :, :], prob[:, b % 2, :, :],
                                  stat[:, b % 2, 3, :].unsqueeze(2).to_broadcast([P, MH, MEM]), ALU.mult).then_inc(normal, 1)

            top(0)
            for b in range(TB):
                normalise(b)
                if b + 1 < TB:
                    top(b + 1)
                dve.wait_ge(p_turned, b + 1)
                if b >= 2:
                    dve.wait_ge(weighed, b - 1)
                dve.tensor_copy(turned_p[:, b % 2, 0, :, :], m.ps[:, 4, :].rearrange("p (h q) -> p h q", h=MH)
                                ).then_inc(p_taken_dve, 1)


class SampleMemory:

    MT = MEM // P
    ROWS = NS * MH

    def __init__(self, st, m, cache):
        self.m, self.scale = m, P ** -0.5
        self.c_v = cache.rearrange("a n (t p) c h e -> p (a n) t c (h e)", p=P)
        self.keys = st.sbuf("keys", [P, 2, self.MT, MEM_W])
        self.vals = st.sbuf("vals", [P, 2, self.MT, MEM_W])
        self.tok = st.sbuf("tok", [NS, MEM_W])
        self.score = st.sbuf("score", [P, self.MT, NS, MH])
        self.prob = st.sbuf("prob", [self.ROWS, self.MT, P])
        self.flat = self.prob[:, :, :].rearrange("p t r -> p (t r)")
        self.small = st.sbuf("small", [self.ROWS, 4])
        self.p_cols = st.sbuf("p_cols", [P, self.MT, self.ROWS])
        self.key_in = [st.sem(f"key_in{i}") for i in range(2)]
        self.val_in = [st.sem(f"val_in{i}") for i in range(2)]
        self.tok_done = st.sem("tok_done")
        self.tok_taken = st.sem("tok_taken")
        self.spread = st.sem("spread")
        self.multiplied = st.sem("multiplied")
        self.side_scored = st.sem("side_scored")
        self.rowed = st.sem("rowed")
        self.side_own = st.sem("side_own")
        self.maxed = st.sem("maxed")
        self.exped = st.sem("exped")
        self.normal = st.sem("normal")
        self.coled = st.sem("coled")
        self.cols_taken = st.sem("cols_taken")
        self.weighed = st.sem("weighed")

    U_TOK, U_SPREAD, U_ROWS, U_COLS, U_WEIGH = 0, 2, 20, 26, 28

    def gpsimd(self, gp):
        for n in range(NS):
            if n >= 2:
                gp.wait_ge(self.side_scored, n - 1)
            gp.dma_start(self.keys[:, n % 2, :, :], self.c_v[:, n, :, 0, :]).then_inc(self.key_in[n % 2], 16)
        for n in range(NS):
            if n >= 2:
                gp.wait_ge(self.weighed, n - 1)
            gp.dma_start(self.vals[:, n % 2, :, :], self.c_v[:, n, :, 1, :]).then_inc(self.val_in[n % 2], 16)

    def tensor(self, pe, u):
        m = self.m
        if u == self.U_TOK:
            for h in range(MH):
                last = pe.transpose(m.ps[0:NS, 6, h * P:(h + 1) * P], m.s_qm[:, h, :], m.ident[:, :])
            last.then_inc(self.tok_done, 1)
        n, off = divmod(u - self.U_SPREAD, 2)
        if off == 0 and 0 <= n < NS:
            if n == 0:
                pe.wait_ge(self.tok_taken, 1)
            if n >= 2:
                pe.wait_ge(self.multiplied, n - 1)
            pe.matmul(m.ps[:, 6 + n % 2, :], m.ident[0:NS, n:n + 1].to_broadcast([NS, P]), self.tok[:, :], start=True,
                      stop=True).then_inc(self.spread, 1)
        if u == self.U_ROWS:
            pe.wait_ge(self.side_scored, NS)
            for t in range(self.MT):
                last = pe.transpose(m.ps[0:self.ROWS, 6, t * P:(t + 1) * P],
                                    self.score[:, t, :, :].rearrange("p n h -> p (n h)"), m.ident[:, :])
            last.then_inc(self.rowed, 1)
        if u == self.U_COLS:
            pe.wait_ge(self.normal, 1)
            for t in range(self.MT):
                last = pe.transpose(m.ps[:, 7, t * self.ROWS:(t + 1) * self.ROWS], self.prob[:, t, :],
                                    m.ident[0:self.ROWS, 0:self.ROWS])
            last.then_inc(self.coled, 1)
        n = u - self.U_WEIGH
        if 0 <= n < NS:
            if n == 0:
                pe.wait_ge(self.cols_taken, 1)
            pe.wait_ge(self.val_in[n % 2], 16 * (n // 2 + 1))
            for h in range(MH):
                col = n * MH + h
                for t in range(self.MT):
                    last = pe.matmul(m.ps[:, 6, col:col + 1], self.vals[:, n % 2, t, h * P:(h + 1) * P],
                                     self.p_cols[:, t, col:col + 1], start=t == 0, stop=t == self.MT - 1)
            last.then_inc(self.weighed, 1)

    def vector(self, dve, u):
        m = self.m
        if u == self.U_TOK:
            dve.wait_ge(self.tok_done, 1)
            dve.tensor_copy(self.tok[:, :], m.ps[0:NS, 6, :]).then_inc(self.tok_taken, 1)
        n, off = divmod(u - self.U_SPREAD, 2)
        if off == 0 and 0 <= n < NS:
            dve.wait_ge(self.spread, n + 1)
            dve.wait_ge(self.key_in[n % 2], 16 * (n // 2 + 1))
            keys = self.keys[:, n % 2, :, :]
            dve.tensor_tensor(keys, keys, m.ps[:, 6 + n % 2, :].unsqueeze(1).to_broadcast([P, self.MT, MEM_W]),
                              ALU.mult).then_inc(self.multiplied, 1)
            dve.wait_ge(self.multiplied, n + 1)
            dve.tensor_reduce(self.score[:, :, n, :], keys.rearrange("p t (h d) -> p t h d", h=MH), AX_X,
                              ALU.add).then_inc(self.side_scored, 1)
        if u == self.U_ROWS + 1:
            order = Count(dve, self.side_own)
            dve.wait_ge(self.rowed, 1)
            order.then_wait(dve.tensor_copy(self.flat, m.ps[0:self.ROWS, 6, 0:MEM]))
            order.then_wait(dve.tensor_reduce(self.small[:, 0:1], self.flat, AX_X, ALU.max))
            dve.tensor_scalar(self.small[:, 1:2], self.small[:, 0:1], -self.scale, None, ALU.mult).then_inc(self.maxed, 1)
        if u == self.U_COLS - 1:
            dve.wait_ge(self.exped, 1)
            dve.reciprocal(self.small[:, 3:4], self.small[:, 2:3]).then_inc(self.side_own, 1)
            dve.wait_ge(self.side_own, 3)
            dve.tensor_scalar(self.flat, self.flat, self.small[:, 3:4], None, ALU.mult).then_inc(self.normal, 1)
        if u == self.U_COLS:
            dve.wait_ge(self.coled, 1)
            dve.tensor_copy(self.p_cols[:, :, :], m.ps[:, 7, 0:self.MT * self.ROWS].rearrange("p (t r) -> p t r", t=self.MT)
                            ).then_inc(self.cols_taken, 1)
        if u == self.U_WEIGH + NS:
            dve.wait_ge(self.weighed, NS)
            dve.tensor_copy(m.s_mem[:, :, :], m.ps[:, 6, 0:self.ROWS].rearrange("p (n h) -> p h n", h=MH))

    def scalar(self, act):
        act.wait_ge(self.maxed, 1)
        act.activation(self.flat, self.flat, ACT.Exp, bias=self.small[:, 1:2], scale=self.scale,
                       accum_out=self.small[:, 2:3]).then_inc(self.exped, 1)


class Memory:
    pass


def decoder_step(nc, i, o):
    SEMS.clear()
    m = Memory()
    with ExitStack() as ctx:
        def sb(name, shape, dt=F32):
            return ctx.enter_context(nc.sbuf_tensor(name, shape, dt))

        m.x = sb("x", [P, KD, T])
        m.uh = sb("uh", [P, KD, T], F32R)
        m.ul = sb("ul", [P, KD, T], F32R)
        m.rstd = sb("rstd", [P, T])
        m.ident = sb("ident", [P, P])
        m.mean = sb("mean", [P, P])
        m.eps = sb("eps", [P, 1])
        m.gain = sb("gain", [P, GAIN_ROWS + NPOOL])
        m.cache_bias = sb("cache_bias", [P, NG, HG])
        m.new_bias = sb("new_bias", [NS, NG * HG])
        m.s_qkv = sb("s_qkv", [P, 6 * NG, NS])
        m.s_att = sb("s_att", [P, 2, NS])
        m.s_pool = sb("s_pool", [P, NPOOL, NS])
        m.s_mem = sb("s_mem", [P, MH, NS])
        m.s_qm = sb("s_qm", [P, MH, NS])
        m.stream = Stream(nc, ctx)
        m.ps = ctx.enter_context(nc.psum_tensor("ps", [P, 8, 512], F32))
        m.bias_rows = nc.dram_tensor("bias_rows", (NG, NG * HG, 384), F32).ap()
        m.group_out = nc.dram_tensor("group_out", (SEQ, NG, RES), F32).ap()
        m.att_out = nc.dram_tensor("att_out", (P, 2, SEQ), F32).ap()
        m.pool_out = nc.dram_tensor("pool_out", (P, NPOOL, SEQ), F32).ap()
        m.mem_kt = nc.dram_tensor("mem_kt", (P, MH, MEM), F32).ap()
        m.mem_v = nc.dram_tensor("mem_v", (P, MEM // P, MEM_W), F32).ap()
        m.mem_out = nc.dram_tensor("mem_out", (P, MH, SEQ), F32).ap()
        m.new_scores = nc.dram_tensor("new_scores", (NS, HG, NG), F32).ap()
        m.sel_in, m.own_in, m.inv_in = i["const_sel"], i["const_own"], i["const_inv"]

        gains = [i[n] for n in ("g_ffn1", "g_mix", "g_mem", "g_ffn2", "g_final")]
        w_in = i["w_in"].rearrange("a (k p) f -> p (a k) f", p=P)
        w_out = i["w_out"].rearrange("a (k p) f -> p (a k) f", p=P)
        w_o = [i[n].rearrange("a (k p) f -> p (a k) f", p=P) for n in ("w_oa", "w_ob", "w_oc")]

        def gates(branch):
            return w_in, GATE_COL + branch * D

        w_gate1, w_gate2 = (i[n].rearrange("a (k p) f -> p (a k) f", p=P) for n in ("w1_gate", "w2_gate"))
        load_tokens(nc, m, i, gains, (w_gate1, 0))
        ffn(nc, m, "ffn1", i["w1_gate"], i["w1_up"], i["w1_down"], G_MIX, (w_in, 0))
        for g in range(NG):
            keys = (lambda st: MemoryKeys(st, nc, m, i["mem_prompt"], i["w_mem_kv"], o["new_mem_kv_prompt"])) if g == 1 else None
            attention(nc, m, g, w_in, o[f"new_win{g}_kv_prompt"], (w_in, (g + 1) * GW if g + 1 < NG else Z_COL), keys)
        clear_semaphores(nc)
        with Stage(nc, "queries") as queries:
            with nc.sbuf_tensor("z", [P, NPOOL, PAD + T], F32, side="right") as z:
                pool_values(nc, m, z, w_in, (w_in, QM_COL), [i[f"cache_win{g}_kv"] for g in range(NG)],
                            [o[f"new_win{g}_kv_sample"] for g in range(NG)])
                q = queries.sbuf("q", [P, MH, T])
                memory_queries(nc, m, q, z, w_in, gates(1), i["state_pool"], i["w_pool"], o["new_pool_prompt"],
                               o["new_pool_sample"])
            memory_attention(nc, m, q)
        clear_semaphores(nc)
        with nc.sbuf_tensor("mix", [P, KD, T], F32, side="right") as mix:
            m.mix = mix
            for branch, name, kt, then, late, job in (
                    (1, "b", NPOOL, gates(0), (m.pool_out, m.s_pool[:, :, :]), None),
                    (0, "a", 2, gates(2), (m.att_out, m.s_att[:, :, :]), lambda st: SampleMemory(st, m, i["cache_mem_kv"])),
                    (2, "c", MH, (w_out, 0), (m.mem_out, m.s_mem[:, :, :]), None)):
                with Stage(nc, f"branch_{name}") as st:
                    high, low = (st.sbuf(n, [P, kt, T], F32R) for n in ("high", "low"))
                    merge(nc, m, f"merge_{name}", branch, branch == 1, w_in, w_o[branch], high, low, kt, then, late, job)
            mix_out(nc, m, w_out, G_FFN2, (w_gate2, 0))
        clear_semaphores(nc)
        ffn(nc, m, "ffn2", i["w2_gate"], i["w2_up"], i["w2_down"], None, None)
        final(nc, m, i["g_final"], o["y_prompt"], o["y_sample"])



N_BUCKETS = 32
MAX_DISTANCE = 2048


def rel_bucket(n):
    exact = N_BUCKETS // 2
    if n < exact:
        return n
    return min(exact + int(np.log(n / exact) / np.log(MAX_DISTANCE / exact) * (N_BUCKETS - exact)), N_BUCKETS - 1)


def constants():
    onehot = np.zeros((N_BUCKETS, 2, NG, REACH + 1), np.float32)
    for g, (_, dil) in enumerate(GROUPS):
        for r in range(REACH + 1):
            onehot[rel_bucket((REACH - r) * dil), 0, g, r] = 1.0
            onehot[rel_bucket(r * dil), 1, g, r] = 1.0
    sel = np.zeros((NS, NS, P), np.float32)
    own = np.zeros((NS * HG, NS), np.float32)
    for n in range(NS):
        sel[n, n, :] = 1.0
        own[n * HG:(n + 1) * HG, n] = 1.0
    inv = np.zeros((P, NPOOL, PAD), np.float32)
    for k, window in enumerate(POOL_WINDOWS):
        inv[:, k, :] = 1.0 / np.minimum(window, np.arange(PAD) + 1)
    return {"const_ident": np.eye(P, dtype=np.float32), "const_onehot": onehot, "const_sel": sel, "const_own": own,
            "const_inv": inv}



_OUTS = [("y_prompt", (1, SEQ, D)), ("y_sample", (NS, 1, D)), ("new_win0_kv_prompt", (1, 1, 128, 2, HG, DH)),
         ("new_win1_kv_prompt", (1, 1, 512, 2, HG, DH)), ("new_win2_kv_prompt", (1, 1, SEQ, 2, HG, DH)),
         ("new_pool_prompt", (1, 1, HIST, POOL_W)), ("new_mem_kv_prompt", (1, 1, MEM, 2, MH, P)),
         ("new_win0_kv_sample", (1, NS, 1, 2, HG, DH)), ("new_win1_kv_sample", (1, NS, 1, 2, HG, DH)),
         ("new_win2_kv_sample", (1, NS, 1, 2, HG, DH)), ("new_pool_sample", (1, NS, 1, POOL_W))]


def kernel(**inputs):
    import concourse.bacc as bacc
    from concourse.bass_utils import run_bass_kernel_spmd as run

    nc = bacc.Bacc("TRN2", target_bir_lowering=False, num_devices=1)
    arrays = {name: np.ascontiguousarray(a) for name, a in inputs.items()} | constants()
    i = {name: nc.dram_tensor(f"in_{name}", a.shape, mybir.dt.from_np(a.dtype), kind="ExternalInput").ap()
         for name, a in arrays.items()}
    o = {name: nc.dram_tensor(f"out_{name}", shape, F32, kind="ExternalOutput").ap() for name, shape in _OUTS}
    decoder_step(nc, i, o)
    r = run(nc, [{f"in_{name}": a for name, a in arrays.items()}], core_ids=[0])
    return tuple(r.results[0][f"out_{name}"] for name, _ in _OUTS)
```
